# Optimizing a Trainium2 kernel written in Bass

```python
import jax, jax.numpy as jnp
from jax import lax
import numpy as np
import math
import jax
import jax.numpy as jnp

D_MODEL = 2048
BATCH = 1
SEQ = 256
DEPTH = 1

ATTN_HEADS = 8
HEAD_DIM = 128
ATTN_WIDTH = ATTN_HEADS * HEAD_DIM
CONV_WIDTH = D_MODEL // 2
CONV_K = 3
MOBA_BLOCK = 256
MOBA_TOP_K = 3
QUERY_CHUNK = 64
D_FF = 4 * D_MODEL
PLE_DIM = 256
RMS_EPS = 1e-6
IN_SIZES = (ATTN_WIDTH, ATTN_WIDTH, ATTN_WIDTH, CONV_WIDTH, CONV_WIDTH, CONV_WIDTH, D_MODEL, D_MODEL)
IN_COLS = sum(IN_SIZES)


def rms_norm(x, g):
    xf = x.astype(jnp.float32)
    y = xf * lax.rsqrt(jnp.mean(xf * xf, axis=-1, keepdims=True) + RMS_EPS)
    return (y * g.astype(jnp.float32)).astype(x.dtype)

def moba_attention(q, k, v):
    B, H, S, hd = q.shape
    dt = q.dtype
    f32 = jnp.float32
    nb = -(-S // MOBA_BLOCK)
    pad = nb * MOBA_BLOCK - S
    kb = jnp.pad(k, ((0, 0), (0, 0), (0, pad), (0, 0))).reshape(B, H, nb, MOBA_BLOCK, hd)
    vb = jnp.pad(v, ((0, 0), (0, 0), (0, pad), (0, 0))).reshape(B, H, nb, MOBA_BLOCK, hd)
    q_blk = jnp.arange(S) // MOBA_BLOCK
    n_sel = min(MOBA_TOP_K, nb - 1)
    scale = HEAD_DIM ** -0.5
    if n_sel > 0:
        k_mean = jnp.mean(kb.astype(f32), axis=3)
        gate = jnp.einsum('bhsd,bhnd->bhsn', q.astype(f32), k_mean)
        past = jnp.arange(nb)[None, :] < q_blk[:, None]
        gate = jnp.where(past[None, None], gate, -jnp.inf)
        _, sel = lax.top_k(gate, n_sel)
        sel_valid = jnp.arange(n_sel)[None, :] < q_blk[:, None]
    bi = jnp.arange(B)[:, None, None, None]
    hi = jnp.arange(H)[None, :, None, None]

    def chunk(c):
        q0 = c * QUERY_CHUNK
        qc = lax.dynamic_slice_in_dim(q, q0, QUERY_CHUNK, axis=2)
        qpos = q0 + jnp.arange(QUERY_CHUNK)
        blk = q0 // MOBA_BLOCK
        k_own = lax.dynamic_index_in_dim(kb, blk, axis=2, keepdims=False)
        v_own = lax.dynamic_index_in_dim(vb, blk, axis=2, keepdims=False)
        kpos = blk * MOBA_BLOCK + jnp.arange(MOBA_BLOCK)
        s_own = jnp.einsum('bhqd,bhkd->bhqk', qc, k_own, preferred_element_type=f32) * scale
        s_own = jnp.where((kpos[None, :] <= qpos[:, None])[None, None], s_own, -jnp.inf)
        if n_sel > 0:
            sel_c = lax.dynamic_slice_in_dim(sel, q0, QUERY_CHUNK, axis=2)
            val_c = lax.dynamic_slice_in_dim(sel_valid, q0, QUERY_CHUNK, axis=0)
            k_sel = kb[bi, hi, sel_c]
            v_sel = vb[bi, hi, sel_c]
            s_sel = jnp.einsum('bhqd,bhqnkd->bhqnk', qc, k_sel, preferred_element_type=f32) * scale
            s_sel = jnp.where(val_c[None, None, :, :, None], s_sel, -jnp.inf)
            s = jnp.concatenate([s_sel.reshape(B, H, QUERY_CHUNK, n_sel * MOBA_BLOCK), s_own], axis=-1)
            probs = jax.nn.softmax(s, axis=-1)
            p_sel = probs[..., :n_sel * MOBA_BLOCK].reshape(B, H, QUERY_CHUNK, n_sel, MOBA_BLOCK)
            p_own = probs[..., n_sel * MOBA_BLOCK:]
            o = (jnp.einsum('bhqnk,bhqnkd->bhqd', p_sel.astype(dt), v_sel, preferred_element_type=f32)
                 + jnp.einsum('bhqk,bhkd->bhqd', p_own.astype(dt), v_own, preferred_element_type=f32))
        else:
            probs = jax.nn.softmax(s_own, axis=-1)
            o = jnp.einsum('bhqk,bhkd->bhqd', probs.astype(dt), v_own, preferred_element_type=f32)
        return o.astype(dt)

    out = lax.map(chunk, jnp.arange(S // QUERY_CHUNK))
    return out.transpose(1, 2, 0, 3, 4).reshape(B, H, S, hd)

def causal_depthwise_conv(u, w):
    C = u.shape[-1]
    return lax.conv_general_dilated(
        u, w[:, None, :].astype(u.dtype), window_strides=(1,), padding=[(CONV_K - 1, 0)],
        dimension_numbers=('NWC', 'WIO', 'NWC'), feature_group_count=C)

def first_inputs(seed: int = 0) -> dict:
    key = jax.random.key(seed)
    ks = jax.random.split(key, 16)
    f32 = jnp.float32

    def nrm(k, shape, scale):
        return jax.random.normal(k, shape, f32) * scale

    def gain(k, shape):
        return 1.0 + 0.05 * jax.random.normal(k, shape, f32)

    return {
        'x': nrm(ks[0], (BATCH, SEQ, D_MODEL), 1.0),
        'p': nrm(ks[1], (DEPTH, BATCH, SEQ, PLE_DIM), 1.0),
        'g_mix': gain(ks[2], (DEPTH, D_MODEL)),
        'w_in': nrm(ks[3], (DEPTH, D_MODEL, IN_COLS), D_MODEL ** -0.5),
        'g_q': gain(ks[4], (DEPTH, HEAD_DIM)),
        'g_k': gain(ks[5], (DEPTH, HEAD_DIM)),
        'w_conv': nrm(ks[6], (DEPTH, CONV_K, CONV_WIDTH), CONV_K ** -0.5),
        'w_attn_out': nrm(ks[7], (DEPTH, ATTN_WIDTH, D_MODEL), ATTN_WIDTH ** -0.5),
        'w_conv_out': nrm(ks[8], (DEPTH, CONV_WIDTH, D_MODEL), CONV_WIDTH ** -0.5),
        'w_o': nrm(ks[9], (DEPTH, D_MODEL, D_MODEL), D_MODEL ** -0.5),
        'g_mlp': gain(ks[10], (DEPTH, D_MODEL)),
        'w_up': nrm(ks[11], (DEPTH, D_MODEL, D_FF), D_MODEL ** -0.5),
        'w_down': nrm(ks[12], (DEPTH, D_FF, D_MODEL), D_FF ** -0.5),
        'g_ple': gain(ks[13], (DEPTH, D_MODEL)),
        'w_ple_gate': nrm(ks[14], (DEPTH, D_MODEL, D_MODEL), D_MODEL ** -0.5),
        'w_ple_proj': nrm(ks[15], (DEPTH, PLE_DIM, D_MODEL), PLE_DIM ** -0.5),
    }

def first_block(x, p, g_mix, w_in, g_q, g_k, w_conv, w_attn_out, w_conv_out, w_o,
              g_mlp, w_up, w_down, g_ple, w_ple_gate, w_ple_proj):
    B, S, D = x.shape
    cuts = [int(c) for c in np.cumsum(IN_SIZES)[:-1]]
    r = x
    for i in range(DEPTH):
        h = rms_norm(r, g_mix[i])
        z = h @ w_in[i]
        q, k, v, c_b, c_c, c_x, g_a, g_c = jnp.split(z, cuts, axis=-1)
        q = rms_norm(q.reshape(B, S, ATTN_HEADS, HEAD_DIM), g_q[i]).transpose(0, 2, 1, 3)
        k = rms_norm(k.reshape(B, S, ATTN_HEADS, HEAD_DIM), g_k[i]).transpose(0, 2, 1, 3)
        v = v.reshape(B, S, ATTN_HEADS, HEAD_DIM).transpose(0, 2, 1, 3)
        attn = moba_attention(q, k, v)
        y_attn = attn.transpose(0, 2, 1, 3).reshape(B, S, ATTN_WIDTH) @ w_attn_out[i]
        y_conv = (c_b * causal_depthwise_conv(c_c * c_x, w_conv[i])) @ w_conv_out[i]
        merged = jax.nn.sigmoid(g_a) * y_attn + jax.nn.sigmoid(g_c) * y_conv
        r = r + merged @ w_o[i]
        h = rms_norm(r, g_mlp[i])
        r = r + jnp.square(jax.nn.relu(h @ w_up[i])) @ w_down[i]
        h = rms_norm(r, g_ple[i])
        r = r + jax.nn.sigmoid(h @ w_ple_gate[i]) * (p[i] @ w_ple_proj[i])
    return r


N_MIXERS = 2
N_META = 16
CONV_WIDTH_2 = 31
HEAD_DIM_2 = 64
N_HEADS = D_MODEL // HEAD_DIM_2
N_KV_HEADS = N_HEADS // 8
GROUP = N_HEADS // N_KV_HEADS
WINDOW = 128
BLOCK = 128
N_BUCKETS = 32
MAX_DISTANCE = 128
D_FF_2 = ((8 * D_MODEL + 3 * 256 - 1) // (3 * 256)) * 256
QKV_WIDTH = (N_HEADS + 2 * N_KV_HEADS) * HEAD_DIM_2
LN_EPS = 1e-5
NEG_INF = -1e30


def rms_norm_2(x, g):
    xf = x.astype(jnp.float32)
    y = xf * lax.rsqrt(jnp.mean(xf * xf, axis=-1, keepdims=True) + RMS_EPS)
    return (y * g.astype(jnp.float32)).astype(x.dtype)

def layer_norm(x, g, b):
    xf = x.astype(jnp.float32)
    mu = jnp.mean(xf, axis=-1, keepdims=True)
    var = jnp.mean(jnp.square(xf - mu), axis=-1, keepdims=True)
    y = (xf - mu) * lax.rsqrt(var + LN_EPS)
    return (y * g.astype(jnp.float32) + b.astype(jnp.float32)).astype(x.dtype)

def t5_bucket(dist):
    max_exact = N_BUCKETS // 2
    d = jnp.maximum(dist, max_exact).astype(jnp.float32)
    large = max_exact + (jnp.log(d / max_exact) / math.log(MAX_DISTANCE / max_exact)
                         * (N_BUCKETS - max_exact)).astype(jnp.int32)
    return jnp.where(dist < max_exact, dist, jnp.minimum(large, N_BUCKETS - 1))

def rel_bias_lookup(rel_bias, dist):
    b = rel_bias.astype(jnp.float32)[t5_bucket(dist)]
    b = jnp.moveaxis(b, -1, -3)
    return b.reshape(b.shape[:-3] + (N_KV_HEADS, GROUP) + b.shape[-2:])

def sink_softmax(scores, sinks):
    sink = jnp.broadcast_to(sinks[None, :, :, None, None], scores.shape[:-1] + (1,))
    p = jax.nn.softmax(jnp.concatenate([scores, sink], axis=-1), axis=-1)
    return p[..., :-1]

def conformer_conv(h, w_in, b_in, w_dw, b_dw, ln_g, ln_b, w_out, b_out):
    u = h @ w_in + b_in
    a, g = jnp.split(u, 2, axis=-1)
    u = a * jax.nn.sigmoid(g)
    u = jnp.pad(u, ((0, 0), (CONV_WIDTH_2 - 1, 0), (0, 0)))
    u = lax.conv_general_dilated(
        u, w_dw[:, None, :].astype(u.dtype), window_strides=(1,), padding='VALID',
        dimension_numbers=('NWC', 'WIO', 'NWC'), feature_group_count=D_MODEL) + b_dw
    u = layer_norm(u, ln_g, ln_b)
    u = jax.nn.silu(u)
    return u @ w_out + b_out

def sliding_window_sink_attention(h, w_qkv, b_qkv, sinks, w_o, b_o, rel_bias):
    B, L, _ = h.shape
    S = L - N_META
    n_blk = S // BLOCK
    qkv = h @ w_qkv + b_qkv
    q, k, v = jnp.split(qkv, [N_HEADS * HEAD_DIM_2, (N_HEADS + N_KV_HEADS) * HEAD_DIM_2], axis=-1)
    q = q.reshape(B, L, N_KV_HEADS, GROUP, HEAD_DIM_2) * (HEAD_DIM_2 ** -0.5)
    k = k.reshape(B, L, N_KV_HEADS, HEAD_DIM_2)
    v = v.reshape(B, L, N_KV_HEADS, HEAD_DIM_2)
    sink_logits = sinks.astype(jnp.float32).reshape(N_KV_HEADS, GROUP)
    q_m, q_r = q[:, :N_META], q[:, N_META:]
    k_m, k_r = k[:, :N_META], k[:, N_META:]
    v_m, v_r = v[:, :N_META], v[:, N_META:]

    d_mm = jnp.arange(N_META)[:, None] - jnp.arange(N_META)[None, :]
    s_mm = (jnp.einsum('bqhgd,bkhd->bhgqk', q_m, k_m).astype(jnp.float32)
            + rel_bias_lookup(rel_bias, jnp.maximum(d_mm, 0)))
    s_mm = jnp.where(d_mm >= 0, s_mm, NEG_INF)
    p_mm = sink_softmax(s_mm, sink_logits).astype(v.dtype)
    o_m = jnp.einsum('bhgqk,bkhd->bqhgd', p_mm, v_m)

    pad = ((0, 0), (BLOCK, 0), (0, 0), (0, 0))
    k_p = jnp.pad(k_r, pad).reshape(B, n_blk + 1, BLOCK, N_KV_HEADS, HEAD_DIM_2)
    v_p = jnp.pad(v_r, pad).reshape(B, n_blk + 1, BLOCK, N_KV_HEADS, HEAD_DIM_2)
    k_band = jnp.concatenate([k_p[:, :-1], k_p[:, 1:]], axis=2)
    v_band = jnp.concatenate([v_p[:, :-1], v_p[:, 1:]], axis=2)
    q_blk = q_r.reshape(B, n_blk, BLOCK, N_KV_HEADS, GROUP, HEAD_DIM_2)

    qpos = jnp.arange(BLOCK)[:, None]
    kpos = jnp.arange(2 * BLOCK)[None, :]
    mpos = jnp.arange(N_META)[None, :]
    d_band = BLOCK + qpos - kpos
    in_window = (d_band >= 0) & (d_band < WINDOW)
    bias_band = rel_bias_lookup(rel_bias, jnp.maximum(d_band, 0))

    def block_fn(args):
        n, q_n, k_n, v_n = args
        valid = in_window & (n * BLOCK + kpos >= BLOCK)
        d_meta = N_META + n * BLOCK + qpos - mpos
        s_meta = (jnp.einsum('bqhgd,bmhd->bhgqm', q_n, k_m).astype(jnp.float32)
                  + rel_bias_lookup(rel_bias, d_meta))
        s_band = jnp.einsum('bqhgd,bjhd->bhgqj', q_n, k_n).astype(jnp.float32) + bias_band
        s_band = jnp.where(valid, s_band, NEG_INF)
        p = sink_softmax(jnp.concatenate([s_meta, s_band], axis=-1), sink_logits).astype(v_n.dtype)
        return (jnp.einsum('bhgqm,bmhd->bqhgd', p[..., :N_META], v_m)
                + jnp.einsum('bhgqj,bjhd->bqhgd', p[..., N_META:], v_n))

    xs = (jnp.arange(n_blk, dtype=jnp.int32), jnp.moveaxis(q_blk, 1, 0),
          jnp.moveaxis(k_band, 1, 0), jnp.moveaxis(v_band, 1, 0))
    o_r = lax.map(block_fn, xs)
    o_r = jnp.moveaxis(o_r, 0, 1).reshape(B, S, N_HEADS * HEAD_DIM_2)
    o = jnp.concatenate([o_m.reshape(B, N_META, N_HEADS * HEAD_DIM_2), o_r], axis=1)
    return o @ w_o + b_o

def swiglu(h, w_gate, w_up, w_down):
    return (jax.nn.silu(h @ w_gate) * (h @ w_up)) @ w_down

def second_inputs(seed: int = 0) -> dict:
    key = jax.random.key(seed)
    ks = list(jax.random.split(key, 24))
    n_conv = len(range(0, DEPTH, N_MIXERS))
    n_attn = len(range(1, DEPTH, N_MIXERS))
    D, F, H = D_MODEL, D_FF_2, N_HEADS * HEAD_DIM_2

    def nrm(k, shape, scale):
        return jax.random.normal(k, shape, jnp.float32) * scale

    def gain(k, shape):
        return 1.0 + nrm(k, shape, 0.02)

    return {
        'x': nrm(ks[0], (BATCH, SEQ, D), 1.0),
        'meta_tokens': nrm(ks[1], (N_META, D), 1.0),
        'rel_bias': nrm(ks[2], (N_BUCKETS, N_HEADS), 0.5),
        'conv_w_in': nrm(ks[3], (n_conv, D, 2 * D), D ** -0.5),
        'conv_b_in': nrm(ks[4], (n_conv, 2 * D), 0.02),
        'conv_w_dw': nrm(ks[5], (n_conv, CONV_WIDTH_2, D), CONV_WIDTH_2 ** -0.5),
        'conv_b_dw': nrm(ks[6], (n_conv, D), 0.02),
        'conv_ln_g': gain(ks[7], (n_conv, D)),
        'conv_ln_b': nrm(ks[8], (n_conv, D), 0.02),
        'conv_w_out': nrm(ks[9], (n_conv, D, D), D ** -0.5),
        'conv_b_out': nrm(ks[10], (n_conv, D), 0.02),
        'attn_w_qkv': nrm(ks[11], (n_attn, D, QKV_WIDTH), D ** -0.5),
        'attn_b_qkv': nrm(ks[12], (n_attn, QKV_WIDTH), 0.02),
        'attn_sinks': nrm(ks[13], (n_attn, N_HEADS), 0.5),
        'attn_w_o': nrm(ks[14], (n_attn, H, D), H ** -0.5),
        'attn_b_o': nrm(ks[15], (n_attn, D), 0.02),
        'norm_mix_pre': gain(ks[16], (DEPTH, D)),
        'norm_mix_post': gain(ks[17], (DEPTH, D)),
        'norm_ffn_pre': gain(ks[18], (DEPTH, D)),
        'norm_ffn_post': gain(ks[19], (DEPTH, D)),
        'ffn_w_gate': nrm(ks[20], (DEPTH, D, F), D ** -0.5),
        'ffn_w_up': nrm(ks[21], (DEPTH, D, F), D ** -0.5),
        'ffn_w_down': nrm(ks[22], (DEPTH, F, D), F ** -0.5),
    }

def second_block(x, meta_tokens, rel_bias, conv_w_in, conv_b_in, conv_w_dw, conv_b_dw,
              conv_ln_g, conv_ln_b, conv_w_out, conv_b_out, attn_w_qkv, attn_b_qkv,
              attn_sinks, attn_w_o, attn_b_o, norm_mix_pre, norm_mix_post,
              norm_ffn_pre, norm_ffn_post, ffn_w_gate, ffn_w_up, ffn_w_down):
    B = x.shape[0]
    meta = jnp.broadcast_to(meta_tokens.astype(x.dtype)[None], (B, N_META, D_MODEL))
    h = jnp.concatenate([meta, x], axis=1)
    for i in range(DEPTH):
        j = i // N_MIXERS
        u = rms_norm_2(h, norm_mix_pre[i])
        if i % N_MIXERS == 0:
            u = conformer_conv(u, conv_w_in[j], conv_b_in[j], conv_w_dw[j], conv_b_dw[j],
                               conv_ln_g[j], conv_ln_b[j], conv_w_out[j], conv_b_out[j])
        else:
            u = sliding_window_sink_attention(u, attn_w_qkv[j], attn_b_qkv[j], attn_sinks[j],
                                              attn_w_o[j], attn_b_o[j], rel_bias)
        h = h + rms_norm_2(u, norm_mix_post[i])
        u = swiglu(rms_norm_2(h, norm_ffn_pre[i]), ffn_w_gate[i], ffn_w_up[i], ffn_w_down[i])
        h = h + rms_norm_2(u, norm_ffn_post[i])
    return h[:, N_META:]


def setup_inputs(seed=0):
    out = dict(first_inputs(seed))
    for name, value in second_inputs(seed + 1).items():
        if name != "x":
            out[name + "_2"] = value
    return out


def reference(
    x, p, g_mix, w_in, g_q, g_k, w_conv, w_attn_out, w_conv_out, w_o, g_mlp, w_up, w_down,
    g_ple, w_ple_gate, w_ple_proj, meta_tokens_2, rel_bias_2, conv_w_in_2, conv_b_in_2,
    conv_w_dw_2, conv_b_dw_2, conv_ln_g_2, conv_ln_b_2, conv_w_out_2, conv_b_out_2,
    attn_w_qkv_2, attn_b_qkv_2, attn_sinks_2, attn_w_o_2, attn_b_o_2, norm_mix_pre_2,
    norm_mix_post_2, norm_ffn_pre_2, norm_ffn_post_2, ffn_w_gate_2, ffn_w_up_2, ffn_w_down_2,
):
    x = first_block(
        x, p, g_mix, w_in, g_q, g_k, w_conv, w_attn_out, w_conv_out, w_o, g_mlp, w_up, w_down,
        g_ple, w_ple_gate, w_ple_proj,
    )
    return second_block(
        x, meta_tokens_2, rel_bias_2, conv_w_in_2, conv_b_in_2, conv_w_dw_2, conv_b_dw_2,
        conv_ln_g_2, conv_ln_b_2, conv_w_out_2, conv_b_out_2, attn_w_qkv_2, attn_b_qkv_2,
        attn_sinks_2, attn_w_o_2, attn_b_o_2, norm_mix_pre_2, norm_mix_post_2, norm_ffn_pre_2,
        norm_ffn_post_2, ffn_w_gate_2, ffn_w_up_2, ffn_w_down_2,
    )


_drawn_inputs = setup_inputs


def setup_inputs(seed=0):
    import zlib

    import numpy as np

    out = dict(_drawn_inputs(seed))
    spreads = {}
    factors = {'g_q': 8.0,
     'g_k': 8.0,
     'g_ple': 8.0,
     'conv_b_in_2': 4.461,
     'conv_b_dw_2': 2.784,
     'conv_ln_g_2': 4.317,
     'conv_ln_b_2': 4.998,
     'conv_b_out_2': 3.063,
     'norm_mix_pre_2': 4.579,
     'norm_mix_post_2': 5.173,
     'norm_ffn_pre_2': 4.368,
     'norm_ffn_post_2': 6.367}
    for name, (base, spread) in spreads.items():
        noise = np.random.default_rng([zlib.crc32(name.encode()), seed]).standard_normal(out[name].shape)
        drawn = base * np.exp(spread * noise) if base else spread * noise
        out[name] = jnp.asarray(drawn.astype(out[name].dtype))
    for name, factor in factors.items():
        out[name] = (out[name] * factor).astype(out[name].dtype)
    return out
```

```python
from contextlib import ExitStack

import concourse.bass as bass
from concourse import mybir

F32 = mybir.dt.float32
F32R = mybir.dt.float32r
ALU = mybir.AluOpType
ACT = mybir.ActivationFunctionType
AX_X = mybir.AxisListType.X
ds = bass.ds

P = 128
D = 2048
T = 256
KT = D // P
HEADS, HD = 8, 128
CONV = 1024
CT = CONV // P
FF1 = 4 * D
PLE = 256
META = 16
TAPS2 = 31
FF2 = 5632
RMS_EPS, LN_EPS = 1e-6, 1e-5
SCALE = HD ** -0.5
NEG = -1e30
RING = 4
UNIT = 1024
HPW = 256
PAD2 = TAPS2 - 1 - META
LEN2 = PAD2 + META + T
XSLOTS = 4


def plan():
    sizes = [("qkv", 12, 4), ("ga", 8, 4), ("ccx", 8, 4), ("cb", 4, 4), ("gc", 8, 4), ("attn_out", 8, 2),
             ("conv_out", 8, 2), ("w_o", 8, 4), ("ple", 8, 0.5)]
    for r in range(4):
        sizes += [(f"up{r}", 8, 4), (f"down{r}", 8, 4)]
    sizes += [("gate", 8, 4), ("conv2", 16, 4), ("out2", 8, 4)]
    for r, pairs in enumerate((8, 8, 6)):
        sizes += [(f"glu{r}", 2 * pairs, 4), (f"back{r}", 8, pairs // 2)]
    at, hp, unit = {}, 0, 0
    for name, n, per in sizes:
        at[name] = (hp, unit)
        hp += n
        unit += int(n * per)
    return at, hp, unit


def two_block_kernel(nc, io, out):
    at, _, UNITS = plan()

    with ExitStack() as ctx:
        def sb(name, shape, dt=F32, where=ctx):
            return where.enter_context(nc.sbuf_tensor(name, shape, dt))

        def sem(name):
            return ctx.enter_context(nc.semaphore(name))

        r = sb("r", [P, KT, T])
        A = sb("A", [P, KT, 2 * T], F32R)
        B = sb("B", [P, KT, 2 * T], F32R)
        stage = sb("stage", [P, RING, UNIT])
        whi = sb("whi", [P, RING, UNIT], F32R)
        wlo = sb("wlo", [P, RING, UNIT], F32R)
        work = sb("work", [P, 12804])
        cross = sb("cross", [P, 2, T])
        cross_meta = sb("cross_meta", [P, 2, META])
        s = sb("s", [P, 2, 2, META + T])
        sq = sb("sq", [P, 2 * T])
        acc = sb("acc", [P, 2 * T])
        var = sb("var", [P, 2 * T])
        root = sb("root", [P, 2 * T])
        rstd = sb("rstd", [P, T])
        ident = sb("ident", [P, P])
        ones = sb("ones", [P, P])
        three = sb("three", [P, 1])
        gv = sb("gv", [P, 2, P])
        taps2 = sb("taps2", [P, KT, TAPS2])
        small = sb("small", [P, 4, 2])
        with ExitStack() as early:
            mask = sb("mask", [P, 3 * P], F32, early)
            S = sb("S", [P, 3 * P], F32, early)
            PT = sb("PT", [P, 3 * P], F32, early)
            vt = sb("vt", [P, 2 * P], F32, early)
            qk = sb("qk", [P, 2, T], F32, early)
            vh = sb("vh", [P, T], F32, early)
        pT = sb("pT", [P, 2, 2 * T], F32R)
        metaA = sb("metaA", [P, KT, 2 * META], F32R)

        gp = ctx.enter_context(nc.psum_tensor("gp", [P, 4, 512], F32))
        xp = ctx.enter_context(nc.psum_tensor("xp", [P, 4, 512], F32))

        def area(a, n, w):
            return work[:, a:a + n * w].rearrange("p (n w) -> p n w", n=n)

        qkv = work[:, 0:24 * T].rearrange("p (a h t) -> p a h t", a=3, h=HEADS)
        qkv_flat = area(0, 24, T)
        GA = area(24 * T, KT, T)
        cr = area(40 * T, CT, T)
        cin = area(48 * T, 2, T + 2)
        GC = area(0, KT, T)
        PP = area(24 * T, KT, T)
        xt = work[:, 24 * T:40 * T].rearrange("p (a d) -> p a d", a=2)
        V1, V2 = work[:, 0:P], work[:, P:2 * P]
        taps_raw = work[0:TAPS2, 4096:4096 + D]
        meta_raw = work[0:META, 16 * T:16 * T + D]
        p_raw = work[:, 40 * T:42 * T].rearrange("p (a d) -> p a d", a=2)
        metaT = work[:, 42 * T:43 * T].rearrange("p (k t) -> p k t", t=META)
        meta_sq = work[:, 43 * T:44 * T].rearrange("p (k t) -> p k t", t=META)
        cin2 = area(0, KT, LEN2)
        V = area(KT * LEN2, KT, T)
        U = area(KT * LEN2 + KT * T, KT, T)
        F = area(0, KT, T)
        ot = work[:, KT * T:3 * KT * T].rearrange("p (a d) -> p a d", a=2)

        vec = {}
        for row, name in enumerate(["g_mix", "g_mlp", "g_ple"]):
            vec[name] = (0, 16 * row)
        vec["b_in"], vec["b_dw"], vec["ln_g"], vec["ln_b"] = (0, 48), (0, 80), (0, 96), (0, 112)
        for row, name in enumerate(["b_out", "mix_pre", "mix_post", "ffn_pre", "ffn_post"]):
            vec[name] = (1, 16 * row)
        vec["g_q"], vec["g_k"], vec["w_conv"] = (1, 80), (1, 81), (1, 82)

        def col(name, i):
            half, c = vec[name]
            return gv[:, half, ds(c + i, 1)]

        loaded = [sem(f"loaded{i}") for i in range(RING)]
        hi_ready, lo_ready, unit_used = sem("hi_ready"), sem("lo_ready"), sem("unit_used")
        cross_out, evacuated = sem("cross_out"), sem("evacuated")
        x_loaded, v_loaded, late_loaded = sem("x_loaded"), sem("v_loaded"), sem("late_loaded")
        consts, consts0 = sem("consts"), sem("consts0")
        x_turned, x_hi, h1_ready = sem("x_turned"), sem("x_hi"), sem("h1_ready")
        vec_turned, vec_ready = sem("vec_turned"), sem("vec_ready")
        acc_ready, squared = sem("acc_ready"), sem("squared")
        stat_ready, var_ready, ln_done, root_ready = sem("stat_ready"), sem("var_ready"), sem("ln_done"), sem("root_ready")
        newton, rstd_ready = sem("newton"), sem("rstd_ready")
        r_updated, r_hi, r_ready = sem("r_updated"), sem("r_hi"), sem("r_ready")
        qk_sq, qk_sum, qk_var, qk_ln, qk_root = sem("qk_sq"), sem("qk_sum"), sem("qk_var"), sem("qk_ln"), sem("qk_root")
        qk_newton, qk_rstd, qk_hat, vh_ready = sem("qk_newton"), sem("qk_rstd"), sem("qk_hat"), sem("vh_ready")
        scored, masked, maxed, neg_max, expd = sem("scored"), sem("masked"), sem("maxed"), sem("neg_max"), sem("expd")
        inv_sum, probs, turned, pt_copied = sem("inv_sum"), sem("probs"), sem("turned"), sem("pt_copied")
        pv_done, attn_hi, attn_ready = sem("pv_done"), sem("attn_hi"), sem("attn_ready")
        qkv_ready, ga_ready, gc_ready = sem("qkv_ready"), sem("ga_ready"), sem("gc_ready")
        cc_normed, cin_ready, cr_step = sem("cc_normed"), sem("cin_ready"), sem("cr_step")
        cb_normed, cb_mul, cb_hi, conv1_ready = sem("cb_normed"), sem("cb_mul"), sem("cb_hi"), sem("conv1_ready")
        ga_sig, ga_y, gc_sig, gc_y = sem("ga_sig"), sem("ga_y"), sem("gc_sig"), sem("gc_y")
        merged, merged_hi, merged_ready = sem("merged"), sem("merged_hi"), sem("merged_ready")
        late_turned, late_hi, p_ready, ple_half = sem("late_turned"), sem("late_hi"), sem("p_ready"), sem("ple_half")
        meta_step, meta_act, meta_sum, meta_hi, meta_ready = (sem("meta_step"), sem("meta_act"), sem("meta_sum"),
                                                              sem("meta_hi"), sem("meta_ready"))
        up_step, up_hi, hidden_ready = sem("up_step"), sem("up_hi"), sem("hidden_ready")
        gate_normed, gate_sig, gate_mul = sem("gate_normed"), sem("gate_sig"), sem("gate_mul")
        cm_out, c2_normed, c2_sig, c2_ready, c2_pad = sem("cm_out"), sem("c2_normed"), sem("c2_sig"), sem("c2_ready"), sem("c2_pad")
        tap_done = sem("tap_done")
        mean_ready, centred, ln_normed, ln_silu, ln_hi, ln_ready = (sem("mean_ready"), sem("centred"), sem("ln_normed"),
                                                                    sem("ln_silu"), sem("ln_hi"), sem("ln_ready"))
        post_normed = sem("post_normed")
        glu_normed, glu_sig, glu_mul, glu_hi, glu_ready = (sem("glu_normed"), sem("glu_sig"), sem("glu_mul"),
                                                           sem("glu_hi"), sem("glu_ready"))
        out_ready, out_turned, stored = sem("out_ready"), sem("out_turned"), sem("stored")
        out_copied = [sem("out_copied0"), sem("out_copied1")]

        def tiles(w):
            return w.rearrange("o (k p) n -> p (o k) n", p=P)

        W = {n: tiles(io[n]) for n in ("w_in", "w_attn_out", "w_conv_out", "w_o", "w_up", "w_down", "w_ple_gate",
                                       "w_ple_proj", "conv_w_in_2", "conv_w_out_2", "ffn_w_gate_2", "ffn_w_up_2",
                                       "ffn_w_down_2")}

        block = ctx.enter_context(nc.Block())

        @block.sync
        def _(sp):
            def load(n, slot, src, first=False):
                if not first:
                    sp.wait_ge(lo_ready, n - RING + 1)
                dst = stage[:, slot, :].rearrange("p (k n) -> p k n", k=src.shape[1])
                sp.dma_start(dst, src).then_inc(loaded[slot], 16)

            def panel(n0, slot0, w, row0, rows, c, first=False):
                for u in range(rows // 4):
                    load(n0 + u, (slot0 + u) % RING, w[:, row0 + 4 * u:row0 + 4 * u + 4, ds(c, HPW)], first)

            def panels(phase, w, its, col0, first_it=0, row0=0):
                n0 = at[phase][1]
                with sp.Fori(first_it, its) as it:
                    for j in range(2):
                        panel(n0 + 8 * it + 4 * j, 0, w, row0, KT, col0 + (2 * it + j) * HPW)

            def pairs(phase, wa, ca, wb, cb, its):
                n0 = at[phase][1]
                with sp.Fori(0, its) as it:
                    panel(n0 + 8 * it, 0, wa, 0, KT, ca + it * HPW)
                    panel(n0 + 8 * it + 4, 0, wb, 0, KT, cb + it * HPW)

            def half_panels(phase, w):
                n0 = at[phase][1]
                with sp.Fori(0, 2) as it:
                    for j in range(4):
                        panel(n0 + 8 * it + 2 * j, 2 * (j % 2), w, 0, 8, (4 * it + j) * HPW)

            win = W["w_in"]
            panel(0, 0, win, 0, KT, 0, first=True)
            panel(4, 0, win, 0, KT, HPW)
            panels("qkv", win, 6, 0, first_it=1)
            panels("ga", win, 4, 6144)
            pairs("ccx", win, 4096, win, 5120, 4)
            panels("cb", win, 2, 3072)
            panels("gc", win, 4, 8192)
            half_panels("attn_out", W["w_attn_out"])
            half_panels("conv_out", W["w_conv_out"])
            sp.wait_ge(cb_mul, 4)
            sp.dma_start(p_raw, io["p"].rearrange("a b (k p) d -> p (a b k) d", p=P)).then_inc(late_loaded, 16)
            sp.wait_ge(vh_ready, HEADS)
            sp.dma_start(meta_raw, io["meta_tokens_2"]).then_inc(late_loaded, 16)
            panels("w_o", W["w_o"], 4, 0)
            with sp.Fori(0, 1) as _it:
                for u in range(4):
                    load(at["ple"][1] + u, u, W["w_ple_proj"][:, 0:2, 512 * u:512 * u + 512])
            with sp.Fori(0, 4) as rnd:
                with sp.Fori(0, 4) as it:
                    for j in range(2):
                        panel(at["up0"][1] + 64 * rnd + 8 * it + 4 * j, 0, W["w_up"], 0, KT,
                              rnd * D + it * (2 * HPW) + j * HPW)
                with sp.Fori(0, 4) as it:
                    for j in range(2):
                        for u in range(4):
                            load(at["down0"][1] + 64 * rnd + 8 * it + 4 * j + u, u,
                                 W["w_down"][:, ds(rnd * KT + 4 * u, 4), ds(it * (2 * HPW) + j * HPW, HPW)])
            panels("gate", W["w_ple_gate"], 4, 0)
            pairs("conv2", W["conv_w_in_2"], 0, W["conv_w_in_2"], D, 8)
            panels("out2", W["conv_w_out_2"], 4, 0)
            for rnd, n in enumerate((8, 8, 6)):
                pairs(f"glu{rnd}", W["ffn_w_gate_2"], rnd * D, W["ffn_w_up_2"], rnd * D, n)
                if n == 8:
                    panels(f"back{rnd}", W["ffn_w_down_2"], 4, 0, row0=rnd * KT)
                else:
                    n0 = at["back2"][1]
                    with sp.Fori(0, 2) as it:
                        for j in range(4):
                            panel(n0 + 12 * it + 3 * j, 3 * j, W["ffn_w_down_2"], 2 * KT, 12, (4 * it + j) * HPW)

        @block.tensor
        def _(pe):
            def step(hp, j, n0, M, kt0=0, units=4, slot0=0, ready=None, after=None, meta=False):
                for u in range(units):
                    slot = (slot0 + u) % RING
                    pe.wait_ge(lo_ready, n0 + u + 1)
                    if u == 0:
                        pe.wait_ge(evacuated, XSLOTS + hp - 1)
                    if ready:
                        pe.wait_ge(ready[0], ready[1] + ready[2] * (u + 1))
                    for k in range(4):
                        kt = kt0 + 4 * u + k
                        first, last = u == 0 and k == 0, u == units - 1 and k == 3
                        for m in range(2):
                            c = k * HPW + m * P
                            hi, lo = whi[:, slot, c:c + P], wlo[:, slot, c:c + P]
                            nc.tensor.matmul(gp[:, 2 * j + m, :], hi, M[:, kt, :], start=first, stop=False)
                            if meta:
                                nc.tensor.matmul(xp[:, 2 * j + m, 0:2 * META], hi, metaA[:, kt, :],
                                                 start=first, stop=False)
                                nc.tensor.matmul(xp[:, 2 * j + m, META:2 * META], lo, metaA[:, kt, 0:META],
                                                 start=False, stop=last)
                            done = nc.tensor.matmul(gp[:, 2 * j + m, T:2 * T], lo, M[:, kt, 0:T],
                                                    start=False, stop=last)
                    done.then_inc(unit_used, 1)
                    if after and u in after:
                        for f in after[u]:
                            f()

            def body(phase, it, M, ready, hooks=None, kt0=0, meta=False):
                hp0, n0 = at[phase]
                for j in range(2):
                    after = {u - 4 * j: f for u, f in (hooks or {}).items() if u // 4 == j}
                    step(hp0 + 2 * it + j, j, n0 + 8 * it + 4 * j, M, kt0, ready=ready, after=after, meta=meta)

            def column_sums(k):
                pe.wait_ge(acc_ready, 9 * (k + 1))
                nc.tensor.matmul(xp[:, 0, 0:T], ones[:], acc[:, 0:T], start=True, stop=False)
                nc.tensor.matmul(xp[:, 0, 0:T], ones[:], acc[:, T:2 * T], start=False, stop=True).then_inc(stat_ready, 1)

            pe.wait_ge(consts, 3)
            pe.wait_ge(x_loaded, 32)
            for c in range(4):
                j = c % 2
                if c >= 2:
                    pe.wait_ge(evacuated, c - 1)
                for kk in range(4):
                    for t in range(2):
                        kt = 4 * c + kk
                        o = (kk % 2) * T + t * P
                        done = nc.tensor.transpose(gp[:, 2 * j + kk // 2, o:o + P], xt[:, t, kt * P:kt * P + P], ident[:])
                done.then_inc(x_turned, 1)
                if c == 0:
                    pe.wait_ge(v_loaded, 16 * 18)
                    nc.tensor.transpose(xp[:, 0, 0:P], V1, ident[:])
                    nc.tensor.transpose(xp[:, 0, P:P + 106], V2[0:106, :], ident[0:106, 0:106]).then_inc(vec_turned, 1)
            for k in range(KT):
                done = nc.tensor.transpose(xp[:, 1, k * TAPS2:(k + 1) * TAPS2], taps_raw[:, k * P:k * P + P],
                                           ident[0:TAPS2, 0:TAPS2])
            done.then_inc(vec_turned, 1)

            def first_half(h):
                def norms():
                    pe.wait_ge(qk_sq, h + 1)
                    if not isinstance(h, int) or h >= 1:
                        pe.wait_ge(qk_var, h)
                    nc.tensor.matmul(xp[:, 0, :], ones[:], sq[:], start=True, stop=True).then_inc(qk_sum, 1)

                def scores():
                    pe.wait_ge(qk_hat, 2 * h + 2)
                    if not isinstance(h, int) or h >= 1:
                        pe.wait_ge(masked, h)
                    nc.tensor.matmul(xp[:, 1, 0:P], qk[:, 0, 0:P], qk[:, 1, 0:P], start=True, stop=True)
                    nc.tensor.matmul(xp[:, 1, P:3 * P], qk[:, 0, P:T], qk[:, 1, :], start=True, stop=True).then_inc(scored, 1)
                return {0: [norms], 5: [scores]}

            def second_half(h):
                def turn():
                    pe.wait_ge(probs, 2 * h + 2)
                    pe.wait_ge(vh_ready, h + 1)
                    if not isinstance(h, int) or h >= 1:
                        pe.wait_ge(attn_ready, h)
                    for c in range(3):
                        nc.tensor.transpose(xp[:, 2, c * P:c * P + P], S[:, c * P:c * P + P], ident[:])
                    nc.tensor.transpose(xp[:, 3, 0:P], vh[:, 0:P], ident[:])
                    nc.tensor.transpose(xp[:, 3, P:2 * P], vh[:, P:2 * P], ident[:]).then_inc(turned, 1)

                def pv():
                    pe.wait_ge(pt_copied, 2 * h + 2)
                    nc.tensor.matmul(xp[:, 3, T:2 * T], vt[:, 0:P], PT[:, 0:2 * P], start=True, stop=False)
                    nc.tensor.matmul(xp[:, 3, T + P:2 * T], vt[:, P:2 * P], PT[:, 2 * P:3 * P], start=False,
                                     stop=True).then_inc(pv_done, 1)
                return {1: [turn], 3: [pv]}

            h1 = (h1_ready, 0, 4)
            body("qkv", 0, A, h1, {2: [lambda: column_sums(0)]})
            with pe.Fori(1, 6) as it:
                body("qkv", it, A, h1)
            body("ga", 0, A, h1, first_half(0))
            with pe.Fori(1, 4) as it:
                body("ga", it, A, h1, {**first_half(it), **second_half(it - 1)})
            with pe.Fori(0, 4) as it:
                body("ccx", it, A, h1, {**first_half(it + 4), **second_half(it + 3)})
            body("cb", 0, A, h1, second_half(7))
            body("cb", 1, A, h1)
            with pe.Fori(0, 4) as it:
                body("gc", it, A, h1)

            for phase, kt0, ready in (("attn_out", 0, (attn_ready, HEADS, 0)), ("conv_out", CT, (conv1_ready, 0, 2))):
                hp0, n0 = at[phase]
                with pe.Fori(0, 2) as it:
                    for j in range(4):
                        step(hp0 + 4 * it + j, j % 2, n0 + 8 * it + 2 * j, B, kt0, 2, 2 * (j % 2), ready)
            pe.wait_ge(late_loaded, 32)
            for k in range(2):
                for t in range(2):
                    nc.tensor.transpose(xp[:, 1, k * T + t * P:k * T + t * P + P], p_raw[:, t, k * P:k * P + P], ident[:])
            for k in range(KT):
                done = nc.tensor.transpose(xp[:, 2, k * META:(k + 1) * META], meta_raw[:, k * P:k * P + P],
                                           ident[0:META, 0:META])
            done.then_inc(late_turned, 1)
            with pe.Fori(0, 4) as it:
                body("w_o", it, A, (merged_ready, 0, 2))
            pe.wait_ge(meta_step, 1)
            for k in range(KT):
                done = nc.tensor.matmul(xp[:, 1, 0:META], ones[:], meta_sq[:, k, :], start=(k == 0), stop=(k == KT - 1))
            done.then_inc(meta_sum, 1)
            pe.wait_ge(p_ready, 1)
            hp0, n0 = at["ple"]
            for u in range(4):
                pe.wait_ge(lo_ready, n0 + u + 1)
                for j in range(2):
                    pe.wait_ge(evacuated, XSLOTS + hp0 + 2 * u + j - 1)
                    for k in range(2):
                        for m in range(2):
                            c = k * 512 + (2 * j + m) * P
                            nc.tensor.matmul(gp[:, 2 * j + m, :], whi[:, u, c:c + P], pT[:, k, :],
                                             start=(k == 0), stop=False)
                            done = nc.tensor.matmul(gp[:, 2 * j + m, T:2 * T], wlo[:, u, c:c + P], pT[:, k, 0:T],
                                                    start=False, stop=(k == 1))
                    done.then_inc([ple_half, unit_used][j], 1)
            column_sums(1)
            with pe.Fori(0, 4) as rnd:
                for phase, M, ready in (("up0", B, (r_ready, 0, 4)), ("down0", A, (hidden_ready, 8 * rnd, 2))):
                    hp0, n0 = at[phase]
                    with pe.Fori(0, 4) as it:
                        for j in range(2):
                            step(hp0 + 16 * rnd + 2 * it + j, j, n0 + 64 * rnd + 8 * it + 4 * j, M, ready=ready)
            body("gate", 0, B, (r_ready, 16, 4), {2: [lambda: column_sums(2)]})
            with pe.Fori(1, 4) as it:
                body("gate", it, B, (r_ready, 16, 4))
            pe.wait_ge(meta_ready, 1)

            def conv2(it):
                hp0, n0 = at["conv2"]
                for j in range(2):
                    step(hp0 + 2 * it + j, j, n0 + 8 * it + 4 * j, A, ready=(r_ready, 32, 4), meta=True)

            column_sums(3)
            pe.wait_ge(var_ready, 4)
            with pe.Fori(0, 8) as it:
                conv2(it)
            pe.wait_ge(c2_normed, 16)
            column_sums(4)
            column_sums(5)
            with pe.Fori(0, 4) as it:
                body("out2", it, B, (ln_ready, 0, 2))
            column_sums(6)
            body("glu0", 0, A, (r_ready, 48, 4), {2: [lambda: column_sums(7)]})
            with pe.Fori(1, 8) as it:
                body("glu0", it, A, (r_ready, 48, 4))
            with pe.Fori(0, 4) as it:
                body("back0", it, B, (glu_ready, 0, 2))
            with pe.Fori(0, 8) as it:
                body("glu1", it, A, (r_ready, 48, 4))
            with pe.Fori(0, 4) as it:
                body("back1", it, B, (glu_ready, 8, 2))
            with pe.Fori(0, 6) as it:
                body("glu2", it, A, (r_ready, 48, 4))
            hp0, n0 = at["back2"]
            with pe.Fori(0, 2) as it:
                for j in range(4):
                    step(hp0 + 4 * it + j, j % 2, n0 + 12 * it + 3 * j, B, 0, 3, 3 * j, (glu_ready, 16, 2))
            column_sums(8)
            pe.wait_ge(evacuated, XSLOTS + hp0 + 8)
            pe.wait_ge(var_ready, 8)
            for c in range(4):
                pe.wait_ge(out_ready, 4 * c + 4)
                for t in range(2):
                    for kk in range(4):
                        bank = (gp if c < 2 else xp)[:, 2 * (c % 2) + t, kk * P:kk * P + P]
                        done = nc.tensor.transpose(bank, r[:, 4 * c + kk, t * P:t * P + P], ident[:])
                done.then_inc(out_turned, 1)

        @block.scalar
        def _(act):
            def take_hi(n, q, slot):
                act.wait_ge(loaded[slot], 16 * q + 16)
                if not isinstance(n, int) or n >= RING:
                    act.wait_ge(unit_used, n - RING + 1)
                nc.scalar.activation(whi[:, slot, :], stage[:, slot, :], ACT.Copy).then_inc(hi_ready, 1)

            def convert(n0, q0, units=4, slot0=0):
                for u in range(units):
                    if not isinstance(n0, int) or n0 + u + RING < UNITS:
                        take_hi(n0 + u + RING, q0 + 1 + (slot0 + u) // RING, (slot0 + u) % RING)

            def take_cross(hp, j, units_done, waited=None, bias=None):
                act.wait_ge(*(waited or (unit_used, units_done)))
                act.wait_ge(evacuated, XSLOTS + hp)
                if bias is None:
                    nc.scalar.activation(cross[:], gp[:, 2 * j:2 * j + 2, T:2 * T], ACT.Copy).then_inc(cross_out, 1)
                else:
                    for m in range(2):
                        last = nc.scalar.activation(cross[:, m, :], gp[:, 2 * j + m, T:2 * T], ACT.Identity, bias=bias(m))
                    last.then_inc(cross_out, 1)

            def body(phase, it, tail, units=None):
                hp0, n0 = at[phase]
                for j in range(2):
                    n = n0 + 8 * it + 4 * j
                    for u in range(4):
                        take_hi(n + RING + u, n0 // RING + 2 * it + j + 1, u)
                        if units and 4 * j + u in units:
                            for f in units[4 * j + u]:
                                f()
                    take_cross(hp0 + 2 * it + j, j, n + 4)
                    tail(it, j)

            def none(it, j):
                pass

            def root_of(k):
                act.wait_ge(var_ready, k + 1)
                nc.scalar.activation(root[:, 0:T], var[:, 0:T], ACT.Ln).then_inc(ln_done, 1)
                act.wait_ge(ln_done, k + 1)
                nc.scalar.activation(root[:, 0:T], root[:, 0:T], ACT.Exp, scale=-0.5).then_inc(root_ready, 1)

            for t in range(2):
                act.dma_start(xt[:, t, :], io["x"].rearrange("b (a p) d -> p (b a) d", p=P)[:, t, :]).then_inc(x_loaded, 16)
            order = [("g_mix", 0, 0), ("g_mlp", 0, 16), ("g_ple", 0, 32), ("conv_b_in_2", 0, 48), ("conv_b_dw_2", 0, 80),
                     ("conv_ln_g_2", 0, 96), ("conv_ln_b_2", 0, 112), ("conv_b_out_2", 1, 0), ("norm_mix_pre_2", 1, 16),
                     ("norm_mix_post_2", 1, 32), ("norm_ffn_pre_2", 1, 48), ("norm_ffn_post_2", 1, 64), ("g_q", 1, 80),
                     ("g_k", 1, 81)]
            for name, half, row in order:
                n = io[name].shape[1] // P
                act.dma_start([V1, V2][half][row:row + n, :], io[name].rearrange("o (k p) -> (o k) p", p=P)).then_inc(v_loaded, 16)
            for t in range(3):
                act.dma_start(V2[82 + 8 * t:90 + 8 * t, :], io["w_conv"][0, t:t + 1, :].rearrange("o (k p) -> (o k) p", p=P)).then_inc(v_loaded, 16)
            act.dma_start(taps_raw, io["conv_w_dw_2"].rearrange("o t d -> (o t) d")).then_inc(v_loaded, 16)

            act.wait_ge(vec_turned, 1)
            nc.scalar.activation(gv[:, 0, :], xp[:, 0, 0:P], ACT.Copy)
            nc.scalar.activation(gv[:, 1, 0:106], xp[:, 0, P:P + 106], ACT.Copy).then_inc(vec_ready, 1)
            act.wait_ge(vec_ready, 1)
            for c in range(4):
                act.wait_ge(x_turned, c + 1)
                j = c % 2
                nc.scalar.activation(r[:, 4 * c:4 * c + 4, :].rearrange("p (a b) t -> p a (b t)", a=2),
                                     gp[:, 2 * j:2 * j + 2, :], ACT.Copy).then_inc(evacuated, 1)
                act.wait_ge(evacuated, c + 1)
                for kt in range(4 * c, 4 * c + 4):
                    nc.scalar.activation(A[:, kt, 0:T], r[:, kt, :], ACT.Copy, scale=col("g_mix", kt)).then_inc(x_hi, 1)
                take_hi(c, 0, c)
            act.wait_ge(vec_turned, 2)
            nc.scalar.activation(taps2[:].rearrange("p k t -> p (k t)"), xp[:, 1, 0:KT * TAPS2], ACT.Copy).then_inc(vec_ready, 1)

            def first_half(h):
                def roots():
                    act.wait_ge(qk_var, h + 1)
                    nc.scalar.activation(root[:], var[:], ACT.Ln).then_inc(qk_ln, 1)
                    act.wait_ge(qk_ln, h + 1)
                    nc.scalar.activation(root[:], root[:], ACT.Exp, scale=-0.5).then_inc(qk_root, 1)

                def exps():
                    act.wait_ge(neg_max, h + 1)
                    for qt, (a, b) in enumerate(((0, P), (P, 3 * P))):
                        nc.scalar.activation(S[:, a:b], S[:, a:b], ACT.Exp, bias=small[:, 1, qt:qt + 1], scale=SCALE,
                                             accum_out=small[:, 2, qt:qt + 1]).then_inc(expd, 1)
                return {2: [roots], 7: [exps]}

            def second_half(h):
                def copies():
                    act.wait_ge(turned, h + 1)
                    nc.scalar.activation(PT[:], xp[:, 2, 0:3 * P], ACT.Copy).then_inc(pt_copied, 1)
                    nc.scalar.activation(vt[:], xp[:, 3, 0:2 * P], ACT.Copy).then_inc(pt_copied, 1)

                def hi():
                    act.wait_ge(pv_done, h + 1)
                    nc.scalar.activation(B[:, ds(h, 1), 0:T], xp[:, 3:4, T:2 * T], ACT.Copy).then_inc(attn_hi, 1)
                return {2: [copies], 4: [hi]}

            def both(a, b):
                return {u: b.get(u, []) + a.get(u, []) for u in {*a, *b}}

            body("qkv", 0, none, {3: [lambda: root_of(0)]})
            with act.Fori(1, 6) as it:
                body("qkv", it, none)
            body("ga", 0, none, first_half(0))
            with act.Fori(1, 4) as it:
                body("ga", it, none, both(first_half(it), second_half(it - 1)))
            with act.Fori(0, 4) as it:
                body("ccx", it, none, both(first_half(it + 4), second_half(it + 3)))

            def cb_tail(it, j):
                hp = 2 * it + j
                act.wait_ge(cb_mul, hp + 1)
                nc.scalar.activation(B[:, ds(CT + 2 * hp, 2), 0:T], s[:, j, :, 0:T], ACT.Copy).then_inc(cb_hi, 1)

            body("cb", 0, cb_tail, second_half(7))
            body("cb", 1, cb_tail)
            with act.Fori(0, 4) as it:
                body("gc", it, none)

            def attn_out_tail(hp, j):
                act.wait_ge(ga_ready, 8)
                nc.scalar.activation(GA[:, ds(2 * hp, 2), :], GA[:, ds(2 * hp, 2), :], ACT.Sigmoid).then_inc(ga_sig, 1)

            def conv_out_tail(hp, j):
                act.wait_ge(gc_ready, 8)
                nc.scalar.activation(GC[:, ds(2 * hp, 2), :], GC[:, ds(2 * hp, 2), :], ACT.Sigmoid).then_inc(gc_sig, 1)
                act.wait_ge(merged, hp + 1)
                nc.scalar.activation(A[:, ds(2 * hp, 2), 0:T], s[:, j % 2, :, 0:T], ACT.Copy).then_inc(merged_hi, 1)

            for phase, tail in (("attn_out", attn_out_tail), ("conv_out", conv_out_tail)):
                hp0, n0 = at[phase]
                with act.Fori(0, 2) as it:
                    for j in range(4):
                        n = n0 + 8 * it + 2 * j
                        convert(n, n0 // RING + 2 * it, 2, 2 * j)
                        take_cross(hp0 + 4 * it + j, j % 2, n + 2)
                        tail(4 * it + j, j)

            act.wait_ge(late_turned, 1)
            nc.scalar.activation(pT[:, :, 0:T], xp[:, 1, :].rearrange("p (k t) -> p k t", k=2), ACT.Copy).then_inc(late_hi, 1)
            nc.scalar.activation(metaT[:].rearrange("p k t -> p (k t)"), xp[:, 2, 0:KT * META], ACT.Copy).then_inc(late_hi, 1)

            def hi_of_r(c0, M, gain, hp):
                act.wait_ge(r_updated, c0 + hp + 1)
                for m in range(2):
                    nc.scalar.activation(M[:, ds(2 * hp + m, 1), 0:T], r[:, ds(2 * hp + m, 1), :], ACT.Copy,
                                         scale=col(gain, 2 * hp + m)).then_inc(r_hi, 1)

            with act.Fori(0, 4) as it:
                body("w_o", it, lambda it, j: hi_of_r(0, B, "g_mlp", 2 * it + j))
            hp0, n0 = at["ple"]
            for u in range(4):
                take_hi(n0 + u + RING, n0 // RING + 1, u)
                take_cross(hp0 + 2 * u, 0, None, (ple_half, u + 1))
                take_cross(hp0 + 2 * u + 1, 1, n0 + u + 1)
            act.wait_ge(meta_step, 2)
            nc.scalar.activation(root[:, T:T + META], var[:, T:T + META], ACT.Ln).then_inc(meta_act, 1)
            act.wait_ge(meta_act, 1)
            nc.scalar.activation(root[:, T:T + META], root[:, T:T + META], ACT.Exp, scale=-0.5).then_inc(meta_act, 1)
            root_of(1)

            def ffn1(rnd, last):
                hp0, n0 = at["up0"]
                with act.Fori(0, 4) as it:
                    for j in range(2):
                        n = n0 + 64 * rnd + 8 * it + 4 * j
                        convert(n, n0 // RING + 16 * rnd + 2 * it + j)
                        take_cross(hp0 + 16 * rnd + 2 * it + j, j, n + 4)
                        act.wait_ge(up_step, 16 * rnd + 4 * it + 2 * j + 2)
                        nc.scalar.activation(A[:, ds(4 * it + 2 * j, 2), 0:T], s[:, j, :, 0:T], ACT.Copy).then_inc(up_hi, 1)
                hp0, n0 = at["down0"]
                with act.Fori(0, 4) as it:
                    for j in range(2):
                        n = n0 + 64 * rnd + 8 * it + 4 * j
                        convert(n, n0 // RING + 16 * rnd + 2 * it + j)
                        take_cross(hp0 + 16 * rnd + 2 * it + j, j, n + 4)
                        if last:
                            hi_of_r(32, B, "g_ple", 2 * it + j)

            with act.Fori(0, 3) as rnd:
                ffn1(rnd, False)
            ffn1(3, True)

            def gate_tail(it, j):
                hp = 2 * it + j
                act.wait_ge(gate_normed, hp + 1)
                nc.scalar.activation(s[:, j, :, 0:T], s[:, j, :, 0:T], ACT.Sigmoid).then_inc(gate_sig, 1)
                hi_of_r(40, A, "mix_pre", hp)

            body("gate", 0, gate_tail, {3: [lambda: root_of(2)]})
            with act.Fori(1, 4) as it:
                body("gate", it, gate_tail)
            act.wait_ge(meta_step, 19)
            nc.scalar.activation(metaA[:, :, 0:META], metaT, ACT.Copy).then_inc(meta_hi, 1)
            root_of(3)

            def conv2(it):
                hp0, n0 = at["conv2"]
                for j in range(2):
                    n, hp = n0 + 8 * it + 4 * j, hp0 + 2 * it + j
                    convert(n, n0 // RING + 2 * it + j)
                    act.wait_ge(unit_used, n + 4)
                    act.wait_ge(evacuated, XSLOTS + hp)
                    nc.scalar.activation(cross_meta[:], xp[:, 2 * j:2 * j + 2, META:2 * META], ACT.Copy).then_inc(cm_out, 1)
                    take_cross(hp, j, n + 4)
                act.wait_ge(c2_normed, 2 * it + 2)
                for m in range(2):
                    nc.scalar.activation(s[:, 1, m, :], s[:, 1, m, :], ACT.Sigmoid,
                                         bias=col("b_in", KT + 2 * it + m)).then_inc(c2_sig, 1)

            with act.Fori(0, 8) as it:
                conv2(it)
            root_of(4)
            for c in range(8):
                act.wait_ge(ln_normed, c + 1)
                for kt in (2 * c, 2 * c + 1):
                    nc.scalar.activation(V[:, kt, :], V[:, kt, :], ACT.Silu, scale=col("ln_g", kt),
                                         bias=col("ln_b", kt)).then_inc(ln_silu, 1)
                act.wait_ge(ln_silu, 2 * c + 2)
                nc.scalar.activation(B[:, 2 * c:2 * c + 2, 0:T], V[:, 2 * c:2 * c + 2, :], ACT.Copy).then_inc(ln_hi, 1)

            hp0, n0 = at["out2"]
            with act.Fori(0, 4) as it:
                for j in range(2):
                    n = n0 + 8 * it + 4 * j
                    convert(n, n0 // RING + 2 * it + j)
                    take_cross(hp0 + 2 * it + j, j, n + 4, bias=lambda m: col("b_out", 4 * it + 2 * j + m))
            root_of(5)
            for hp in range(8):
                hi_of_r(48, A, "ffn_pre", hp)

            def glu(rnd, it, units=None, hp_done=0):
                def tail(it, j):
                    if j == 1:
                        c = hp_done + it
                        act.wait_ge(glu_normed, c + 1)
                        nc.scalar.activation(root[:].rearrange("p (m t) -> p m t", m=2), s[:, 0, :, 0:T],
                                             ACT.Sigmoid).then_inc(glu_sig, 1)
                        act.wait_ge(glu_mul, 2 * c + 2)
                        nc.scalar.activation(B[:, ds(2 * it, 2), 0:T], s[:, 0, :, 0:T], ACT.Copy).then_inc(glu_hi, 1)
                body(f"glu{rnd}", it, tail, units)

            glu(0, 0, {3: [lambda: root_of(6)]})
            with act.Fori(1, 8) as it:
                glu(0, it)
            with act.Fori(0, 4) as it:
                body("back0", it, none)
            with act.Fori(0, 8) as it:
                glu(1, it, None, 8)
            with act.Fori(0, 4) as it:
                body("back1", it, none)
            with act.Fori(0, 6) as it:
                glu(2, it, None, 16)
            hp0, n0 = at["back2"]
            for h in range(8):
                convert(n0 + 3 * h, n0 // RING, 3, 3 * h)
                take_cross(hp0 + h, h % 2, n0 + 3 * h + 3)
            root_of(7)
            for c in range(4):
                act.wait_ge(out_turned, c + 1)
                bank = (gp if c < 2 else xp)[:, 2 * (c % 2), :]
                nc.scalar.activation(ot[:, 0, 512 * c:512 * c + 512], bank, ACT.Copy).then_inc(out_copied[0], 1)
                for t in range(2):
                    act.wait_ge(out_copied[t], c + 1)
                act.dma_start(out.rearrange("b (a p) d -> p (b a) d", p=P)[:, :, 512 * c:512 * c + 512],
                              ot[:, :, 512 * c:512 * c + 512]).then_inc(stored, 16)
            act.wait_ge(stored, 64)

        @block.vector
        def _(dve):
            def take_lo(n, slot):
                dve.wait_ge(hi_ready, n + 1)
                nc.vector.tensor_tensor(wlo[:, slot, :], stage[:, slot, :], whi[:, slot, :].bitcast(F32),
                                        ALU.subtract).then_inc(lo_ready, 1)

            def convert(n0, units=4, slot0=0):
                for u in range(units):
                    if not isinstance(n0, int) or n0 + u + RING < UNITS:
                        take_lo(n0 + u + RING, (slot0 + u) % RING)

            def add_up(hp, j, dst):
                dve.wait_ge(cross_out, hp + 1)
                nc.vector.tensor_tensor(dst, gp[:, 2 * j:2 * j + 2, 0:T], cross[:], ALU.add).then_inc(evacuated, 1)
                dve.wait_ge(evacuated, XSLOTS + hp + 1)

            def by_rstd(n=2):
                return rstd[:].unsqueeze(1).broadcast_to([P, n, T])

            def body(phase, it, tail, units=None):
                hp0, n0 = at[phase]
                for j in range(2):
                    for u in range(4):
                        take_lo(n0 + 8 * it + 4 * j + RING + u, u)
                        if units and 4 * j + u in units:
                            for f in units[4 * j + u]:
                                f()
                    tail(hp0 + 2 * it + j, it, j)

            def variance(k, n, eps):
                dve.wait_ge(stat_ready, n + 1)
                nc.vector.tensor_scalar(var[:, 0:T], xp[:, 0, 0:T], 4.0 / D, 4.0 * eps, ALU.mult, ALU.add).then_inc(var_ready, 1)
                dve.wait_ge(rstd_ready, k + 1)

            def lo_of_r(c0, M, gain, hp):
                for m in range(2):
                    dve.wait_ge(r_hi, 2 * c0 + 2 * hp + m + 1)
                    nc.vector.scalar_tensor_tensor(M[:, ds(2 * hp + m, 1), T:2 * T], r[:, ds(2 * hp + m, 1), :],
                                                   col(gain, 2 * hp + m), M[:, ds(2 * hp + m, 1), 0:T].bitcast(F32),
                                                   ALU.mult, ALU.subtract).then_inc(r_ready, 1)

            dve.wait_ge(vec_ready, 1)
            for c in range(4):
                for kt in range(4 * c, 4 * c + 4):
                    dve.wait_ge(x_hi, kt + 1)
                    nc.vector.scalar_tensor_tensor(A[:, kt, T:2 * T], r[:, kt, :], col("g_mix", kt),
                                                   A[:, kt, 0:T].bitcast(F32), ALU.mult, ALU.subtract).then_inc(h1_ready, 1)
                take_lo(c, c)

            def normed_into(dst, ready):
                def tail(hp, it, j):
                    d = dst(it, j)
                    add_up(hp, j, d)
                    nc.vector.tensor_tensor(d, d, by_rstd(), ALU.mult).then_inc(ready, 1)
                return tail

            def first_half(h):
                def variances():
                    dve.wait_ge(qk_sum, h + 1)
                    if not isinstance(h, int) or h >= 1:
                        dve.wait_ge(qk_rstd, h)
                    nc.vector.tensor_scalar(var[:], xp[:, 0, :], 4.0 / HD, 4.0 * RMS_EPS, ALU.mult, ALU.add).then_inc(qk_var, 1)

                def hats():
                    dve.wait_ge(qk_rstd, h + 1)
                    if not isinstance(h, int) or h >= 1:
                        dve.wait_ge(scored, h)
                    for i, g in enumerate(("g_q", "g_k")):
                        nc.vector.scalar_tensor_tensor(qk[:, i:i + 1, :], qkv[:, i, ds(h, 1), :], col(g, 0),
                                                       root[:, i * T:(i + 1) * T].unsqueeze(1), ALU.mult, ALU.mult).then_inc(qk_hat, 1)

                def maxima():
                    dve.wait_ge(scored, h + 1)
                    if not isinstance(h, int) or h >= 1:
                        dve.wait_ge(turned, h)
                    nc.vector.tensor_tensor(S[:], xp[:, 1, 0:3 * P], mask[:], ALU.add).then_inc(masked, 1)
                    dve.wait_ge(masked, h + 1)
                    nc.vector.tensor_reduce(small[:, 0, 0:1], S[:, 0:P], AX_X, ALU.max).then_inc(maxed, 1)
                    nc.vector.tensor_reduce(small[:, 0, 1:2], S[:, P:3 * P], AX_X, ALU.max).then_inc(maxed, 1)
                    dve.wait_ge(maxed, 2 * h + 2)
                    nc.vector.tensor_scalar(small[:, 1, :], small[:, 0, :], -SCALE, None, ALU.mult).then_inc(neg_max, 1)

                def probabilities():
                    dve.wait_ge(expd, 2 * h + 2)
                    nc.vector.reciprocal(small[:, 3, :], small[:, 2, :]).then_inc(inv_sum, 1)
                    dve.wait_ge(inv_sum, h + 1)
                    for qt, (a, b) in enumerate(((0, P), (P, 3 * P))):
                        nc.vector.tensor_scalar(S[:, a:b], S[:, a:b], small[:, 3, qt:qt + 1], None, ALU.mult).then_inc(probs, 1)
                return {1: [variances], 4: [hats], 6: [maxima], 7: [probabilities]}

            def second_half(h):
                def lo():
                    dve.wait_ge(attn_hi, h + 1)
                    nc.vector.tensor_tensor(B[:, ds(h, 1), T:2 * T], xp[:, 3:4, T:2 * T], B[:, ds(h, 1), 0:T].bitcast(F32),
                                            ALU.subtract).then_inc(attn_ready, 1)
                return {5: [lo]}

            qkv_tail = normed_into(lambda it, j: qkv_flat[:, ds(4 * it + 2 * j, 2), :], qkv_ready)
            body("qkv", 0, qkv_tail, {3: [lambda: variance(0, 0, RMS_EPS)]})
            with dve.Fori(1, 6) as it:
                body("qkv", it, qkv_tail)
            ga_tail = normed_into(lambda it, j: GA[:, ds(4 * it + 2 * j, 2), :], ga_ready)
            body("ga", 0, ga_tail, first_half(0))
            with dve.Fori(1, 4) as it:
                body("ga", it, ga_tail, {**first_half(it), **second_half(it - 1)})

            def ccx_tail(hp, it, j):
                add_up(hp, j, s[:, j, :, 0:T])
                if j == 0:
                    return
                four = s[:].rearrange("p j m t -> p (j m) t")[:, :, 0:T]
                nc.vector.tensor_tensor(four, four, by_rstd(4), ALU.mult).then_inc(cc_normed, 1)
                dve.wait_ge(cc_normed, it + 1)
                nc.vector.tensor_tensor(cin[:, :, 2:T + 2], s[:, 0, :, 0:T], s[:, 1, :, 0:T], ALU.mult).then_inc(cin_ready, 1)
                dve.wait_ge(cin_ready, it + 1)
                for tap in range(3):
                    for m in range(2):
                        o, i = cr[:, ds(2 * it + m, 1), :], cin[:, m:m + 1, tap:tap + T]
                        w = col("w_conv", 8 * tap + 2 * it + m)
                        if tap == 0:
                            nc.vector.tensor_scalar(o, i, w, None, ALU.mult).then_inc(cr_step, 1)
                        else:
                            dve.wait_ge(cr_step, 6 * it + 2 * (tap - 1) + m + 1)
                            nc.vector.scalar_tensor_tensor(o, i, w, o, ALU.mult, ALU.add).then_inc(cr_step, 1)

            dve.wait_ge(consts, 4)
            with dve.Fori(0, 4) as it:
                body("ccx", it, ccx_tail, {**first_half(it + 4), **second_half(it + 3)})

            def cb_tail(hp, it, j):
                t = s[:, j, :, 0:T]
                add_up(hp, j, t)
                nc.vector.tensor_tensor(t, t, by_rstd(), ALU.mult).then_inc(cb_normed, 1)
                dve.wait_ge(cb_normed, 2 * it + j + 1)
                dve.wait_ge(cr_step, 24)
                nc.vector.tensor_tensor(t, t, cr[:, ds(4 * it + 2 * j, 2), :], ALU.mult).then_inc(cb_mul, 1)
                dve.wait_ge(cb_hi, 2 * it + j + 1)
                o = ds(CT + 4 * it + 2 * j, 2)
                nc.vector.tensor_tensor(B[:, o, T:2 * T], t, B[:, o, 0:T].bitcast(F32), ALU.subtract).then_inc(conv1_ready, 2)

            body("cb", 0, cb_tail, second_half(7))
            body("cb", 1, cb_tail)
            gc_tail = normed_into(lambda it, j: GC[:, ds(4 * it + 2 * j, 2), :], gc_ready)
            with dve.Fori(0, 4) as it:
                body("gc", it, gc_tail)

            def attn_out_tail(hp, h, j):
                t, g = s[:, j, :, 0:T], GA[:, ds(2 * h, 2), :]
                add_up(hp, j, t)
                dve.wait_ge(ga_sig, h + 1)
                nc.vector.tensor_tensor(g, g, t, ALU.mult).then_inc(ga_y, 1)

            def conv_out_tail(hp, h, j):
                t = s[:, j, :, 0:T]
                add_up(hp, j, t)
                dve.wait_ge(gc_sig, h + 1)
                nc.vector.tensor_tensor(t, t, GC[:, ds(2 * h, 2), :], ALU.mult).then_inc(gc_y, 1)
                dve.wait_ge(gc_y, h + 1)
                dve.wait_ge(ga_y, 8)
                nc.vector.tensor_tensor(t, t, GA[:, ds(2 * h, 2), :], ALU.add).then_inc(merged, 1)
                dve.wait_ge(merged_hi, h + 1)
                nc.vector.tensor_tensor(A[:, ds(2 * h, 2), T:2 * T], t, A[:, ds(2 * h, 2), 0:T].bitcast(F32),
                                        ALU.subtract).then_inc(merged_ready, 1)

            for phase, tail in (("attn_out", attn_out_tail), ("conv_out", conv_out_tail)):
                hp0, n0 = at[phase]
                with dve.Fori(0, 2) as it:
                    for j in range(4):
                        convert(n0 + 8 * it + 2 * j, 2, 2 * j)
                        tail(hp0 + 4 * it + j, 4 * it + j, j % 2)

            dve.wait_ge(late_hi, 2)
            nc.vector.tensor_tensor(pT[:, :, T:2 * T], xp[:, 1, :].rearrange("p (k t) -> p k t", k=2),
                                    pT[:, :, 0:T].bitcast(F32), ALU.subtract).then_inc(p_ready, 1)
            nc.vector.tensor_tensor(meta_sq, metaT, metaT, ALU.mult).then_inc(meta_step, 1)

            def update_r(hp, h, j, c0, M, gain):
                t, rr = s[:, j, :, 0:T], r[:, ds(2 * h, 2), :]
                add_up(hp, j, t)
                nc.vector.tensor_tensor(rr, rr, t, ALU.add).then_inc(r_updated, 1)
                if M is not None:
                    lo_of_r(c0, M, gain, h)

            with dve.Fori(0, 4) as it:
                body("w_o", it, lambda hp, it, j: update_r(hp, 2 * it + j, j, 0, B, "g_mlp"))
            hp0, n0 = at["ple"]
            for u in range(4):
                take_lo(n0 + u + RING, u)
                for j in range(2):
                    add_up(hp0 + 2 * u + j, j, PP[:, 4 * u + 2 * j:4 * u + 2 * j + 2, :])
            dve.wait_ge(meta_sum, 1)
            mv, my, mt = var[:, T:T + META], root[:, T:T + META], var[:, T + META:T + 2 * META]
            nc.vector.tensor_scalar(mv, xp[:, 1, 0:META], 1.0 / D, RMS_EPS, ALU.mult, ALU.add).then_inc(meta_step, 1)
            variance(1, 1, RMS_EPS)
            dve.wait_ge(meta_act, 2)
            nc.vector.tensor_tensor(mt, my, my, ALU.mult).then_inc(meta_step, 1)
            dve.wait_ge(meta_step, 3)
            nc.vector.tensor_tensor(mt, mt, mv, ALU.mult).then_inc(meta_step, 1)
            dve.wait_ge(meta_step, 4)
            nc.vector.tensor_scalar(mt, mt, -0.5, 1.5, ALU.mult, ALU.add).then_inc(meta_step, 1)
            dve.wait_ge(meta_step, 5)
            nc.vector.tensor_tensor(my, my, mt, ALU.mult).then_inc(meta_step, 1)
            dve.wait_ge(meta_step, 6)
            for k in range(KT):
                nc.vector.scalar_tensor_tensor(metaT[:, k, :], metaT[:, k, :], col("mix_pre", k), my, ALU.mult,
                                               ALU.mult).then_inc(meta_step, 1)

            def ffn1(rnd, last):
                hp0, n0 = at["up0"]
                with dve.Fori(0, 4) as it:
                    for j in range(2):
                        convert(n0 + 64 * rnd + 8 * it + 4 * j)
                        t = s[:, j, :, 0:T]
                        add_up(hp0 + 16 * rnd + 2 * it + j, j, t)
                        c = 8 * rnd + 2 * it + j
                        nc.vector.tensor_tensor(t, t, by_rstd(), ALU.mult).then_inc(up_step, 1)
                        dve.wait_ge(up_step, 2 * c + 1)
                        nc.vector.scalar_tensor_tensor(t, t, 0.0, t, ALU.max, ALU.mult).then_inc(up_step, 1)
                        dve.wait_ge(up_hi, c + 1)
                        o = ds(4 * it + 2 * j, 2)
                        nc.vector.tensor_tensor(A[:, o, T:2 * T], t, A[:, o, 0:T].bitcast(F32),
                                                ALU.subtract).then_inc(hidden_ready, 1)
                hp0, n0 = at["down0"]
                with dve.Fori(0, 4) as it:
                    for j in range(2):
                        convert(n0 + 64 * rnd + 8 * it + 4 * j)
                        update_r(hp0 + 16 * rnd + 2 * it + j, 2 * it + j, j, 8, B if last else None, "g_ple")

            with dve.Fori(0, 3) as rnd:
                ffn1(rnd, False)
            ffn1(3, True)

            def gate_tail(hp, it, j):
                h, t, rr = 2 * it + j, s[:, j, :, 0:T], r[:, ds(4 * it + 2 * j, 2), :]
                add_up(hp, j, t)
                nc.vector.tensor_tensor(t, t, by_rstd(), ALU.mult).then_inc(gate_normed, 1)
                dve.wait_ge(gate_sig, h + 1)
                nc.vector.tensor_tensor(t, t, PP[:, ds(4 * it + 2 * j, 2), :], ALU.mult).then_inc(gate_mul, 1)
                dve.wait_ge(gate_mul, h + 1)
                nc.vector.tensor_tensor(rr, rr, t, ALU.add).then_inc(r_updated, 1)
                lo_of_r(16, A, "mix_pre", h)

            body("gate", 0, gate_tail, {3: [lambda: variance(2, 2, RMS_EPS)]})
            with dve.Fori(1, 4) as it:
                body("gate", it, gate_tail)
            dve.wait_ge(meta_step, 6 + KT)
            dve.wait_ge(meta_hi, 1)
            nc.vector.tensor_tensor(metaA[:, :, META:2 * META], metaT, metaA[:, :, 0:META].bitcast(F32),
                                    ALU.subtract).then_inc(meta_ready, 1)
            variance(3, 3, RMS_EPS)
            dve.wait_ge(c2_pad, 1)

            def conv2(it):
                hp0, n0 = at["conv2"]
                for j in range(2):
                    hp = hp0 + 2 * it + j
                    convert(n0 + 8 * it + 4 * j)
                    dve.wait_ge(cm_out, 2 * it + j + 1)
                    nc.vector.tensor_tensor(s[:, j, :, 0:META], xp[:, 2 * j:2 * j + 2, 0:META], cross_meta[:], ALU.add)
                    add_up(hp, j, s[:, j, :, META:META + T])
                    nc.vector.tensor_tensor(s[:, j, :, META:META + T], s[:, j, :, META:META + T], by_rstd(),
                                            ALU.mult).then_inc(c2_normed, 1)
                for m in range(2):
                    dve.wait_ge(c2_sig, 2 * it + m + 1)
                    nc.vector.scalar_tensor_tensor(cin2[:, ds(2 * it + m, 1), PAD2:LEN2], s[:, 0, m:m + 1, :],
                                                   col("b_in", 2 * it + m), s[:, 1, m:m + 1, :], ALU.add,
                                                   ALU.mult).then_inc(c2_ready, 1)
                dve.wait_ge(c2_ready, 2 * it + 2)
                for tap in range(TAPS2):
                    for m in range(2):
                        o, i = V[:, ds(2 * it + m, 1), :], cin2[:, ds(2 * it + m, 1), tap:tap + T]
                        w = taps2[:, ds(2 * it + m, 1), tap]
                        if tap == 0:
                            nc.vector.tensor_scalar(o, i, w, col("b_dw", 2 * it + m), ALU.mult, ALU.add).then_inc(tap_done, 1)
                        else:
                            dve.wait_ge(tap_done, 2 * TAPS2 * it + 2 * (tap - 1) + m + 1)
                            nc.vector.scalar_tensor_tensor(o, i, w, o, ALU.mult, ALU.add).then_inc(tap_done, 1)

            with dve.Fori(0, 8) as it:
                conv2(it)
            dve.wait_ge(stat_ready, 5)
            nc.vector.tensor_scalar(var[:, T:2 * T], xp[:, 0, 0:T], 1.0 / D, None, ALU.mult).then_inc(mean_ready, 1)
            dve.wait_ge(mean_ready, 1)
            mean = var[:, T:2 * T].unsqueeze(1).broadcast_to([P, 2, T])
            for c in range(8):
                v = V[:, 2 * c:2 * c + 2, :]
                nc.vector.tensor_tensor(v, v, mean, ALU.subtract).then_inc(centred, 1)
            variance(4, 5, LN_EPS)
            for c in range(8):
                v = V[:, 2 * c:2 * c + 2, :]
                dve.wait_ge(centred, c + 1)
                nc.vector.tensor_tensor(v, v, by_rstd(), ALU.mult).then_inc(ln_normed, 1)
            for c in range(8):
                dve.wait_ge(ln_hi, c + 1)
                nc.vector.tensor_tensor(B[:, 2 * c:2 * c + 2, T:2 * T], V[:, 2 * c:2 * c + 2, :],
                                        B[:, 2 * c:2 * c + 2, 0:T].bitcast(F32), ALU.subtract).then_inc(ln_ready, 1)

            hp0, n0 = at["out2"]
            with dve.Fori(0, 4) as it:
                for j in range(2):
                    convert(n0 + 8 * it + 4 * j)
                    add_up(hp0 + 2 * it + j, j, U[:, ds(4 * it + 2 * j, 2), :])
            variance(5, 6, RMS_EPS)

            def post_norm(src, gain, h, c, ready):
                t = src[:, 2 * h:2 * h + 2, :]
                nc.vector.tensor_tensor(t, t, by_rstd(), ALU.mult).then_inc(post_normed, 1)
                dve.wait_ge(post_normed, c + h + 1)
                for m in range(2):
                    kt = 2 * h + m
                    last = nc.vector.scalar_tensor_tensor(r[:, kt, :], src[:, kt, :], col(gain, kt), r[:, kt, :], ALU.mult, ALU.add)
                    if m == 1 or ready is out_ready:
                        last.then_inc(ready, 1)

            for h in range(8):
                post_norm(U, "mix_post", h, 0, r_updated)
            for h in range(8):
                lo_of_r(24, A, "ffn_pre", h)

            def glu(rnd, it, units=None, hp_done=0):
                def tail(hp, it, j):
                    c = hp_done + it
                    if j == 0 and not (isinstance(it, int) and c == 0):
                        dve.wait_ge(glu_ready, c)
                    add_up(hp, j, s[:, j, :, 0:T])
                    if j == 0:
                        return
                    four = s[:].rearrange("p j m t -> p (j m) t")[:, :, 0:T]
                    nc.vector.tensor_tensor(four, four, by_rstd(4), ALU.mult).then_inc(glu_normed, 1)
                    dve.wait_ge(glu_normed, c + 1)
                    a, b = s[:, 0, :, 0:T], s[:, 1, :, 0:T]
                    nc.vector.tensor_tensor(b, b, a, ALU.mult).then_inc(glu_mul, 1)
                    dve.wait_ge(glu_mul, 2 * c + 1)
                    dve.wait_ge(glu_sig, c + 1)
                    nc.vector.tensor_tensor(a, b, root[:].rearrange("p (m t) -> p m t", m=2), ALU.mult).then_inc(glu_mul, 1)
                    dve.wait_ge(glu_hi, c + 1)
                    nc.vector.tensor_tensor(B[:, ds(2 * it, 2), T:2 * T], a, B[:, ds(2 * it, 2), 0:T].bitcast(F32),
                                            ALU.subtract).then_inc(glu_ready, 1)
                body(f"glu{rnd}", it, tail, units)

            def back_tail(first):
                def tail(hp, it, j):
                    f = F[:, ds(4 * it + 2 * j, 2), :]
                    if first:
                        add_up(hp, j, f)
                    else:
                        t = s[:, j, :, 0:T]
                        add_up(hp, j, t)
                        nc.vector.tensor_tensor(f, f, t, ALU.add).then_inc(r_updated, 1)
                return tail

            glu(0, 0, {3: [lambda: variance(6, 7, RMS_EPS)]})
            with dve.Fori(1, 8) as it:
                glu(0, it)
            with dve.Fori(0, 4) as it:
                body("back0", it, back_tail(True))
            with dve.Fori(0, 8) as it:
                glu(1, it, None, 8)
            with dve.Fori(0, 4) as it:
                body("back1", it, back_tail(False))
            with dve.Fori(0, 6) as it:
                glu(2, it, None, 16)
            hp0, n0 = at["back2"]
            for h in range(8):
                convert(n0 + 3 * h, 3, 3 * h)
                back_tail(False)(hp0 + h, h // 2, h % 2)
            variance(7, 8, RMS_EPS)
            for h in range(8):
                post_norm(F, "ffn_post", h, 8, out_ready)
            for c in range(4):
                dve.wait_ge(out_turned, c + 1)
                bank = (gp if c < 2 else xp)[:, 2 * (c % 2) + 1, :]
                nc.vector.tensor_copy(ot[:, 1, 512 * c:512 * c + 512], bank).then_inc(out_copied[1], 1)

        @block.gpsimd
        def _(pool):
            nc.gpsimd.memset(ident[:], 0.0).then_inc(consts0, 1)
            nc.gpsimd.memset(mask[:], 0.0).then_inc(consts0, 1)
            nc.gpsimd.memset(three[:], 3.0)
            nc.gpsimd.memset(ones[:], 1.0).then_inc(consts, 1)
            pool.wait_ge(consts0, 1)
            nc.gpsimd.affine_select(out=ident[:], in_=ident[:], compare_op=ALU.not_equal, fill=1.0, base=0,
                                    pattern=[[-1, P]], channel_multiplier=1).then_inc(consts, 1)
            pool.wait_ge(consts0, 2)
            for c in (0, 2):
                last = nc.gpsimd.affine_select(out=mask[:, c * P:c * P + P], in_=mask[:, c * P:c * P + P],
                                               compare_op=ALU.is_ge, fill=NEG, base=0, pattern=[[-1, P]],
                                               channel_multiplier=1)
            last.then_inc(consts, 1)

            def clear(k):
                if k:
                    pool.wait_ge(stat_ready, k)
                nc.gpsimd.memset(acc[:], 0.0).then_inc(acc_ready, 1)

            def two(x):
                return x[:].rearrange("p (m t) -> p m t", m=2)

            def add_squares(k, h, src, nsq):
                nc.gpsimd.tensor_tensor(two(sq), src, src, ALU.mult).then_inc(squared, 1)
                pool.wait_ge(squared, nsq + h + 1)
                pool.wait_ge(acc_ready, 9 * k + h + 1)
                nc.gpsimd.tensor_tensor(acc[:], acc[:], sq[:], ALU.add).then_inc(acc_ready, 1)
                pool.wait_ge(acc_ready, 9 * k + h + 2)

            def refine(k):
                pool.wait_ge(root_ready, k + 1)
                t, y, v = sq[:, 0:T], root[:, 0:T], var[:, 0:T]
                nc.gpsimd.tensor_tensor(t, y, y, ALU.mult).then_inc(newton, 1)
                pool.wait_ge(newton, 3 * k + 1)
                nc.gpsimd.tensor_tensor(t, t, v, ALU.mult).then_inc(newton, 1)
                pool.wait_ge(newton, 3 * k + 2)
                nc.gpsimd.tensor_tensor(t, three[:].broadcast_to([P, T]), t, ALU.subtract).then_inc(newton, 1)
                pool.wait_ge(newton, 3 * k + 3)
                nc.gpsimd.tensor_tensor(rstd[:], y, t, ALU.mult).then_inc(rstd_ready, 1)
                pool.wait_ge(rstd_ready, k + 1)

            clear(0)
            for h in range(8):
                pool.wait_ge(evacuated, h // 2 + 1)
                add_squares(0, h, r[:, 2 * h:2 * h + 2, :], 0)
            nc.gpsimd.memset(cin[:, :, 0:2], 0.0).then_inc(consts, 1)
            refine(0)

            def attention(h):
                pool.wait_ge(qkv_ready, 12)
                nc.gpsimd.tensor_tensor(two(sq), qkv[:, 0:2, ds(h, 1), :].rearrange("p a h t -> p (a h) t"),
                                        qkv[:, 0:2, ds(h, 1), :].rearrange("p a h t -> p (a h) t"), ALU.mult).then_inc(qk_sq, 1)
                pool.wait_ge(qk_root, h + 1)
                nc.gpsimd.tensor_tensor(sq[:], root[:], root[:], ALU.mult).then_inc(qk_newton, 1)
                pool.wait_ge(qk_newton, 3 * h + 1)
                nc.gpsimd.tensor_tensor(sq[:], sq[:], var[:], ALU.mult).then_inc(qk_newton, 1)
                pool.wait_ge(qk_newton, 3 * h + 2)
                nc.gpsimd.tensor_tensor(sq[:], three[:].broadcast_to([P, 2 * T]), sq[:], ALU.subtract).then_inc(qk_newton, 1)
                pool.wait_ge(qk_newton, 3 * h + 3)
                nc.gpsimd.tensor_tensor(root[:], root[:], sq[:], ALU.mult).then_inc(qk_rstd, 1)
                pool.wait_ge(qk_rstd, h + 1)
                if not isinstance(h, int) or h >= 1:
                    pool.wait_ge(turned, h)
                nc.gpsimd.tensor_copy(vh[:].unsqueeze(1), qkv[:, 2, ds(h, 1), :]).then_inc(vh_ready, 1)

            attention(0)
            with pool.Fori(1, HEADS) as h:
                attention(h)

            def squares_of_r(k, c0, nsq):
                clear(k)
                with pool.Fori(0, 8) as h:
                    pool.wait_ge(r_updated, c0 + h + 1)
                    add_squares(k, h, r[:, ds(2 * h, 2), :], nsq)

            squares_of_r(1, 0, 8)
            refine(1)
            squares_of_r(2, 32, 16)
            refine(2)
            squares_of_r(3, 40, 24)
            refine(3)
            pool.wait_ge(gate_mul, 8)
            nc.gpsimd.memset(cin2[:, :, 0:PAD2], 0.0).then_inc(c2_pad, 1)
            clear(4)
            with pool.Fori(0, 8) as h:
                pool.wait_ge(tap_done, 2 * TAPS2 * h + 2 * TAPS2)
                pool.wait_ge(acc_ready, 36 + h + 1)
                nc.gpsimd.tensor_tensor(two(acc), two(acc), V[:, ds(2 * h, 2), :], ALU.add).then_inc(acc_ready, 1)
            clear(5)
            with pool.Fori(0, 8) as h:
                pool.wait_ge(centred, h + 1)
                add_squares(5, h, V[:, ds(2 * h, 2), :], 32)
            refine(4)
            clear(6)
            with pool.Fori(0, 8) as h:
                pool.wait_ge(evacuated, XSLOTS + at["out2"][0] + h + 1)
                add_squares(6, h, U[:, ds(2 * h, 2), :], 40)
            refine(5)
            squares_of_r(7, 48, 48)
            refine(6)
            clear(8)
            with pool.Fori(0, 8) as h:
                pool.wait_ge(r_updated, 64 + h + 1)
                add_squares(8, h, F[:, ds(2 * h, 2), :], 56)
            refine(7)


_INS = ["x", "p", "g_mix", "w_in", "g_q", "g_k", "w_conv", "w_attn_out", "w_conv_out", "w_o", "g_mlp", "w_up", "w_down",
        "g_ple", "w_ple_gate", "w_ple_proj", "meta_tokens_2", "conv_w_in_2", "conv_b_in_2", "conv_w_dw_2", "conv_b_dw_2",
        "conv_ln_g_2", "conv_ln_b_2", "conv_w_out_2", "conv_b_out_2", "norm_mix_pre_2", "norm_mix_post_2",
        "norm_ffn_pre_2", "norm_ffn_post_2", "ffn_w_gate_2", "ffn_w_up_2", "ffn_w_down_2"]


def kernel(**inputs):
    import numpy as _np
    import concourse.bacc as _bacc
    from concourse import mybir as _mybir
    from concourse.bass_utils import run_bass_kernel_spmd as _run

    nc = _bacc.Bacc("TRN2", target_bir_lowering=False, num_devices=1)
    arrays, io = {}, {}
    for name in _INS:
        a = _np.ascontiguousarray(inputs[name])
        arrays[f"in_{name}"] = a
        io[name] = nc.dram_tensor(f"in_{name}", a.shape, _mybir.dt.from_np(a.dtype), kind="ExternalInput").ap()
    out = nc.dram_tensor("out_0", (1, T, D), F32, kind="ExternalOutput").ap()
    two_block_kernel(nc, io, out)
    r = _run(nc, [arrays], core_ids=[0])
    return r.results[0]["out_0"]
```

```python
from contextlib import ExitStack

import concourse.bass as bass
from concourse import mybir

F32 = mybir.dt.float32
F32R = mybir.dt.float32r
ALU = mybir.AluOpType
ACT = mybir.ActivationFunctionType
AX_X = mybir.AxisListType.X
ds = bass.ds

P = 128
D = 2048
T = 256
KT = D // P
HEADS, HD = 8, 128
CONV = 1024
CT = CONV // P
FF1 = 4 * D
PLE = 256
META = 16
TM = T + META
TAPS2 = 31
FF2 = 5632
RMS_EPS, LN_EPS = 1e-6, 1e-5
SCALE = HD ** -0.5
NEG = -1e30
RING = 4
UNIT = 1024
HPW = 256
PAD2 = TAPS2 - 1 - META
LEN2 = PAD2 + META + T
OUT_POOL = 5
XSLOTS = 4


def plan():
    sizes = [("qkv", 12, 4), ("ga", 8, 4), ("ccx", 8, 4), ("cb", 4, 4), ("gc", 8, 4), ("attn_out", 8, 2),
             ("conv_out", 8, 2), ("w_o", 8, 4), ("ple", 8, 0.5)]
    for r in range(4):
        sizes += [(f"up{r}", 8, 4), (f"down{r}", 8, 4)]
    sizes += [("gate", 8, 4), ("conv2", 16, 4), ("out2", 8, 4)]
    for r, pairs in enumerate((8, 8, 6)):
        sizes += [(f"glu{r}", 2 * pairs, 4), (f"back{r}", 8, pairs // 2)]
    at, hp, unit = {}, 0, 0
    for name, n, per in sizes:
        at[name] = (hp, unit)
        hp += n
        unit += int(n * per)
    return at, hp, unit


def two_block_kernel(nc, io, out):
    at, _, UNITS = plan()

    with ExitStack() as ctx:
        def sb(name, shape, dt=F32, where=ctx):
            return where.enter_context(nc.sbuf_tensor(name, shape, dt))

        def sem(name):
            return ctx.enter_context(nc.semaphore(name))

        r = sb("r", [P, KT, T])
        A = sb("A", [P, KT, 2 * TM], F32R)
        B = sb("B", [P, KT, 2 * T], F32R)
        stage = sb("stage", [P, RING, UNIT])
        whi = sb("whi", [P, RING, UNIT], F32R)
        wlo = sb("wlo", [P, RING, UNIT], F32R)
        work = sb("work", [P, 12804])
        cross = sb("cross", [P, 2, T])
        s = sb("s", [P, 2, 2, TM])
        sq = sb("sq", [P, 2 * T])
        acc = sb("acc", [P, 2 * T])
        var = sb("var", [P, 2 * T])
        root = sb("root", [P, 2 * T])
        rstd = sb("rstd", [P, TM])
        ident = sb("ident", [P, P])
        ones = sb("ones", [P, P])
        three = sb("three", [P, 1])
        gv = sb("gv", [P, 2, P])
        taps2 = sb("taps2", [P, KT, TAPS2])
        small = sb("small", [P, 4, 2])
        with ExitStack() as early:
            mask = sb("mask", [P, 3 * P], F32, early)
            S = sb("S", [P, 3 * P], F32, early)
            PT = sb("PT", [P, 3 * P], F32, early)
            vt = sb("vt", [P, 2 * P], F32, early)
            qk = sb("qk", [P, 2, T], F32, early)
            vh = sb("vh", [P, T], F32, early)
        pT = sb("pT", [P, 2, 2 * T], F32R)

        gp = ctx.enter_context(nc.psum_tensor("gp", [P, 4, 512], F32))
        xp = ctx.enter_context(nc.psum_tensor("xp", [P, 4, 512], F32))

        def part(M, which, i, n):
            a = which * (TM if M is A else T)
            return M[:, i:i + n, a:a + T] if isinstance(i, int) else M[:, ds(i, n), a:a + T]

        def both_parts(M, kt):
            return M[:, kt, :].rearrange("p (a t) -> p a t", a=2)[:, :, 0:T]

        def area(a, n, w):
            return work[:, a:a + n * w].rearrange("p (n w) -> p n w", n=n)

        qkv = work[:, 0:24 * T].rearrange("p (a h t) -> p a h t", a=3, h=HEADS)
        qkv_flat = area(0, 24, T)
        GA = area(24 * T, KT, T)
        cr = area(40 * T, CT, T)
        cin = area(48 * T, 2, T + 2)
        GC = area(0, KT, T)
        PP = area(24 * T, KT, T)
        xt = work[:, 24 * T:40 * T].rearrange("p (a d) -> p a d", a=2)
        V1, V2 = work[:, 0:P], work[:, P:2 * P]
        taps_raw = work[0:TAPS2, 4096:4096 + D]
        meta_raw = work[0:META, 16 * T:16 * T + D]
        p_raw = work[:, 40 * T:42 * T].rearrange("p (a d) -> p a d", a=2)
        metaT = work[:, 42 * T:43 * T].rearrange("p (k t) -> p k t", t=META)
        meta_sq = work[:, 43 * T:44 * T].rearrange("p (k t) -> p k t", t=META)
        cin2 = area(0, KT, LEN2)
        V = area(KT * LEN2, KT, T)
        U = area(KT * LEN2 + KT * T, KT, T)
        F = area(0, KT, T)
        ot = work[:, KT * T:3 * KT * T].rearrange("p (a d) -> p a d", a=2)

        vec = {}
        for row, name in enumerate(["g_mix", "g_mlp", "g_ple"]):
            vec[name] = (0, 16 * row)
        vec["b_in"], vec["b_dw"], vec["ln_g"], vec["ln_b"] = (0, 48), (0, 80), (0, 96), (0, 112)
        for row, name in enumerate(["b_out", "mix_pre", "mix_post", "ffn_pre", "ffn_post"]):
            vec[name] = (1, 16 * row)
        vec["g_q"], vec["g_k"], vec["w_conv"] = (1, 80), (1, 81), (1, 82)

        def col(name, i):
            half, c = vec[name]
            return gv[:, half, ds(c + i, 1)]

        loaded = [sem(f"loaded{i}") for i in range(RING)]
        hi_ready, lo_ready, unit_used = sem("hi_ready"), sem("lo_ready"), sem("unit_used")
        cross_out, evacuated = sem("cross_out"), sem("evacuated")
        x_loaded = [sem(f"x_loaded{i}") for i in range(4)]
        v_loaded, late_loaded = sem("v_loaded"), sem("late_loaded")
        consts, consts0 = sem("consts"), sem("consts0")
        x_turned, x_hi, h1_ready = sem("x_turned"), sem("x_hi"), sem("h1_ready")
        vec_turned, vec_ready = sem("vec_turned"), sem("vec_ready")
        acc_ready, squared = sem("acc_ready"), sem("squared")
        stat_ready, var_ready, ln_done, root_ready = sem("stat_ready"), sem("var_ready"), sem("ln_done"), sem("root_ready")
        newton, rstd_ready = sem("newton"), sem("rstd_ready")
        r_updated, r_hi, r_ready = sem("r_updated"), sem("r_hi"), sem("r_ready")
        qk_sq, qk_sum, qk_var, qk_ln, qk_root = sem("qk_sq"), sem("qk_sum"), sem("qk_var"), sem("qk_ln"), sem("qk_root")
        qk_newton, qk_rstd, qk_hat, vh_ready = sem("qk_newton"), sem("qk_rstd"), sem("qk_hat"), sem("vh_ready")
        scored, masked, maxed, neg_max, expd = sem("scored"), sem("masked"), sem("maxed"), sem("neg_max"), sem("expd")
        inv_sum, probs, turned, pt_copied = sem("inv_sum"), sem("probs"), sem("turned"), sem("pt_copied")
        pv_done, attn_hi, attn_ready = sem("pv_done"), sem("attn_hi"), sem("attn_ready")
        qkv_ready, ga_ready, gc_ready = sem("qkv_ready"), sem("ga_ready"), sem("gc_ready")
        cc_normed, cin_ready, cr_step = sem("cc_normed"), sem("cin_ready"), sem("cr_step")
        cb_normed, cb_mul, cb_hi, conv1_ready = sem("cb_normed"), sem("cb_mul"), sem("cb_hi"), sem("conv1_ready")
        ga_sig, ga_y, gc_sig, gc_y = sem("ga_sig"), sem("ga_y"), sem("gc_sig"), sem("gc_y")
        merged, merged_hi, merged_ready = sem("merged"), sem("merged_hi"), sem("merged_ready")
        late_turned, late_hi, p_ready, ple_half = sem("late_turned"), sem("late_hi"), sem("p_ready"), sem("ple_half")
        meta_step, meta_sum, meta_var, meta_act = sem("meta_step"), sem("meta_sum"), sem("meta_var"), sem("meta_act")
        meta_hi, meta_ready = sem("meta_hi"), sem("meta_ready")
        up_step, up_hi, hidden_ready = sem("up_step"), sem("up_hi"), sem("hidden_ready")
        gate_normed, gate_sig, gate_mul = sem("gate_normed"), sem("gate_sig"), sem("gate_mul")
        c2_normed, c2_sig, c2_ready, c2_pad = sem("c2_normed"), sem("c2_sig"), sem("c2_ready"), sem("c2_pad")
        tap_done, v_ready = sem("tap_done"), sem("v_ready")
        ln_sq, ln_summed = sem("ln_sq"), sem("ln_summed")
        mean_ready, centred, ln_normed, ln_silu, ln_hi, ln_ready = (sem("mean_ready"), sem("centred"), sem("ln_normed"),
                                                                    sem("ln_silu"), sem("ln_hi"), sem("ln_ready"))
        post_normed, post_sq, out_last = sem("post_normed"), sem("post_sq"), sem("out_last")
        glu_normed, glu_sig, glu_mul, glu_hi, glu_ready = (sem("glu_normed"), sem("glu_sig"), sem("glu_mul"),
                                                           sem("glu_hi"), sem("glu_ready"))
        out_ready, out_turned, stored = sem("out_ready"), sem("out_turned"), sem("stored")
        out_copied = [sem("out_copied0"), sem("out_copied1")]

        def tiles(w):
            return w.rearrange("o (k p) n -> p (o k) n", p=P)

        W = {n: tiles(io[n]) for n in ("w_in", "w_attn_out", "w_conv_out", "w_o", "w_up", "w_down", "w_ple_gate",
                                       "w_ple_proj", "conv_w_in_2", "conv_w_out_2", "ffn_w_gate_2", "ffn_w_up_2",
                                       "ffn_w_down_2")}

        block = ctx.enter_context(nc.Block())

        @block.sync
        def _(sp):
            def load(n, slot, src, first=False):
                if not first:
                    sp.wait_ge(lo_ready, n - RING + 1)
                dst = stage[:, slot, :].rearrange("p (k n) -> p k n", k=src.shape[1])
                sp.dma_start(dst, src).then_inc(loaded[slot], 16)

            def panel(n0, slot0, w, row0, rows, c):
                for u in range(rows // 4):
                    load(n0 + u, (slot0 + u) % RING, w[:, row0 + 4 * u:row0 + 4 * u + 4, ds(c, HPW)])

            def panels(phase, w, its, col0, first_it=0, row0=0):
                n0 = at[phase][1]
                with sp.Fori(first_it, its) as it:
                    for j in range(2):
                        panel(n0 + 8 * it + 4 * j, 0, w, row0, KT, col0 + (2 * it + j) * HPW)

            def pairs(phase, wa, ca, wb, cb, its):
                n0 = at[phase][1]
                with sp.Fori(0, its) as it:
                    panel(n0 + 8 * it, 0, wa, 0, KT, ca + it * HPW)
                    panel(n0 + 8 * it + 4, 0, wb, 0, KT, cb + it * HPW)

            def half_panels(phase, w):
                n0 = at[phase][1]
                with sp.Fori(0, 2) as it:
                    for j in range(4):
                        panel(n0 + 8 * it + 2 * j, 2 * (j % 2), w, 0, 8, (4 * it + j) * HPW)

            win = W["w_in"]
            xv = io["x"].rearrange("b (a p) d -> p (b a) d", p=P)
            for c in range(4):
                sp.dma_start(xt[:, :, 512 * c:512 * c + 512], xv[:, :, 512 * c:512 * c + 512]).then_inc(x_loaded[c], 16)
                load(c, c, win[:, 4 * c:4 * c + 4, 0:HPW], first=True)
            panel(4, 0, win, 0, KT, HPW)
            panels("qkv", win, 6, 0, first_it=1)
            panels("ga", win, 4, 6144)
            pairs("ccx", win, 4096, win, 5120, 4)
            panels("cb", win, 2, 3072)
            panels("gc", win, 4, 8192)
            half_panels("attn_out", W["w_attn_out"])
            half_panels("conv_out", W["w_conv_out"])
            sp.wait_ge(cb_mul, 4)
            sp.dma_start(p_raw, io["p"].rearrange("a b (k p) d -> p (a b k) d", p=P)).then_inc(late_loaded, 16)
            sp.wait_ge(vh_ready, HEADS)
            sp.dma_start(meta_raw, io["meta_tokens_2"]).then_inc(late_loaded, 16)
            panels("w_o", W["w_o"], 4, 0)
            with sp.Fori(0, 1) as _it:
                for u in range(4):
                    load(at["ple"][1] + u, u, W["w_ple_proj"][:, 0:2, 512 * u:512 * u + 512])
            with sp.Fori(0, 4) as rnd:
                with sp.Fori(0, 4) as it:
                    for j in range(2):
                        panel(at["up0"][1] + 64 * rnd + 8 * it + 4 * j, 0, W["w_up"], 0, KT,
                              rnd * D + it * (2 * HPW) + j * HPW)
                with sp.Fori(0, 4) as it:
                    for j in range(2):
                        for u in range(4):
                            load(at["down0"][1] + 64 * rnd + 8 * it + 4 * j + u, u,
                                 W["w_down"][:, ds(rnd * KT + 4 * u, 4), ds(it * (2 * HPW) + j * HPW, HPW)])
            panels("gate", W["w_ple_gate"], 4, 0)
            pairs("conv2", W["conv_w_in_2"], 0, W["conv_w_in_2"], D, 8)
            panels("out2", W["conv_w_out_2"], 4, 0)
            for rnd, n in enumerate((8, 8, 6)):
                pairs(f"glu{rnd}", W["ffn_w_gate_2"], rnd * D, W["ffn_w_up_2"], rnd * D, n)
                if n == 8:
                    panels(f"back{rnd}", W["ffn_w_down_2"], 4, 0, row0=rnd * KT)
                else:
                    n0 = at["back2"][1]
                    with sp.Fori(0, 2) as it:
                        for j in range(4):
                            panel(n0 + 12 * it + 3 * j, 3 * j, W["ffn_w_down_2"], 2 * KT, 12, (4 * it + j) * HPW)

        @block.tensor
        def _(pe):
            def step(hp, j, n0, M, kt0=0, units=4, slot0=0, ready=None, after=None, meta=False):
                for u in range(units):
                    slot = (slot0 + u) % RING
                    pe.wait_ge(lo_ready, n0 + u + 1)
                    if u == 0:
                        pe.wait_ge(evacuated, XSLOTS + hp - 1)
                    if ready:
                        pe.wait_ge(ready[0], ready[1] + ready[2] * (u + 1))
                    for k in range(4):
                        kt = kt0 + 4 * u + k
                        first, last = u == 0 and k == 0, u == units - 1 and k == 3
                        for m in range(2):
                            c = k * HPW + m * P
                            hi, lo = whi[:, slot, c:c + P], wlo[:, slot, c:c + P]
                            bank = gp[:, 2 * j + m, :]
                            if meta:
                                o = bank[:, 0:TM]
                                nc.tensor.matmul(o, hi, M[:, kt, 0:TM], start=first, stop=False)
                                nc.tensor.matmul(o, hi, M[:, kt, TM:2 * TM], start=False, stop=False)
                                done = nc.tensor.matmul(o, lo, M[:, kt, 0:TM], start=False, stop=last)
                            else:
                                nc.tensor.matmul(bank.rearrange("p (a t) -> p a t", a=2), hi, both_parts(M, kt),
                                                 start=first, stop=False)
                                done = nc.tensor.matmul(bank[:, T:2 * T], lo, M[:, kt, 0:T], start=False, stop=last)
                    done.then_inc(unit_used, 1)
                    if after and u in after:
                        for f in after[u]:
                            f()

            def body(phase, it, M, ready, hooks=None, kt0=0, meta=False):
                hp0, n0 = at[phase]
                for j in range(2):
                    after = {u - 4 * j: f for u, f in (hooks or {}).items() if u // 4 == j}
                    step(hp0 + 2 * it + j, j, n0 + 8 * it + 4 * j, M, kt0, ready=ready, after=after, meta=meta)

            def column_sums(k):
                pe.wait_ge(acc_ready, 9 * (k + 1))
                nc.tensor.matmul(xp[:, 0, 0:T], ones[:], acc[:, 0:T], start=True, stop=False)
                nc.tensor.matmul(xp[:, 0, 0:T], ones[:], acc[:, T:2 * T], start=False, stop=True).then_inc(stat_ready, 1)

            pe.wait_ge(consts, 3)
            for c in range(4):
                j = c % 2
                pe.wait_ge(x_loaded[c], 16)
                if c >= 2:
                    pe.wait_ge(evacuated, c - 1)
                for kk in range(4):
                    for t in range(2):
                        kt = 4 * c + kk
                        o = (kk % 2) * T + t * P
                        done = nc.tensor.transpose(gp[:, 2 * j + kk // 2, o:o + P], xt[:, t, kt * P:kt * P + P], ident[:])
                done.then_inc(x_turned, 1)
                if c == 0:
                    pe.wait_ge(v_loaded, 16 * 18)
                    nc.tensor.transpose(xp[:, 0, 0:P], V1, ident[:])
                    nc.tensor.transpose(xp[:, 0, P:P + 106], V2[0:106, :], ident[0:106, 0:106]).then_inc(vec_turned, 1)
            for k in range(KT):
                done = nc.tensor.transpose(xp[:, 1, k * TAPS2:(k + 1) * TAPS2], taps_raw[:, k * P:k * P + P],
                                           ident[0:TAPS2, 0:TAPS2])
            done.then_inc(vec_turned, 1)

            def past(h):
                return not isinstance(h, int) or h >= 1

            def norms(h):
                def f():
                    pe.wait_ge(qk_sq, h + 1)
                    if past(h):
                        pe.wait_ge(qk_var, h)
                    nc.tensor.matmul(xp[:, 0, :], ones[:], sq[:], start=True, stop=True).then_inc(qk_sum, 1)
                return {4: [f]}

            def scores(h):
                def f():
                    pe.wait_ge(qk_hat, 2 * h + 2)
                    if past(h):
                        pe.wait_ge(masked, h)
                    nc.tensor.matmul(xp[:, 1, 0:P], qk[:, 0, 0:P], qk[:, 1, 0:P], start=True, stop=True)
                    nc.tensor.matmul(xp[:, 1, P:3 * P], qk[:, 0, P:T], qk[:, 1, :], start=True, stop=True).then_inc(scored, 1)

                def turn():
                    pe.wait_ge(probs, 2 * h + 2)
                    pe.wait_ge(vh_ready, h + 1)
                    if past(h):
                        pe.wait_ge(attn_ready, h)
                    for c in range(3):
                        nc.tensor.transpose(xp[:, 2, c * P:c * P + P], S[:, c * P:c * P + P], ident[:])
                    nc.tensor.transpose(xp[:, 3, 0:P], vh[:, 0:P], ident[:])
                    nc.tensor.transpose(xp[:, 3, P:2 * P], vh[:, P:2 * P], ident[:]).then_inc(turned, 1)
                return {2: [f], 6: [turn]}

            def output(h):
                def f():
                    pe.wait_ge(pt_copied, 2 * h + 2)
                    nc.tensor.matmul(xp[:, 3, T:2 * T], vt[:, 0:P], PT[:, 0:2 * P], start=True, stop=False)
                    nc.tensor.matmul(xp[:, 3, T + P:2 * T], vt[:, P:2 * P], PT[:, 2 * P:3 * P], start=False,
                                     stop=True).then_inc(pv_done, 1)
                return {0: [f]}

            h1 = (h1_ready, 0, 4)
            body("qkv", 0, A, h1, {4: [lambda: column_sums(0)]})
            with pe.Fori(1, 5) as it:
                body("qkv", it, A, h1)
            body("qkv", 5, A, h1, norms(0))
            body("ga", 0, A, h1, {**scores(0), **norms(1)})
            with pe.Fori(1, 4) as it:
                body("ga", it, A, h1, {**output(it - 1), **scores(it), **norms(it + 1)})
            with pe.Fori(0, 3) as it:
                body("ccx", it, A, h1, {**output(it + 3), **scores(it + 4), **norms(it + 5)})
            body("ccx", 3, A, h1, {**output(6), **scores(7)})
            body("cb", 0, A, h1, output(7))
            body("cb", 1, A, h1)
            with pe.Fori(0, 4) as it:
                body("gc", it, A, h1)

            for phase, kt0, ready in (("attn_out", 0, (attn_ready, HEADS, 0)), ("conv_out", CT, (conv1_ready, 0, 2))):
                hp0, n0 = at[phase]
                with pe.Fori(0, 2) as it:
                    for j in range(4):
                        step(hp0 + 4 * it + j, j % 2, n0 + 8 * it + 2 * j, B, kt0, 2, 2 * (j % 2), ready)
            pe.wait_ge(late_loaded, 32)
            for k in range(2):
                for t in range(2):
                    nc.tensor.transpose(xp[:, 1, k * T + t * P:k * T + t * P + P], p_raw[:, t, k * P:k * P + P], ident[:])
            for k in range(KT):
                done = nc.tensor.transpose(xp[:, 2, k * META:(k + 1) * META], meta_raw[:, k * P:k * P + P],
                                           ident[0:META, 0:META])
            done.then_inc(late_turned, 1)
            with pe.Fori(0, 4) as it:
                body("w_o", it, A, (merged_ready, 0, 2))
            pe.wait_ge(meta_step, 1)
            for k in range(KT):
                done = nc.tensor.matmul(xp[:, 1, 0:META], ones[:], meta_sq[:, k, :], start=(k == 0), stop=(k == KT - 1))
            done.then_inc(meta_sum, 1)
            pe.wait_ge(p_ready, 1)
            hp0, n0 = at["ple"]
            for u in range(4):
                pe.wait_ge(lo_ready, n0 + u + 1)
                for j in range(2):
                    pe.wait_ge(evacuated, XSLOTS + hp0 + 2 * u + j - 1)
                    for k in range(2):
                        for m in range(2):
                            c = k * 512 + (2 * j + m) * P
                            nc.tensor.matmul(gp[:, 2 * j + m, :], whi[:, u, c:c + P], pT[:, k, :],
                                             start=(k == 0), stop=False)
                            done = nc.tensor.matmul(gp[:, 2 * j + m, T:2 * T], wlo[:, u, c:c + P], pT[:, k, 0:T],
                                                    start=False, stop=(k == 1))
                    done.then_inc([ple_half, unit_used][j], 1)
            column_sums(1)
            with pe.Fori(0, 4) as rnd:
                for phase, M, ready in (("up0", B, (r_ready, 0, 4)), ("down0", A, (hidden_ready, 8 * rnd, 2))):
                    hp0, n0 = at[phase]
                    with pe.Fori(0, 4) as it:
                        for j in range(2):
                            step(hp0 + 16 * rnd + 2 * it + j, j, n0 + 64 * rnd + 8 * it + 4 * j, M, ready=ready)
            body("gate", 0, B, (r_ready, 16, 4), {3: [lambda: column_sums(2)]})
            with pe.Fori(1, 4) as it:
                body("gate", it, B, (r_ready, 16, 4))
            pe.wait_ge(meta_ready, 1)

            def conv2(it, after=None):
                hp0, n0 = at["conv2"]
                for j in range(2):
                    step(hp0 + 2 * it + j, j, n0 + 8 * it + 4 * j, A, ready=(r_ready, 32, 4), meta=True,
                         after=after if j == 0 else None)

            conv2(0, {3: [lambda: column_sums(3)]})
            with pe.Fori(1, 8) as it:
                conv2(it)
            pe.wait_ge(var_ready, 4)
            for h in range(8):
                pe.wait_ge(v_ready, h + 1)
                for m in range(2):
                    done = nc.tensor.matmul(xp[:, 0, 0:T], ones[:], V[:, 2 * h + m, :], start=(h + m == 0), stop=(h + m == 8))
            done.then_inc(stat_ready, 1)
            for h in range(8):
                pe.wait_ge(ln_sq, h + 1)
                for m in range(2):
                    done = nc.tensor.matmul(xp[:, 1, 0:T], ones[:], [sq, acc][h % 2][:, m * T:m * T + T],
                                            start=(h + m == 0), stop=(h + m == 8))
                done.then_inc(ln_summed if h < 7 else stat_ready, 1)
            with pe.Fori(0, 4) as it:
                body("out2", it, B, (ln_ready, 0, 2))
            column_sums(4)
            body("glu0", 0, A, (r_ready, 48, 4), {6: [lambda: column_sums(5)]})
            with pe.Fori(1, 8) as it:
                body("glu0", it, A, (r_ready, 48, 4))
            with pe.Fori(0, 4) as it:
                body("back0", it, B, (glu_ready, 0, 2))
            with pe.Fori(0, 8) as it:
                body("glu1", it, A, (r_ready, 48, 4))
            with pe.Fori(0, 4) as it:
                body("back1", it, B, (glu_ready, 8, 2))
            with pe.Fori(0, 6) as it:
                body("glu2", it, A, (r_ready, 48, 4))
            hp0, n0 = at["back2"]
            with pe.Fori(0, 2) as it:
                for j in range(4):
                    step(hp0 + 4 * it + j, j % 2, n0 + 12 * it + 3 * j, B, 0, 3, 3 * j, (glu_ready, 16, 2))
            column_sums(6)
            pe.wait_ge(evacuated, XSLOTS + hp0 + 8)
            pe.wait_ge(var_ready, 8)
            for c in range(4):
                pe.wait_ge(out_ready, min(2 * c + 2, OUT_POOL))
                if 2 * c + 2 > OUT_POOL:
                    pe.wait_ge(out_last, 2 * c + 2 - OUT_POOL)
                for t in range(2):
                    for kk in range(4):
                        bank = (gp if c < 2 else xp)[:, 2 * (c % 2) + t, kk * P:kk * P + P]
                        done = nc.tensor.transpose(bank, r[:, 4 * c + kk, t * P:t * P + P], ident[:])
                done.then_inc(out_turned, 1)

        @block.scalar
        def _(act):
            def take_hi(n, q, slot):
                act.wait_ge(loaded[slot], 16 * q + 16)
                if not isinstance(n, int) or n >= RING:
                    act.wait_ge(unit_used, n - RING + 1)
                nc.scalar.activation(whi[:, slot, :], stage[:, slot, :], ACT.Copy).then_inc(hi_ready, 1)

            def convert(n0, q0, units=4, slot0=0):
                for u in range(units):
                    if not isinstance(n0, int) or n0 + u + RING < UNITS:
                        take_hi(n0 + u + RING, q0 + 1 + (slot0 + u) // RING, (slot0 + u) % RING)

            def take_cross(hp, j, units_done, waited=None, bias=None):
                act.wait_ge(*(waited or (unit_used, units_done)))
                act.wait_ge(evacuated, XSLOTS + hp)
                if bias is None:
                    nc.scalar.activation(cross[:], gp[:, 2 * j:2 * j + 2, T:2 * T], ACT.Copy).then_inc(cross_out, 1)
                else:
                    for m in range(2):
                        last = nc.scalar.activation(cross[:, m, :], gp[:, 2 * j + m, T:2 * T], ACT.Identity, bias=bias(m))
                    last.then_inc(cross_out, 1)

            def body(phase, it, tail, units=None):
                hp0, n0 = at[phase]
                for j in range(2):
                    n = n0 + 8 * it + 4 * j
                    for u in range(4):
                        take_hi(n + RING + u, n0 // RING + 2 * it + j + 1, u)
                        if units and 4 * j + u in units:
                            for f in units[4 * j + u]:
                                f()
                    take_cross(hp0 + 2 * it + j, j, n + 4)
                    tail(it, j)

            def none(it, j):
                pass

            def root_of(k):
                act.wait_ge(var_ready, k + 1)
                nc.scalar.activation(root[:, 0:T], var[:, 0:T], ACT.Ln).then_inc(ln_done, 1)
                act.wait_ge(ln_done, k + 1)
                nc.scalar.activation(root[:, 0:T], root[:, 0:T], ACT.Exp, scale=-0.5).then_inc(root_ready, 1)

            order = [("g_mix", 0, 0), ("g_mlp", 0, 16), ("g_ple", 0, 32), ("conv_b_in_2", 0, 48), ("conv_b_dw_2", 0, 80),
                     ("conv_ln_g_2", 0, 96), ("conv_ln_b_2", 0, 112), ("conv_b_out_2", 1, 0), ("norm_mix_pre_2", 1, 16),
                     ("norm_mix_post_2", 1, 32), ("norm_ffn_pre_2", 1, 48), ("norm_ffn_post_2", 1, 64), ("g_q", 1, 80),
                     ("g_k", 1, 81)]
            for name, half, row in order:
                n = io[name].shape[1] // P
                act.dma_start([V1, V2][half][row:row + n, :], io[name].rearrange("o (k p) -> (o k) p", p=P)).then_inc(v_loaded, 16)
            for t in range(3):
                act.dma_start(V2[82 + 8 * t:90 + 8 * t, :], io["w_conv"][0, t:t + 1, :].rearrange("o (k p) -> (o k) p", p=P)).then_inc(v_loaded, 16)
            act.dma_start(taps_raw, io["conv_w_dw_2"].rearrange("o t d -> (o t) d")).then_inc(v_loaded, 16)

            act.wait_ge(vec_turned, 1)
            nc.scalar.activation(gv[:, 0, :], xp[:, 0, 0:P], ACT.Copy)
            nc.scalar.activation(gv[:, 1, 0:106], xp[:, 0, P:P + 106], ACT.Copy).then_inc(vec_ready, 1)
            act.wait_ge(vec_ready, 1)
            for c in range(4):
                act.wait_ge(x_turned, c + 1)
                j = c % 2
                nc.scalar.activation(r[:, 4 * c:4 * c + 4, :].rearrange("p (a b) t -> p a (b t)", a=2),
                                     gp[:, 2 * j:2 * j + 2, :], ACT.Copy).then_inc(evacuated, 1)
                act.wait_ge(evacuated, c + 1)
                for kt in range(4 * c, 4 * c + 4):
                    nc.scalar.activation(A[:, kt, 0:T], r[:, kt, :], ACT.Copy, scale=col("g_mix", kt)).then_inc(x_hi, 1)
                take_hi(c, 0, c)
            act.wait_ge(vec_turned, 2)
            nc.scalar.activation(taps2[:].rearrange("p k t -> p (k t)"), xp[:, 1, 0:KT * TAPS2], ACT.Copy).then_inc(vec_ready, 1)

            def past(h):
                return not isinstance(h, int) or h >= 1

            def norms(h):
                def roots():
                    act.wait_ge(qk_var, h + 1)
                    if past(h):
                        act.wait_ge(qk_hat, 2 * h)
                    nc.scalar.activation(root[:], var[:], ACT.Ln).then_inc(qk_ln, 1)
                    act.wait_ge(qk_ln, h + 1)
                    nc.scalar.activation(root[:], root[:], ACT.Exp, scale=-0.5).then_inc(qk_root, 1)
                return {6: [roots]}

            def scores(h):
                def exps():
                    act.wait_ge(neg_max, h + 1)
                    for qt, (a, b) in enumerate(((0, P), (P, 3 * P))):
                        nc.scalar.activation(S[:, a:b], S[:, a:b], ACT.Exp, bias=small[:, 1, qt:qt + 1], scale=SCALE,
                                             accum_out=small[:, 2, qt:qt + 1]).then_inc(expd, 1)

                def copies():
                    act.wait_ge(turned, h + 1)
                    if past(h):
                        act.wait_ge(pv_done, h)
                    nc.scalar.activation(PT[:], xp[:, 2, 0:3 * P], ACT.Copy).then_inc(pt_copied, 1)
                    nc.scalar.activation(vt[:], xp[:, 3, 0:2 * P], ACT.Copy).then_inc(pt_copied, 1)
                return {4: [exps], 7: [copies]}

            def output(h):
                def hi():
                    act.wait_ge(pv_done, h + 1)
                    nc.scalar.activation(B[:, ds(h, 1), 0:T], xp[:, 3:4, T:2 * T], ACT.Copy).then_inc(attn_hi, 1)
                return {1: [hi]}

            def root_first(k, tail):
                def f(it, j):
                    if j == 0:
                        root_of(k)
                    tail(it, j)
                return f

            body("qkv", 0, root_first(0, none))
            with act.Fori(1, 5) as it:
                body("qkv", it, none)
            body("qkv", 5, none, norms(0))
            body("ga", 0, none, {**scores(0), **norms(1)})
            with act.Fori(1, 4) as it:
                body("ga", it, none, {**output(it - 1), **scores(it), **norms(it + 1)})
            with act.Fori(0, 3) as it:
                body("ccx", it, none, {**output(it + 3), **scores(it + 4), **norms(it + 5)})
            body("ccx", 3, none, {**output(6), **scores(7)})

            def cb_tail(it, j):
                hp = 2 * it + j
                act.wait_ge(cb_mul, hp + 1)
                nc.scalar.activation(B[:, ds(CT + 2 * hp, 2), 0:T], s[:, j, :, 0:T], ACT.Copy).then_inc(cb_hi, 1)

            body("cb", 0, cb_tail, output(7))
            body("cb", 1, cb_tail)
            with act.Fori(0, 4) as it:
                body("gc", it, none)

            def attn_out_tail(hp, j):
                act.wait_ge(ga_ready, 8)
                nc.scalar.activation(GA[:, ds(2 * hp, 2), :], GA[:, ds(2 * hp, 2), :], ACT.Sigmoid).then_inc(ga_sig, 1)

            def conv_out_tail(hp, j):
                act.wait_ge(gc_ready, 8)
                nc.scalar.activation(GC[:, ds(2 * hp, 2), :], GC[:, ds(2 * hp, 2), :], ACT.Sigmoid).then_inc(gc_sig, 1)
                act.wait_ge(merged, hp + 1)
                nc.scalar.activation(part(A, 0, 2 * hp, 2), s[:, j % 2, :, 0:T], ACT.Copy).then_inc(merged_hi, 1)

            for phase, tail in (("attn_out", attn_out_tail), ("conv_out", conv_out_tail)):
                hp0, n0 = at[phase]
                with act.Fori(0, 2) as it:
                    for j in range(4):
                        n = n0 + 8 * it + 2 * j
                        convert(n, n0 // RING + 2 * it, 2, 2 * j)
                        take_cross(hp0 + 4 * it + j, j % 2, n + 2)
                        tail(4 * it + j, j)

            act.wait_ge(late_turned, 1)
            nc.scalar.activation(pT[:, :, 0:T], xp[:, 1, :].rearrange("p (k t) -> p k t", k=2), ACT.Copy).then_inc(late_hi, 1)
            nc.scalar.activation(metaT[:].rearrange("p k t -> p (k t)"), xp[:, 2, 0:KT * META], ACT.Copy).then_inc(late_hi, 1)

            def hi_of_r(c0, M, gain, hp):
                act.wait_ge(r_updated, c0 + hp + 1)
                for m in range(2):
                    nc.scalar.activation(part(M, 0, 2 * hp + m, 1), r[:, ds(2 * hp + m, 1), :], ACT.Copy,
                                         scale=col(gain, 2 * hp + m)).then_inc(r_hi, 1)

            with act.Fori(0, 4) as it:
                body("w_o", it, lambda it, j: hi_of_r(0, B, "g_mlp", 2 * it + j))
            hp0, n0 = at["ple"]
            for u in range(4):
                take_hi(n0 + u + RING, n0 // RING + 1, u)
                take_cross(hp0 + 2 * u, 0, None, (ple_half, u + 1))
                take_cross(hp0 + 2 * u + 1, 1, n0 + u + 1)
            root_of(1)
            act.wait_ge(meta_var, 1)
            nc.scalar.activation(root[:, T:TM], var[:, T:TM], ACT.Ln).then_inc(meta_act, 1)
            act.wait_ge(meta_act, 1)
            nc.scalar.activation(root[:, T:TM], root[:, T:TM], ACT.Exp, scale=-0.5).then_inc(meta_act, 1)

            def ffn1(rnd, last):
                hp0, n0 = at["up0"]
                with act.Fori(0, 4) as it:
                    for j in range(2):
                        n = n0 + 64 * rnd + 8 * it + 4 * j
                        convert(n, n0 // RING + 16 * rnd + 2 * it + j)
                        take_cross(hp0 + 16 * rnd + 2 * it + j, j, n + 4)
                        act.wait_ge(up_step, 16 * rnd + 4 * it + 2 * j + 2)
                        nc.scalar.activation(part(A, 0, 4 * it + 2 * j, 2), s[:, j, :, 0:T], ACT.Copy).then_inc(up_hi, 1)
                hp0, n0 = at["down0"]
                with act.Fori(0, 4) as it:
                    for j in range(2):
                        n = n0 + 64 * rnd + 8 * it + 4 * j
                        convert(n, n0 // RING + 16 * rnd + 2 * it + j)
                        take_cross(hp0 + 16 * rnd + 2 * it + j, j, n + 4)
                        if last:
                            hi_of_r(32, B, "g_ple", 2 * it + j)

            with act.Fori(0, 3) as rnd:
                ffn1(rnd, False)
            ffn1(3, True)

            def gate_tail(it, j):
                hp = 2 * it + j
                act.wait_ge(gate_normed, hp + 1)
                nc.scalar.activation(s[:, j, :, 0:T], s[:, j, :, 0:T], ACT.Sigmoid).then_inc(gate_sig, 1)
                hi_of_r(40, A, "mix_pre", hp)

            body("gate", 0, root_first(2, gate_tail))
            act.wait_ge(meta_step, 6)
            nc.scalar.activation(A[:, :, T:TM], metaT, ACT.Copy).then_inc(meta_hi, 1)
            with act.Fori(1, 4) as it:
                body("gate", it, gate_tail)
            def conv2(it, first=False):
                hp0, n0 = at["conv2"]
                for j in range(2):
                    n, hp = n0 + 8 * it + 4 * j, hp0 + 2 * it + j
                    convert(n, n0 // RING + 2 * it + j)
                    act.wait_ge(unit_used, n + 4)
                    act.wait_ge(evacuated, XSLOTS + hp)
                    if not first:
                        act.wait_ge(c2_ready, 2 * it)
                    nc.scalar.activation(s[:, j, :, :], gp[:, 2 * j:2 * j + 2, 0:TM], ACT.Copy).then_inc(evacuated, 1)
                if first:
                    root_of(3)
                act.wait_ge(c2_normed, it + 1)
                for m in range(2):
                    nc.scalar.activation(s[:, 1, m, :], s[:, 1, m, :], ACT.Sigmoid,
                                         bias=col("b_in", KT + 2 * it + m)).then_inc(c2_sig, 1)

            conv2(0, True)
            with act.Fori(1, 8) as it:
                conv2(it)
            for h in range(8):
                act.wait_ge(centred, h + 1)
                if h >= 2:
                    act.wait_ge(ln_summed, h - 1)
                nc.scalar.activation([sq, acc][h % 2][:].rearrange("p (m t) -> p m t", m=2), V[:, 2 * h:2 * h + 2, :],
                                     ACT.Square).then_inc(ln_sq, 1)
            root_of(4)
            for c in range(8):
                act.wait_ge(ln_normed, c + 1)
                for kt in (2 * c, 2 * c + 1):
                    nc.scalar.activation(V[:, kt, :], V[:, kt, :], ACT.Silu, scale=col("ln_g", kt),
                                         bias=col("ln_b", kt)).then_inc(ln_silu, 1)

            hp0, n0 = at["out2"]
            with act.Fori(0, 4) as it:
                for j in range(2):
                    n = n0 + 8 * it + 4 * j
                    convert(n, n0 // RING + 2 * it + j)
                    take_cross(hp0 + 2 * it + j, j, n + 4, bias=lambda m: col("b_out", 4 * it + 2 * j + m))
            root_of(5)
            for h in range(9):
                if h < 8:
                    hi_of_r(48, A, "ffn_pre", h)
                if h >= 1:
                    if h >= 2:
                        act.wait_ge(acc_ready, 9 * 5 + h)
                    nc.scalar.activation(sq[:].rearrange("p (m t) -> p m t", m=2), r[:, 2 * h - 2:2 * h, :],
                                         ACT.Square).then_inc(post_sq, 1)

            def glu(rnd, it, hp_done=0):
                def tail(it, j):
                    if j == 1:
                        c = hp_done + it
                        if isinstance(it, int):
                            root_of(6)
                        act.wait_ge(glu_normed, c + 1)
                        nc.scalar.activation(root[:].rearrange("p (m t) -> p m t", m=2), s[:, 0, :, 0:T],
                                             ACT.Sigmoid).then_inc(glu_sig, 1)
                        act.wait_ge(glu_mul, 2 * c + 2)
                        nc.scalar.activation(B[:, ds(2 * it, 2), 0:T], s[:, 0, :, 0:T], ACT.Copy).then_inc(glu_hi, 1)
                body(f"glu{rnd}", it, tail)

            glu(0, 0)
            with act.Fori(1, 8) as it:
                glu(0, it)
            with act.Fori(0, 4) as it:
                body("back0", it, none)
            with act.Fori(0, 8) as it:
                glu(1, it, 8)
            with act.Fori(0, 4) as it:
                body("back1", it, none)
            with act.Fori(0, 6) as it:
                glu(2, it, 16)
            hp0, n0 = at["back2"]
            for h in range(8):
                convert(n0 + 3 * h, n0 // RING, 3, 3 * h)
                take_cross(hp0 + h, h % 2, n0 + 3 * h + 3)
            root_of(7)
            for c in range(4):
                act.wait_ge(out_turned, c + 1)
                bank = (gp if c < 2 else xp)[:, 2 * (c % 2), :]
                nc.scalar.activation(ot[:, 0, 512 * c:512 * c + 512], bank, ACT.Copy).then_inc(out_copied[0], 1)
                for t in range(2):
                    act.wait_ge(out_copied[t], c + 1)
                act.dma_start(out.rearrange("b (a p) d -> p (b a) d", p=P)[:, :, 512 * c:512 * c + 512],
                              ot[:, :, 512 * c:512 * c + 512]).then_inc(stored, 16)
            act.wait_ge(stored, 64)

        @block.vector
        def _(dve):
            def take_lo(n, slot):
                dve.wait_ge(hi_ready, n + 1)
                nc.vector.tensor_tensor(wlo[:, slot, :], stage[:, slot, :], whi[:, slot, :].bitcast(F32),
                                        ALU.subtract).then_inc(lo_ready, 1)

            def convert(n0, units=4, slot0=0):
                for u in range(units):
                    if not isinstance(n0, int) or n0 + u + RING < UNITS:
                        take_lo(n0 + u + RING, (slot0 + u) % RING)

            def add_up(hp, j, dst):
                dve.wait_ge(cross_out, hp + 1 - no_cross[0])
                nc.vector.tensor_tensor(dst, gp[:, 2 * j:2 * j + 2, 0:T], cross[:], ALU.add).then_inc(evacuated, 1)
                dve.wait_ge(evacuated, XSLOTS + hp + 1)

            no_cross = [0]

            def by_rstd(n=2):
                return rstd[:, 0:T].unsqueeze(1).broadcast_to([P, n, T])

            def body(phase, it, tail, units=None):
                hp0, n0 = at[phase]
                for j in range(2):
                    for u in range(4):
                        take_lo(n0 + 8 * it + 4 * j + RING + u, u)
                        if units and 4 * j + u in units:
                            for f in units[4 * j + u]:
                                f()
                    tail(hp0 + 2 * it + j, it, j)

            def variance(k, n, eps, bank=0):
                dve.wait_ge(stat_ready, n + 1)
                nc.vector.tensor_scalar(var[:, 0:T], xp[:, bank, 0:T], 4.0 / D, 4.0 * eps, ALU.mult, ALU.add).then_inc(var_ready, 1)
                dve.wait_ge(rstd_ready, k + 1)

            def lo_of_r(c0, M, gain, hp):
                for m in range(2):
                    dve.wait_ge(r_hi, 2 * c0 + 2 * hp + m + 1)
                    nc.vector.scalar_tensor_tensor(part(M, 1, 2 * hp + m, 1), r[:, ds(2 * hp + m, 1), :],
                                                   col(gain, 2 * hp + m), part(M, 0, 2 * hp + m, 1).bitcast(F32),
                                                   ALU.mult, ALU.subtract).then_inc(r_ready, 1)

            dve.wait_ge(vec_ready, 1)
            for c in range(4):
                for kt in range(4 * c, 4 * c + 4):
                    dve.wait_ge(x_hi, kt + 1)
                    nc.vector.scalar_tensor_tensor(A[:, kt, TM:TM + T], r[:, kt, :], col("g_mix", kt),
                                                   A[:, kt, 0:T].bitcast(F32), ALU.mult, ALU.subtract).then_inc(h1_ready, 1)
                take_lo(c, c)

            def normed_into(dst, ready, first=None):
                def tail(hp, it, j):
                    d = dst(it, j)
                    add_up(hp, j, d)
                    if first and j == 0 and isinstance(it, int) and it == 0:
                        first()
                    nc.vector.tensor_tensor(d, d, by_rstd(), ALU.mult).then_inc(ready, 1)
                return tail

            def past(h):
                return not isinstance(h, int) or h >= 1

            def norms(h):
                def variances():
                    dve.wait_ge(qk_sum, h + 1)
                    if past(h):
                        dve.wait_ge(qk_rstd, h)
                    nc.vector.tensor_scalar(var[:], xp[:, 0, :], 4.0 / HD, 4.0 * RMS_EPS, ALU.mult, ALU.add).then_inc(qk_var, 1)
                return {5: [variances]}

            def scores(h):
                def hats():
                    dve.wait_ge(qk_rstd, h + 1)
                    if past(h):
                        dve.wait_ge(scored, h)
                    for i, g in enumerate(("g_q", "g_k")):
                        nc.vector.scalar_tensor_tensor(qk[:, i:i + 1, :], qkv[:, i, ds(h, 1), :], col(g, 0),
                                                       root[:, i * T:(i + 1) * T].unsqueeze(1), ALU.mult, ALU.mult).then_inc(qk_hat, 1)

                def maxima():
                    dve.wait_ge(scored, h + 1)
                    if past(h):
                        dve.wait_ge(turned, h)
                    nc.vector.tensor_tensor(S[:], xp[:, 1, 0:3 * P], mask[:], ALU.add).then_inc(masked, 1)
                    dve.wait_ge(masked, h + 1)
                    nc.vector.tensor_reduce(small[:, 0, 0:1], S[:, 0:P], AX_X, ALU.max).then_inc(maxed, 1)
                    nc.vector.tensor_reduce(small[:, 0, 1:2], S[:, P:3 * P], AX_X, ALU.max).then_inc(maxed, 1)
                    dve.wait_ge(maxed, 2 * h + 2)
                    nc.vector.tensor_scalar(small[:, 1, :], small[:, 0, :], -SCALE, None, ALU.mult).then_inc(neg_max, 1)

                def probabilities():
                    dve.wait_ge(expd, 2 * h + 2)
                    nc.vector.reciprocal(small[:, 3, :], small[:, 2, :]).then_inc(inv_sum, 1)
                    dve.wait_ge(inv_sum, h + 1)
                    for qt, (a, b) in enumerate(((0, P), (P, 3 * P))):
                        nc.vector.tensor_scalar(S[:, a:b], S[:, a:b], small[:, 3, qt:qt + 1], None, ALU.mult).then_inc(probs, 1)
                return {1: [hats], 3: [maxima], 5: [probabilities]}

            def output(h):
                def lo():
                    dve.wait_ge(attn_hi, h + 1)
                    nc.vector.tensor_tensor(B[:, ds(h, 1), T:2 * T], xp[:, 3:4, T:2 * T], B[:, ds(h, 1), 0:T].bitcast(F32),
                                            ALU.subtract).then_inc(attn_ready, 1)
                return {2: [lo]}

            def merge(*hooks):
                return {u: [f for h in hooks for f in h.get(u, [])] for u in range(8)}

            qkv_tail = normed_into(lambda it, j: qkv_flat[:, ds(4 * it + 2 * j, 2), :], qkv_ready,
                                   lambda: variance(0, 0, RMS_EPS))
            body("qkv", 0, qkv_tail)
            with dve.Fori(1, 5) as it:
                body("qkv", it, qkv_tail)
            body("qkv", 5, qkv_tail, norms(0))
            ga_tail = normed_into(lambda it, j: GA[:, ds(4 * it + 2 * j, 2), :], ga_ready)
            body("ga", 0, ga_tail, merge(scores(0), norms(1)))
            with dve.Fori(1, 4) as it:
                body("ga", it, ga_tail, merge(output(it - 1), scores(it), norms(it + 1)))

            def ccx_tail(hp, it, j):
                add_up(hp, j, s[:, j, :, 0:T])
                if j == 0:
                    return
                four = s[:].rearrange("p j m t -> p (j m) t")[:, :, 0:T]
                nc.vector.tensor_tensor(four, four, by_rstd(4), ALU.mult).then_inc(cc_normed, 1)
                dve.wait_ge(cc_normed, it + 1)
                nc.vector.tensor_tensor(cin[:, :, 2:T + 2], s[:, 0, :, 0:T], s[:, 1, :, 0:T], ALU.mult).then_inc(cin_ready, 1)
                dve.wait_ge(cin_ready, it + 1)
                for tap in range(3):
                    for m in range(2):
                        o, i = cr[:, ds(2 * it + m, 1), :], cin[:, m:m + 1, tap:tap + T]
                        w = col("w_conv", 8 * tap + 2 * it + m)
                        if tap == 0:
                            nc.vector.tensor_scalar(o, i, w, None, ALU.mult).then_inc(cr_step, 1)
                        else:
                            dve.wait_ge(cr_step, 6 * it + 2 * (tap - 1) + m + 1)
                            nc.vector.scalar_tensor_tensor(o, i, w, o, ALU.mult, ALU.add).then_inc(cr_step, 1)

            dve.wait_ge(consts, 4)
            with dve.Fori(0, 3) as it:
                body("ccx", it, ccx_tail, merge(output(it + 3), scores(it + 4), norms(it + 5)))
            body("ccx", 3, ccx_tail, merge(output(6), scores(7)))

            def cb_tail(hp, it, j):
                t = s[:, j, :, 0:T]
                add_up(hp, j, t)
                nc.vector.tensor_tensor(t, t, by_rstd(), ALU.mult).then_inc(cb_normed, 1)
                dve.wait_ge(cb_normed, 2 * it + j + 1)
                dve.wait_ge(cr_step, 24)
                nc.vector.tensor_tensor(t, t, cr[:, ds(4 * it + 2 * j, 2), :], ALU.mult).then_inc(cb_mul, 1)
                dve.wait_ge(cb_hi, 2 * it + j + 1)
                o = ds(CT + 4 * it + 2 * j, 2)
                nc.vector.tensor_tensor(B[:, o, T:2 * T], t, B[:, o, 0:T].bitcast(F32), ALU.subtract).then_inc(conv1_ready, 2)

            body("cb", 0, cb_tail, output(7))
            body("cb", 1, cb_tail)
            gc_tail = normed_into(lambda it, j: GC[:, ds(4 * it + 2 * j, 2), :], gc_ready)
            with dve.Fori(0, 4) as it:
                body("gc", it, gc_tail)

            def attn_out_tail(hp, h, j):
                t, g = s[:, j, :, 0:T], GA[:, ds(2 * h, 2), :]
                add_up(hp, j, t)
                dve.wait_ge(ga_sig, h + 1)
                nc.vector.tensor_tensor(g, g, t, ALU.mult).then_inc(ga_y, 1)

            def conv_out_tail(hp, h, j):
                t = s[:, j, :, 0:T]
                add_up(hp, j, t)
                dve.wait_ge(gc_sig, h + 1)
                nc.vector.tensor_tensor(t, t, GC[:, ds(2 * h, 2), :], ALU.mult).then_inc(gc_y, 1)
                dve.wait_ge(gc_y, h + 1)
                dve.wait_ge(ga_y, 8)
                nc.vector.tensor_tensor(t, t, GA[:, ds(2 * h, 2), :], ALU.add).then_inc(merged, 1)
                dve.wait_ge(merged_hi, h + 1)
                nc.vector.tensor_tensor(part(A, 1, 2 * h, 2), t, part(A, 0, 2 * h, 2).bitcast(F32),
                                        ALU.subtract).then_inc(merged_ready, 1)

            for phase, tail in (("attn_out", attn_out_tail), ("conv_out", conv_out_tail)):
                hp0, n0 = at[phase]
                with dve.Fori(0, 2) as it:
                    for j in range(4):
                        convert(n0 + 8 * it + 2 * j, 2, 2 * j)
                        tail(hp0 + 4 * it + j, 4 * it + j, j % 2)

            dve.wait_ge(late_hi, 1)
            nc.vector.tensor_tensor(pT[:, :, T:2 * T], xp[:, 1, :].rearrange("p (k t) -> p k t", k=2),
                                    pT[:, :, 0:T].bitcast(F32), ALU.subtract).then_inc(p_ready, 1)

            def update_r(hp, h, j, c0, M, gain):
                t, rr = s[:, j, :, 0:T], r[:, ds(2 * h, 2), :]
                add_up(hp, j, t)
                nc.vector.tensor_tensor(rr, rr, t, ALU.add).then_inc(r_updated, 1)
                if M is not None:
                    lo_of_r(c0, M, gain, h)

            with dve.Fori(0, 4) as it:
                body("w_o", it, lambda hp, it, j: update_r(hp, 2 * it + j, j, 0, B, "g_mlp"))
            hp0, n0 = at["ple"]
            for u in range(4):
                take_lo(n0 + u + RING, u)
                for j in range(2):
                    add_up(hp0 + 2 * u + j, j, PP[:, 4 * u + 2 * j:4 * u + 2 * j + 2, :])
            variance(1, 1, RMS_EPS)
            dve.wait_ge(meta_sum, 1)
            nc.vector.tensor_scalar(var[:, T:TM], xp[:, 1, 0:META], 4.0 / D, 4.0 * RMS_EPS, ALU.mult, ALU.add).then_inc(meta_var, 1)

            def ffn1(rnd, last):
                hp0, n0 = at["up0"]
                with dve.Fori(0, 4) as it:
                    for j in range(2):
                        convert(n0 + 64 * rnd + 8 * it + 4 * j)
                        t = s[:, j, :, 0:T]
                        add_up(hp0 + 16 * rnd + 2 * it + j, j, t)
                        c = 8 * rnd + 2 * it + j
                        nc.vector.tensor_tensor(t, t, by_rstd(), ALU.mult).then_inc(up_step, 1)
                        dve.wait_ge(up_step, 2 * c + 1)
                        nc.vector.scalar_tensor_tensor(t, t, 0.0, t, ALU.max, ALU.mult).then_inc(up_step, 1)
                        dve.wait_ge(up_hi, c + 1)
                        nc.vector.tensor_tensor(part(A, 1, 4 * it + 2 * j, 2), t, part(A, 0, 4 * it + 2 * j, 2).bitcast(F32),
                                                ALU.subtract).then_inc(hidden_ready, 1)
                hp0, n0 = at["down0"]
                with dve.Fori(0, 4) as it:
                    for j in range(2):
                        convert(n0 + 64 * rnd + 8 * it + 4 * j)
                        update_r(hp0 + 16 * rnd + 2 * it + j, 2 * it + j, j, 8, B if last else None, "g_ple")

            with dve.Fori(0, 3) as rnd:
                ffn1(rnd, False)
            ffn1(3, True)

            def gate_tail(hp, it, j):
                h, t, rr = 2 * it + j, s[:, j, :, 0:T], r[:, ds(4 * it + 2 * j, 2), :]
                add_up(hp, j, t)
                if j == 0 and isinstance(it, int):
                    variance(2, 2, RMS_EPS)
                nc.vector.tensor_tensor(t, t, by_rstd(), ALU.mult).then_inc(gate_normed, 1)
                dve.wait_ge(gate_sig, h + 1)
                nc.vector.tensor_tensor(t, t, PP[:, ds(4 * it + 2 * j, 2), :], ALU.mult).then_inc(gate_mul, 1)
                dve.wait_ge(gate_mul, h + 1)
                nc.vector.tensor_tensor(rr, rr, t, ALU.add).then_inc(r_updated, 1)
                lo_of_r(16, A, "mix_pre", h)

            body("gate", 0, gate_tail)
            with dve.Fori(1, 4) as it:
                body("gate", it, gate_tail)
            dve.wait_ge(c2_pad, 1)

            def conv2(it, first=False):
                hp0, _ = at["conv2"]
                dve.wait_ge(evacuated, XSLOTS + hp0 + 2 * it + 2)
                if first:
                    variance(3, 3, RMS_EPS)
                four = s[:].rearrange("p j m t -> p (j m) t")
                nc.vector.tensor_tensor(four, four, rstd[:].unsqueeze(1).broadcast_to([P, 4, TM]), ALU.mult).then_inc(c2_normed, 1)
                for m in range(2):
                    dve.wait_ge(c2_sig, 2 * it + m + 1)
                    o = cin2[:, ds(2 * it + m, 1), :]
                    for dst, a, b in ((o[:, :, PAD2 + META:LEN2], 0, T), (o[:, :, PAD2:PAD2 + META], T, TM)):
                        last = nc.vector.scalar_tensor_tensor(dst, s[:, 0, m:m + 1, a:b], col("b_in", 2 * it + m),
                                                              s[:, 1, m:m + 1, a:b], ALU.add, ALU.mult)
                    last.then_inc(c2_ready, 1)
                dve.wait_ge(c2_ready, 2 * it + 2)
                odd = sq[:].rearrange("p (m t) -> p m t", m=2)
                for tap in range(TAPS2):
                    for m in range(2):
                        o = odd[:, m:m + 1, :] if tap % 2 else V[:, ds(2 * it + m, 1), :]
                        i, w = cin2[:, ds(2 * it + m, 1), tap:tap + T], taps2[:, ds(2 * it + m, 1), tap]
                        done = 2 * TAPS2 * it + 2 * tap + m
                        if tap == 0:
                            nc.vector.tensor_scalar(o, i, w, col("b_dw", 2 * it + m), ALU.mult, ALU.add).then_inc(tap_done, 1)
                        elif tap == 1:
                            nc.vector.tensor_scalar(o, i, w, None, ALU.mult).then_inc(tap_done, 1)
                        else:
                            dve.wait_ge(tap_done, done - 3)
                            nc.vector.scalar_tensor_tensor(o, i, w, o, ALU.mult, ALU.add).then_inc(tap_done, 1)
                dve.wait_ge(tap_done, 2 * TAPS2 * it + 2 * TAPS2)
                v = V[:, ds(2 * it, 2), :]
                nc.vector.tensor_tensor(v, v, odd, ALU.add).then_inc(v_ready, 1)
                dve.wait_ge(v_ready, it + 1)

            conv2(0, True)
            with dve.Fori(1, 8) as it:
                conv2(it)
            no_cross[0] = 16
            dve.wait_ge(stat_ready, 5)
            nc.vector.tensor_scalar(var[:, T:2 * T], xp[:, 0, 0:T], 1.0 / D, None, ALU.mult).then_inc(mean_ready, 1)
            dve.wait_ge(mean_ready, 1)
            mean = var[:, T:2 * T].unsqueeze(1).broadcast_to([P, 2, T])
            for c in range(8):
                v = V[:, 2 * c:2 * c + 2, :]
                nc.vector.tensor_tensor(v, v, mean, ALU.subtract).then_inc(centred, 1)
            variance(4, 5, LN_EPS, bank=1)
            for c in range(8 + 3):
                if c < 8:
                    v = V[:, 2 * c:2 * c + 2, :]
                    dve.wait_ge(ln_sq, c + 1)
                    nc.vector.tensor_tensor(v, v, by_rstd(), ALU.mult).then_inc(ln_normed, 1)
                if c >= 3:
                    h = c - 3
                    dve.wait_ge(ln_hi, h + 1)
                    nc.vector.tensor_tensor(part(B, 1, 2 * h, 2), V[:, 2 * h:2 * h + 2, :], part(B, 0, 2 * h, 2).bitcast(F32),
                                            ALU.subtract).then_inc(ln_ready, 1)
            dve.wait_ge(lo_ready, at["out2"][1] + RING)

            hp0, n0 = at["out2"]
            with dve.Fori(0, 4) as it:
                for j in range(2):
                    convert(n0 + 8 * it + 4 * j)
                    add_up(hp0 + 2 * it + j, j, U[:, ds(4 * it + 2 * j, 2), :])
            variance(5, 6, RMS_EPS)

            def post_norm(src, gain, h):
                for kt in (2 * h, 2 * h + 1):
                    nc.vector.scalar_tensor_tensor(src[:, kt, :], src[:, kt, :], col(gain, kt), rstd[:, 0:T], ALU.mult,
                                                   ALU.mult).then_inc(post_normed, 1)

            for h in range(8 + 3):
                if h < 8:
                    post_norm(U, "mix_post", h)
                if h >= 3:
                    lo_of_r(24, A, "ffn_pre", h - 3)

            def glu(rnd, it, hp_done=0):
                def tail(hp, it, j):
                    c = hp_done + it
                    if j == 0 and not (isinstance(it, int) and c == 0):
                        dve.wait_ge(glu_ready, c)
                    add_up(hp, j, s[:, j, :, 0:T])
                    if j == 0:
                        return
                    if isinstance(it, int):
                        variance(6, 7, RMS_EPS)
                    four = s[:].rearrange("p j m t -> p (j m) t")[:, :, 0:T]
                    nc.vector.tensor_tensor(four, four, by_rstd(4), ALU.mult).then_inc(glu_normed, 1)
                    dve.wait_ge(glu_normed, c + 1)
                    a, b = s[:, 0, :, 0:T], s[:, 1, :, 0:T]
                    nc.vector.tensor_tensor(b, b, a, ALU.mult).then_inc(glu_mul, 1)
                    dve.wait_ge(glu_mul, 2 * c + 1)
                    dve.wait_ge(glu_sig, c + 1)
                    nc.vector.tensor_tensor(a, b, root[:].rearrange("p (m t) -> p m t", m=2), ALU.mult).then_inc(glu_mul, 1)
                    dve.wait_ge(glu_hi, c + 1)
                    nc.vector.tensor_tensor(B[:, ds(2 * it, 2), T:2 * T], a, B[:, ds(2 * it, 2), 0:T].bitcast(F32),
                                            ALU.subtract).then_inc(glu_ready, 1)
                body(f"glu{rnd}", it, tail)

            def back_tail(first):
                def tail(hp, it, j):
                    f = F[:, ds(4 * it + 2 * j, 2), :]
                    if first:
                        add_up(hp, j, f)
                    else:
                        t = s[:, j, :, 0:T]
                        add_up(hp, j, t)
                        nc.vector.tensor_tensor(f, f, t, ALU.add).then_inc(r_updated, 1)
                return tail

            glu(0, 0)
            with dve.Fori(1, 8) as it:
                glu(0, it)
            with dve.Fori(0, 4) as it:
                body("back0", it, back_tail(True))
            with dve.Fori(0, 8) as it:
                glu(1, it, 8)
            with dve.Fori(0, 4) as it:
                body("back1", it, back_tail(False))
            with dve.Fori(0, 6) as it:
                glu(2, it, 16)
            hp0, n0 = at["back2"]
            for h in range(8):
                convert(n0 + 3 * h, 3, 3 * h)
                back_tail(False)(hp0 + h, h // 2, h % 2)
            variance(7, 8, RMS_EPS)
            for h in range(8):
                post_norm(F, "ffn_post", h)
            for h in range(OUT_POOL, 8):
                dve.wait_ge(post_normed, 16 + 2 * h + 2)
                o = r[:, 2 * h:2 * h + 2, :]
                nc.vector.tensor_tensor(o, o, F[:, 2 * h:2 * h + 2, :], ALU.add).then_inc(out_last, 1)
            for c in range(4):
                dve.wait_ge(out_turned, c + 1)
                bank = (gp if c < 2 else xp)[:, 2 * (c % 2) + 1, :]
                nc.vector.tensor_copy(ot[:, 1, 512 * c:512 * c + 512], bank).then_inc(out_copied[1], 1)

        @block.gpsimd
        def _(pool):
            nc.gpsimd.memset(ident[:], 0.0).then_inc(consts0, 1)
            nc.gpsimd.memset(mask[:], 0.0).then_inc(consts0, 1)
            nc.gpsimd.memset(three[:], 3.0)
            nc.gpsimd.memset(ones[:], 1.0).then_inc(consts, 1)
            pool.wait_ge(consts0, 1)
            nc.gpsimd.affine_select(out=ident[:], in_=ident[:], compare_op=ALU.not_equal, fill=1.0, base=0,
                                    pattern=[[-1, P]], channel_multiplier=1).then_inc(consts, 1)
            pool.wait_ge(consts0, 2)
            for c in (0, 2):
                last = nc.gpsimd.affine_select(out=mask[:, c * P:c * P + P], in_=mask[:, c * P:c * P + P],
                                               compare_op=ALU.is_ge, fill=NEG, base=0, pattern=[[-1, P]],
                                               channel_multiplier=1)
            last.then_inc(consts, 1)

            def clear(n):
                if n:
                    pool.wait_ge(stat_ready, n)
                nc.gpsimd.memset(acc[:], 0.0).then_inc(acc_ready, 1)

            def two(x):
                return x[:].rearrange("p (m t) -> p m t", m=2)

            def add_squares(k, h, src, nsq):
                nc.gpsimd.tensor_tensor(two(sq), src, src, ALU.mult).then_inc(squared, 1)
                pool.wait_ge(squared, nsq + h + 1)
                pool.wait_ge(acc_ready, 9 * k + h + 1)
                nc.gpsimd.tensor_tensor(acc[:], acc[:], sq[:], ALU.add).then_inc(acc_ready, 1)
                pool.wait_ge(acc_ready, 9 * k + h + 2)

            def refine(k):
                pool.wait_ge(root_ready, k + 1)
                t, y, v = sq[:, 0:T], root[:, 0:T], var[:, 0:T]
                nc.gpsimd.tensor_tensor(t, y, y, ALU.mult).then_inc(newton, 1)
                pool.wait_ge(newton, 3 * k + 1)
                nc.gpsimd.tensor_tensor(t, t, v, ALU.mult).then_inc(newton, 1)
                pool.wait_ge(newton, 3 * k + 2)
                nc.gpsimd.tensor_tensor(t, three[:].broadcast_to([P, T]), t, ALU.subtract).then_inc(newton, 1)
                pool.wait_ge(newton, 3 * k + 3)
                nc.gpsimd.tensor_tensor(rstd[:, 0:T], y, t, ALU.mult).then_inc(rstd_ready, 1)
                pool.wait_ge(rstd_ready, k + 1)

            clear(0)
            for h in range(8):
                pool.wait_ge(evacuated, h // 2 + 1)
                add_squares(0, h, r[:, 2 * h:2 * h + 2, :], 0)
            nc.gpsimd.memset(cin[:, :, 0:2], 0.0).then_inc(consts, 1)
            refine(0)

            def attention(h):
                pool.wait_ge(qkv_ready, 8)
                nc.gpsimd.tensor_tensor(two(sq), qkv[:, 0:2, ds(h, 1), :].rearrange("p a h t -> p (a h) t"),
                                        qkv[:, 0:2, ds(h, 1), :].rearrange("p a h t -> p (a h) t"), ALU.mult).then_inc(qk_sq, 1)
                pool.wait_ge(qk_root, h + 1)
                nc.gpsimd.tensor_tensor(sq[:], root[:], root[:], ALU.mult).then_inc(qk_newton, 1)
                pool.wait_ge(qk_newton, 3 * h + 1)
                nc.gpsimd.tensor_tensor(sq[:], sq[:], var[:], ALU.mult).then_inc(qk_newton, 1)
                pool.wait_ge(qk_newton, 3 * h + 2)
                nc.gpsimd.tensor_tensor(sq[:], three[:].broadcast_to([P, 2 * T]), sq[:], ALU.subtract).then_inc(qk_newton, 1)
                pool.wait_ge(qk_newton, 3 * h + 3)
                nc.gpsimd.tensor_tensor(root[:], root[:], sq[:], ALU.mult).then_inc(qk_rstd, 1)
                pool.wait_ge(qk_rstd, h + 1)
                if not isinstance(h, int) or h >= 1:
                    pool.wait_ge(turned, h)
                pool.wait_ge(qkv_ready, 12)
                nc.gpsimd.tensor_copy(vh[:].unsqueeze(1), qkv[:, 2, ds(h, 1), :]).then_inc(vh_ready, 1)

            attention(0)
            with pool.Fori(1, HEADS) as h:
                attention(h)

            def squares_of_r(k, c0, nsq):
                clear(k)
                with pool.Fori(0, 8) as h:
                    pool.wait_ge(r_updated, c0 + h + 1)
                    add_squares(k, h, r[:, ds(2 * h, 2), :], nsq)

            pool.wait_ge(late_hi, 2)
            nc.gpsimd.tensor_tensor(meta_sq, metaT, metaT, ALU.mult).then_inc(meta_step, 1)
            squares_of_r(1, 0, 8)
            refine(1)
            nc.gpsimd.memset(rstd[:, T:TM], 1.0)
            mt, my, mv = sq[:, 0:META], root[:, T:TM], var[:, T:TM]
            pool.wait_ge(meta_act, 2)
            nc.gpsimd.tensor_tensor(mt, my, my, ALU.mult).then_inc(meta_step, 1)
            pool.wait_ge(meta_step, 2)
            nc.gpsimd.tensor_tensor(mt, mt, mv, ALU.mult).then_inc(meta_step, 1)
            pool.wait_ge(meta_step, 3)
            nc.gpsimd.tensor_tensor(mt, three[:].broadcast_to([P, META]), mt, ALU.subtract).then_inc(meta_step, 1)
            pool.wait_ge(meta_step, 4)
            nc.gpsimd.tensor_tensor(my, my, mt, ALU.mult)
            half, c = vec["mix_pre"]
            nc.gpsimd.tensor_tensor(metaT, metaT, gv[:, half, c:c + KT].unsqueeze(2).broadcast_to([P, KT, META]),
                                    ALU.mult).then_inc(meta_step, 1)
            pool.wait_ge(meta_step, 5)
            nc.gpsimd.tensor_tensor(metaT, metaT, my.unsqueeze(1).broadcast_to([P, KT, META]), ALU.mult).then_inc(meta_step, 1)
            squares_of_r(2, 32, 16)
            refine(2)
            pool.wait_ge(meta_hi, 1)
            nc.gpsimd.tensor_tensor(A[:, :, TM + T:2 * TM], metaT, A[:, :, T:TM].bitcast(F32), ALU.subtract).then_inc(meta_ready, 1)
            squares_of_r(3, 40, 24)
            pool.wait_ge(gate_mul, 8)
            nc.gpsimd.memset(cin2[:, :, 0:PAD2], 0.0).then_inc(c2_pad, 1)

            def take_lo(n, slot):
                pool.wait_ge(hi_ready, n + 1)
                nc.gpsimd.tensor_tensor(wlo[:, slot, :], stage[:, slot, :], whi[:, slot, :].bitcast(F32),
                                        ALU.subtract).then_inc(lo_ready, 1)

            n0 = at["conv2"][1]
            pool.wait_ge(lo_ready, n0 + RING)
            for u in range(8):
                take_lo(n0 + RING + u, u % RING)
                if u == 4:
                    refine(3)
            with pool.Fori(1, 8) as it:
                for u in range(8):
                    take_lo(n0 + RING + 8 * it + u, u % RING)
            refine(4)
            for h in range(8):
                pool.wait_ge(ln_silu, 2 * h + 2)
                nc.gpsimd.tensor_copy(part(B, 0, 2 * h, 2), V[:, 2 * h:2 * h + 2, :]).then_inc(ln_hi, 1)
            clear(6)
            with pool.Fori(0, 8) as h:
                pool.wait_ge(evacuated, XSLOTS + at["out2"][0] + h + 1)
                add_squares(4, h, U[:, ds(2 * h, 2), :], 32)
            refine(5)
            clear(7)
            for h in range(9):
                if h < 8:
                    pool.wait_ge(post_normed, 2 * h + 2)
                    o = r[:, 2 * h:2 * h + 2, :]
                    nc.gpsimd.tensor_tensor(o, o, U[:, 2 * h:2 * h + 2, :], ALU.add).then_inc(r_updated, 1)
                if h >= 1:
                    pool.wait_ge(post_sq, h)
                    pool.wait_ge(acc_ready, 9 * 5 + h)
                    nc.gpsimd.tensor_tensor(acc[:], acc[:], sq[:], ALU.add).then_inc(acc_ready, 1)
            refine(6)
            clear(8)
            with pool.Fori(0, 8) as h:
                pool.wait_ge(r_updated, 64 + h + 1)
                add_squares(6, h, F[:, ds(2 * h, 2), :], 40)
            refine(7)
            for h in range(OUT_POOL):
                pool.wait_ge(post_normed, 16 + 2 * h + 2)
                o = r[:, 2 * h:2 * h + 2, :]
                nc.gpsimd.tensor_tensor(o, o, F[:, 2 * h:2 * h + 2, :], ALU.add).then_inc(out_ready, 1)


_INS = ["x", "p", "g_mix", "w_in", "g_q", "g_k", "w_conv", "w_attn_out", "w_conv_out", "w_o", "g_mlp", "w_up", "w_down",
        "g_ple", "w_ple_gate", "w_ple_proj", "meta_tokens_2", "conv_w_in_2", "conv_b_in_2", "conv_w_dw_2", "conv_b_dw_2",
        "conv_ln_g_2", "conv_ln_b_2", "conv_w_out_2", "conv_b_out_2", "norm_mix_pre_2", "norm_mix_post_2",
        "norm_ffn_pre_2", "norm_ffn_post_2", "ffn_w_gate_2", "ffn_w_up_2", "ffn_w_down_2"]


def kernel(**inputs):
    import numpy as _np
    import concourse.bacc as _bacc
    from concourse import mybir as _mybir
    from concourse.bass_utils import run_bass_kernel_spmd as _run

    nc = _bacc.Bacc("TRN2", target_bir_lowering=False, num_devices=1)
    arrays, io = {}, {}
    for name in _INS:
        a = _np.ascontiguousarray(inputs[name])
        arrays[f"in_{name}"] = a
        io[name] = nc.dram_tensor(f"in_{name}", a.shape, _mybir.dt.from_np(a.dtype), kind="ExternalInput").ap()
    out = nc.dram_tensor("out_0", (1, T, D), F32, kind="ExternalOutput").ap()
    two_block_kernel(nc, io, out)
    r = _run(nc, [arrays], core_ids=[0])
    return r.results[0]["out_0"]
```

```python
from contextlib import ExitStack

import concourse.bass as bass
from concourse import mybir

F32 = mybir.dt.float32
F32R = mybir.dt.float32r
ALU = mybir.AluOpType
ACT = mybir.ActivationFunctionType
AX_X = mybir.AxisListType.X
ds = bass.ds

P = 128
D = 2048
T = 256
KT = D // P
HEADS, HD = 8, 128
CONV = 1024
CT = CONV // P
FF1 = 4 * D
PLE = 256
META = 16
TM = T + META
TAPS2 = 31
FF2 = 5632
RMS_EPS, LN_EPS = 1e-6, 1e-5
SCALE = HD ** -0.5
NEG = -1e30
RING = 4
UNIT = 1024
HPW = 256
PAD2 = TAPS2 - 1 - META
LEN2 = PAD2 + META + T
PE_TAPS = 2
PE_LAST = 14
DVE_TAPS = TAPS2 - PE_TAPS
FIRST14 = (KT - 2) * P
OUT_POOL = ((2, 1), (3, 1))
XSLOTS = 4


def plan():
    sizes = [("qkv", 12, 4), ("ga", 8, 4), ("ccx", 8, 4), ("cb", 4, 4), ("gc", 8, 4), ("attn_out", 8, 2),
             ("conv_out", 8, 2), ("w_o", 8, 4), ("ple", 8, 0.5)]
    for r in range(4):
        sizes += [(f"up{r}", 8, 4), (f"down{r}", 8, 4)]
    sizes += [("gate", 8, 4), ("conv2", 16, 4), ("out2", 8, 4)]
    for r, pairs in enumerate((8, 8, 6)):
        sizes += [(f"glu{r}", 2 * pairs, 4), (f"back{r}", 8, pairs // 2)]
    at, hp, unit = {}, 0, 0
    for name, n, per in sizes:
        at[name] = (hp, unit)
        hp += n
        unit += int(n * per)
    return at, hp, unit


def two_block_kernel(nc, io, out):
    at, _, UNITS = plan()

    with ExitStack() as ctx:
        def sb(name, shape, dt=F32, where=ctx):
            return where.enter_context(nc.sbuf_tensor(name, shape, dt))

        def sem(name):
            return ctx.enter_context(nc.semaphore(name))

        r = sb("r", [P, KT, T])
        A = sb("A", [P, KT, 2 * TM], F32R)
        B = sb("B", [P, KT, 2 * T], F32R)
        stage = sb("stage", [P, RING, UNIT])
        whi = sb("whi", [P, RING, UNIT], F32R)
        wlo = sb("wlo", [P, RING, UNIT], F32R)
        work = sb("work", [P, 12804])
        cross = sb("cross", [P, 2, T])
        s = sb("s", [P, 2, 2, TM])
        sq = sb("sq", [P, 2 * T])
        acc = sb("acc", [P, 2 * T])
        var = sb("var", [P, 2 * T])
        root = sb("root", [P, 2 * T])
        rstd = sb("rstd", [P, TM])
        ident = sb("ident", [P, P])
        ones_r = sb("ones_r", [P, P], F32R)
        three = sb("three", [P, 1])
        gv = sb("gv", [P, 2, P])
        taps2 = sb("taps2", [P, KT, TAPS2])
        small = sb("small", [P, 4, 2])
        with ExitStack() as early:
            mask = sb("mask", [P, 3 * P], F32, early)
            S = sb("S", [P, 3 * P], F32, early)
            PT = sb("PT", [P, 3 * P], F32, early)
            vt = sb("vt", [P, 2 * P], F32, early)
            qk = sb("qk", [P, 2, T], F32, early)
            vh = sb("vh", [P, T], F32, early)
        pT = sb("pT", [P, 2, 2 * T], F32R)

        gp = ctx.enter_context(nc.psum_tensor("gp", [P, 4, 512], F32))
        xp = ctx.enter_context(nc.psum_tensor("xp", [P, 4, 512], F32))

        ones = ones_r[:].bitcast(F32)
        sq_parts = B[:, KT - 2:KT, :]

        def part(M, which, i, n):
            a = which * (TM if M is A else T)
            return M[:, i:i + n, a:a + T] if isinstance(i, int) else M[:, ds(i, n), a:a + T]

        def both_parts(M, kt):
            return M[:, kt, :].rearrange("p (a t) -> p a t", a=2)[:, :, 0:T]

        def area(a, n, w):
            return work[:, a:a + n * w].rearrange("p (n w) -> p n w", n=n)

        qkv = work[:, 0:24 * T].rearrange("p (a h t) -> p a h t", a=3, h=HEADS)
        qkv_flat = area(0, 24, T)
        GA = area(24 * T, KT, T)
        cr = area(40 * T, CT, T)
        cin = area(48 * T, 2, T + 2)
        GC = area(0, KT, T)
        PP = area(24 * T, KT, T)
        first_gain = work[0:KT, 2 * P:3 * P]
        xt = work[:, 24 * T:40 * T].rearrange("p (a d) -> p a d", a=2)
        V1, V2 = work[:, 40 * T:40 * T + P], work[:, 40 * T + P:40 * T + 2 * P]
        taps_raw = work[0:TAPS2, 4096:4096 + D]
        meta_raw = work[0:META, 16 * T:16 * T + D]
        p_raw = work[:, 40 * T:42 * T].rearrange("p (a d) -> p a d", a=2)
        metaT = work[:, 42 * T:43 * T].rearrange("p (k t) -> p k t", t=META)
        meta_sq = work[:, 43 * T:44 * T].rearrange("p (k t) -> p k t", t=META)
        meta_acc = work[:, 44 * T:44 * T + META]
        cin2 = area(0, KT, LEN2)
        V = area(KT * LEN2, KT, T)
        U = area(KT * LEN2 + KT * T, KT, T)
        F = area(0, KT, T)
        diag = area(KT * LEN2 + KT * T, 2 * PE_TAPS, P)
        diag_at = KT * LEN2 + KT * T + 2 * PE_TAPS * P
        diag_last = work[:, diag_at:diag_at + 2 * PE_LAST * P].rearrange("p (m a f) -> p m a f", m=2, a=PE_LAST)
        rt = work[:, KT * T:KT * T + 2 * D].rearrange("p (a d) -> p a d", a=2)
        ot = work[:, KT * T + 2 * D:KT * T + 4 * D].rearrange("p (a d) -> p a d", a=2)
        table_ahead = work[:, 12800:12801]
        tok = small

        vec = {}
        for row, name in enumerate(["g_mix", "g_mlp", "g_ple"]):
            vec[name] = (0, 16 * row)
        vec["b_in"], vec["b_dw"], vec["ln_g"], vec["ln_b"] = (0, 48), (0, 80), (0, 96), (0, 112)
        for row, name in enumerate(["b_out", "mix_pre", "mix_post", "ffn_pre", "ffn_post"]):
            vec[name] = (1, 16 * row)
        vec["g_q"], vec["g_k"], vec["w_conv"] = (1, 80), (1, 81), (1, 82)

        def col(name, i):
            half, c = vec[name]
            return gv[:, half, ds(c + i, 1)]

        loaded = [sem(f"loaded{i}") for i in range(RING)]
        hi_ready, lo_ready, unit_used = sem("hi_ready"), sem("lo_ready"), sem("unit_used")
        cross_out, evacuated = sem("cross_out"), sem("evacuated")
        x_loaded = [sem(f"x_loaded{i}") for i in range(4)]
        v_loaded, late_loaded, gain_loaded = sem("v_loaded"), sem("late_loaded"), sem("gain_loaded")
        consts, consts0 = sem("consts"), sem("consts0")
        x_turned, x_hi, h1_ready = sem("x_turned"), sem("x_hi"), sem("h1_ready")
        vec_turned, vec_ready = sem("vec_turned"), sem("vec_ready")
        acc_ready, squared = sem("acc_ready"), sem("squared")
        stat_ready, var_ready, root_ready = sem("stat_ready"), sem("var_ready"), sem("root_ready")
        inverse_ready = sem("inverse_ready")
        newton, rstd_ready = sem("newton"), sem("rstd_ready")
        r_updated, r_hi, r_ready = sem("r_updated"), sem("r_hi"), sem("r_ready")
        qk_sq, qk_sum, qk_var, qk_ln, qk_root = sem("qk_sq"), sem("qk_sum"), sem("qk_var"), sem("qk_ln"), sem("qk_root")
        qk_newton, qk_rstd, qk_hat, vh_ready = sem("qk_newton"), sem("qk_rstd"), sem("qk_hat"), sem("vh_ready")
        scored, masked, maxed, neg_max, expd = sem("scored"), sem("masked"), sem("maxed"), sem("neg_max"), sem("expd")
        inv_sum, probs, turned, pt_copied = sem("inv_sum"), sem("probs"), sem("turned"), sem("pt_copied")
        pv_done, attn_hi, attn_ready = sem("pv_done"), sem("attn_hi"), sem("attn_ready")
        qkv_ready, ga_ready, gc_ready = sem("qkv_ready"), sem("ga_ready"), sem("gc_ready")
        cc_normed, cin_ready, cr_step = sem("cc_normed"), sem("cin_ready"), sem("cr_step")
        cb_normed, cb_mul, cb_hi, conv1_ready = sem("cb_normed"), sem("cb_mul"), sem("cb_hi"), sem("conv1_ready")
        ga_sig, ga_y, gc_sig, gc_y = sem("ga_sig"), sem("ga_y"), sem("gc_sig"), sem("gc_y")
        merged, merged_hi, merged_ready = sem("merged"), sem("merged_hi"), sem("merged_ready")
        late_turned, late_hi, p_ready, ple_half = sem("late_turned"), sem("late_hi"), sem("p_ready"), sem("ple_half")
        meta_step, meta_sum, meta_var, meta_act = sem("meta_step"), sem("meta_sum"), sem("meta_var"), sem("meta_act")
        meta_acc_ready = sem("meta_acc_ready")
        meta_hi, meta_ready = sem("meta_hi"), sem("meta_ready")
        up_step, up_hi, hidden_ready = sem("up_step"), sem("up_hi"), sem("hidden_ready")
        gate_normed, gate_sig, gate_mul = sem("gate_normed"), sem("gate_sig"), sem("gate_mul")
        c2_normed, c2_sig, c2_ready, c2_pad = sem("c2_normed"), sem("c2_sig"), sem("c2_ready"), sem("c2_pad")
        tap_done, v_ready = sem("tap_done"), sem("v_ready")
        ln_sq, ln_summed = sem("ln_sq"), sem("ln_summed")
        diag_ready, diag_last_ready, pe_tapped = sem("diag_ready"), sem("diag_last_ready"), sem("pe_tapped")
        centre_ready, last_centred, last_sum, mean_taken = sem("centre_ready"), sem("last_centred"), sem("last_sum"), sem("mean_taken")
        corrected = sem("corrected")
        mean_ready, centred, ln_normed, ln_silu, ln_hi, ln_ready = (sem("mean_ready"), sem("centred"), sem("ln_normed"),
                                                                    sem("ln_silu"), sem("ln_hi"), sem("ln_ready"))
        last_sq, gained = sem("last_sq"), sem("gained")
        r_turned, rt_copied, f_turned = sem("r_turned"), sem("rt_copied"), sem("f_turned")
        token_var, token_inverse, token_root, token_newton = sem("token_var"), sem("token_inverse"), sem("token_root"), sem("token_newton")
        token_rstd, scaled, added = sem("token_rstd"), sem("scaled"), sem("added")
        post_normed, post_sq = sem("post_normed"), sem("post_sq")
        glu_normed, glu_sig, glu_mul, glu_hi, glu_ready = (sem("glu_normed"), sem("glu_sig"), sem("glu_mul"),
                                                           sem("glu_hi"), sem("glu_ready"))
        out_ready, stored = sem("out_ready"), sem("stored")

        def tiles(w):
            return w.rearrange("o (k p) n -> p (o k) n", p=P)

        W = {n: tiles(io[n]) for n in ("w_in", "w_attn_out", "w_conv_out", "w_o", "w_up", "w_down", "w_ple_gate",
                                       "w_ple_proj", "conv_w_in_2", "conv_w_out_2", "ffn_w_gate_2", "ffn_w_up_2",
                                       "ffn_w_down_2")}

        block = ctx.enter_context(nc.Block())

        @block.sync
        def _(sp):
            def load(n, slot, src, first=False):
                if not first:
                    sp.wait_ge(lo_ready, n - RING + 1)
                dst = stage[:, slot, :].rearrange("p (k n) -> p k n", k=src.shape[1])
                sp.dma_start(dst, src).then_inc(loaded[slot], 16)

            def panel(n0, slot0, w, row0, rows, c):
                for u in range(rows // 4):
                    load(n0 + u, (slot0 + u) % RING, w[:, row0 + 4 * u:row0 + 4 * u + 4, ds(c, HPW)])

            def panels(phase, w, its, col0, first_it=0, row0=0):
                n0 = at[phase][1]
                with sp.Fori(first_it, its) as it:
                    for j in range(2):
                        panel(n0 + 8 * it + 4 * j, 0, w, row0, KT, col0 + (2 * it + j) * HPW)

            def pairs(phase, wa, ca, wb, cb, its):
                n0 = at[phase][1]
                with sp.Fori(0, its) as it:
                    panel(n0 + 8 * it, 0, wa, 0, KT, ca + it * HPW)
                    panel(n0 + 8 * it + 4, 0, wb, 0, KT, cb + it * HPW)

            def half_panels(phase, w):
                n0 = at[phase][1]
                with sp.Fori(0, 2) as it:
                    for j in range(4):
                        panel(n0 + 8 * it + 2 * j, 2 * (j % 2), w, 0, 8, (4 * it + j) * HPW)

            win = W["w_in"]
            xv = io["x"].rearrange("b (a p) d -> p (b a) d", p=P)
            for c in range(4):
                sp.dma_start(xt[:, :, 512 * c:512 * c + 512], xv[:, :, 512 * c:512 * c + 512]).then_inc(x_loaded[c], 16)
                load(c, c, win[:, 4 * c:4 * c + 4, 0:HPW], first=True)
            panel(4, 0, win, 0, KT, HPW)
            panels("qkv", win, 6, 0, first_it=1)
            panels("ga", win, 4, 6144)
            pairs("ccx", win, 4096, win, 5120, 4)
            panels("cb", win, 2, 3072)
            panels("gc", win, 4, 8192)
            half_panels("attn_out", W["w_attn_out"])
            half_panels("conv_out", W["w_conv_out"])
            sp.wait_ge(cb_mul, 4)
            sp.dma_start(p_raw, io["p"].rearrange("a b (k p) d -> p (a b k) d", p=P)).then_inc(late_loaded, 16)
            sp.wait_ge(vh_ready, HEADS)
            sp.dma_start(meta_raw, io["meta_tokens_2"]).then_inc(late_loaded, 16)
            panels("w_o", W["w_o"], 4, 0)
            with sp.Fori(0, 1) as _it:
                for u in range(4):
                    load(at["ple"][1] + u, u, W["w_ple_proj"][:, 0:2, 512 * u:512 * u + 512])
            with sp.Fori(0, 4) as rnd:
                with sp.Fori(0, 4) as it:
                    for j in range(2):
                        panel(at["up0"][1] + 64 * rnd + 8 * it + 4 * j, 0, W["w_up"], 0, KT,
                              rnd * D + it * (2 * HPW) + j * HPW)
                with sp.Fori(0, 4) as it:
                    for j in range(2):
                        for u in range(4):
                            load(at["down0"][1] + 64 * rnd + 8 * it + 4 * j + u, u,
                                 W["w_down"][:, ds(rnd * KT + 4 * u, 4), ds(it * (2 * HPW) + j * HPW, HPW)])
            panels("gate", W["w_ple_gate"], 4, 0)
            pairs("conv2", W["conv_w_in_2"], 0, W["conv_w_in_2"], D, 8)
            panels("out2", W["conv_w_out_2"], 4, 0)
            for rnd, n in enumerate((8, 8, 6)):
                pairs(f"glu{rnd}", W["ffn_w_gate_2"], rnd * D, W["ffn_w_up_2"], rnd * D, n)
                if n == 8:
                    panels(f"back{rnd}", W["ffn_w_down_2"], 4, 0, row0=rnd * KT)
                else:
                    n0 = at["back2"][1]
                    with sp.Fori(0, 2) as it:
                        for j in range(4):
                            panel(n0 + 12 * it + 3 * j, 3 * j, W["ffn_w_down_2"], 2 * KT, 12, (4 * it + j) * HPW)

            for c in range(4):
                blocks = [(a, t) for a in range(c + 1) for t in range(2)]
                pool_blocks = sum(b in OUT_POOL for b in blocks)
                sp.wait_ge(added, len(blocks) - pool_blocks)
                if pool_blocks:
                    sp.wait_ge(out_ready, pool_blocks)
                sp.dma_start(out.rearrange("b (a p) d -> p (b a) d", p=P)[:, :, 512 * c:512 * c + 512],
                             ot[:, :, 512 * c:512 * c + 512]).then_inc(stored, 16)
            sp.wait_ge(stored, 64)

        @block.tensor
        def _(pe):
            def step(hp, j, n0, M, kt0=0, units=4, slot0=0, ready=None, after=None, meta=False):
                for u in range(units):
                    slot = (slot0 + u) % RING
                    pe.wait_ge(lo_ready, n0 + u + 1)
                    if u == 0:
                        pe.wait_ge(evacuated, XSLOTS + hp - 1)
                    for k in range(4):
                        if ready and k % 2 == 0:
                            pe.wait_ge(ready[0], ready[1] + ready[2] * u + ready[2] // 2 * (k // 2 + 1))
                        kt = kt0 + 4 * u + k
                        first, last = u == 0 and k == 0, u == units - 1 and k == 3
                        for m in range(2):
                            c = k * HPW + m * P
                            hi, lo = whi[:, slot, c:c + P], wlo[:, slot, c:c + P]
                            bank = gp[:, 2 * j + m, :]
                            if meta:
                                o = bank[:, 0:TM]
                                nc.tensor.matmul(o, hi, M[:, kt, 0:TM], start=first, stop=False)
                                nc.tensor.matmul(o, hi, M[:, kt, TM:2 * TM], start=False, stop=False)
                                done = nc.tensor.matmul(o, lo, M[:, kt, 0:TM], start=False, stop=last)
                            else:
                                nc.tensor.matmul(bank.rearrange("p (a t) -> p a t", a=2), hi, both_parts(M, kt),
                                                 start=first, stop=False)
                                done = nc.tensor.matmul(bank[:, T:2 * T], lo, M[:, kt, 0:T], start=False, stop=last)
                    done.then_inc(unit_used, 1)
                    if after and u in after:
                        for f in after[u]:
                            f()

            def body(phase, it, M, ready, hooks=None, kt0=0, meta=False):
                hp0, n0 = at[phase]
                for j in range(2):
                    after = {u - 4 * j: f for u, f in (hooks or {}).items() if u // 4 == j}
                    step(hp0 + 2 * it + j, j, n0 + 8 * it + 4 * j, M, kt0, ready=ready, after=after, meta=meta)

            def column_sums(k, last=0):
                pe.wait_ge(acc_ready, 9 * (k + 1))
                nc.tensor.matmul(xp[:, 0, 0:T], ones, acc[:, 0:T], start=True, stop=False)
                done = nc.tensor.matmul(xp[:, 0, 0:T], ones, acc[:, T:2 * T], start=False, stop=not last)
                if last:
                    pe.wait_ge(last_sq, last)
                    nc.tensor.matmul(xp[:, 0, 0:T], ones, root[:, 0:T], start=False, stop=False)
                    done = nc.tensor.matmul(xp[:, 0, 0:T], ones, root[:, T:2 * T], start=False, stop=True)
                done.then_inc(stat_ready, 1)

            pe.wait_ge(consts, 4)
            for c in range(4):
                j = c % 2
                pe.wait_ge(x_loaded[c], 16)
                if c >= 2:
                    pe.wait_ge(evacuated, c - 1)
                for kk in range(4):
                    for t in range(2):
                        kt = 4 * c + kk
                        o = (kk % 2) * T + t * P
                        done = nc.tensor.transpose(gp[:, 2 * j + kk // 2, o:o + P], xt[:, t, kt * P:kt * P + P], ident[:])
                done.then_inc(x_turned, 1)
                if c == 0:
                    pe.wait_ge(gain_loaded, 16)
                    nc.tensor.transpose(xp[:, 1, 0:KT], first_gain, ident[0:KT, 0:KT]).then_inc(vec_turned, 1)

            def past(h):
                return not isinstance(h, int) or h >= 1

            def norms(h):
                def f():
                    pe.wait_ge(qk_sq, 3 * h + 3)
                    if past(h):
                        pe.wait_ge(qk_var, h)
                    nc.tensor.matmul(xp[:, 0, :], ones_r[:], sq_parts[:, 0, :], start=True, stop=False)
                    nc.tensor.matmul(xp[:, 0, :], ones_r[:], sq_parts[:, 1, :], start=False, stop=True).then_inc(qk_sum, 1)
                return f

            def scores(h):
                def f():
                    pe.wait_ge(qk_hat, 2 * h + 2)
                    if past(h):
                        pe.wait_ge(masked, h)
                    nc.tensor.matmul(xp[:, 1, 0:P], qk[:, 0, 0:P], qk[:, 1, 0:P], start=True, stop=True)
                    nc.tensor.matmul(xp[:, 1, P:3 * P], qk[:, 0, P:T], qk[:, 1, :], start=True, stop=True).then_inc(scored, 1)
                return f

            def turn(h):
                def f():
                    pe.wait_ge(probs, 2 * h + 2)
                    pe.wait_ge(vh_ready, h + 1)
                    if past(h):
                        pe.wait_ge(pt_copied, 2 * h)
                    for c in range(3):
                        nc.tensor.transpose(xp[:, 2, c * P:c * P + P], S[:, c * P:c * P + P], ident[:])
                    nc.tensor.transpose(xp[:, 3, 0:P], vh[:, 0:P], ident[:])
                    nc.tensor.transpose(xp[:, 3, P:2 * P], vh[:, P:2 * P], ident[:]).then_inc(turned, 1)
                return f

            def output(h):
                def f():
                    pe.wait_ge(pt_copied, 2 * h + 2)
                    if past(h):
                        pe.wait_ge(attn_ready, h)
                    nc.tensor.matmul(xp[:, 3, T:2 * T], vt[:, 0:P], PT[:, 0:2 * P], start=True, stop=False)
                    nc.tensor.matmul(xp[:, 3, T + P:2 * T], vt[:, P:2 * P], PT[:, 2 * P:3 * P], start=False,
                                     stop=True).then_inc(pv_done, 1)
                return f

            def beside(i):
                if not isinstance(i, int):
                    return {4: [turn(i - 1), scores(i), norms(i + 1)], 6: [output(i - 1)]}
                return {4: ([turn(i - 1)] if i else []) + ([scores(i)] if i < HEADS else [])
                        + ([norms(i + 1)] if i + 1 < HEADS else []), 6: [output(i - 1)] if i else []}

            h1 = (h1_ready, 0, 4)
            body("qkv", 0, A, h1, {4: [lambda: column_sums(0)]})
            pe.wait_ge(v_loaded, 16 * 18)
            nc.tensor.transpose(xp[:, 2, 0:P], V1, ident[:])
            nc.tensor.transpose(xp[:, 2, P:P + 106], V2[0:106, :], ident[0:106, 0:106]).then_inc(vec_turned, 1)
            for k in range(KT):
                done = nc.tensor.transpose(xp[:, 3, k * TAPS2:(k + 1) * TAPS2], taps_raw[:, k * P:k * P + P],
                                           ident[0:TAPS2, 0:TAPS2])
            done.then_inc(vec_turned, 1)
            with pe.Fori(1, 5) as it:
                body("qkv", it, A, h1)
            body("qkv", 5, A, h1, {4: [norms(0)]})
            body("ga", 0, A, h1, beside(0))
            with pe.Fori(1, 4) as it:
                body("ga", it, A, h1, beside(it))
            with pe.Fori(0, 3) as it:
                body("ccx", it, A, h1, beside(it + 4))
            body("ccx", 3, A, h1, beside(7))
            body("cb", 0, A, h1, beside(8))
            body("cb", 1, A, h1)
            with pe.Fori(0, 4) as it:
                body("gc", it, A, h1)

            for phase, kt0, ready in (("attn_out", 0, (attn_ready, HEADS, 0)), ("conv_out", CT, (conv1_ready, 0, 4))):
                hp0, n0 = at[phase]
                with pe.Fori(0, 2) as it:
                    for j in range(4):
                        step(hp0 + 4 * it + j, j % 2, n0 + 8 * it + 2 * j, B, kt0, 2, 2 * (j % 2), ready)
            pe.wait_ge(late_loaded, 32)
            for k in range(2):
                for t in range(2):
                    nc.tensor.transpose(xp[:, 1, k * T + t * P:k * T + t * P + P], p_raw[:, t, k * P:k * P + P], ident[:])
            for k in range(KT):
                done = nc.tensor.transpose(xp[:, 2, k * META:(k + 1) * META], meta_raw[:, k * P:k * P + P],
                                           ident[0:META, 0:META])
            done.then_inc(late_turned, 1)
            with pe.Fori(0, 4) as it:
                body("w_o", it, A, (merged_ready, 0, 2))
            pe.wait_ge(meta_acc_ready, 1)
            nc.tensor.matmul(xp[:, 1, 0:META], ones, meta_acc, start=True, stop=True).then_inc(meta_sum, 1)
            pe.wait_ge(p_ready, 1)
            hp0, n0 = at["ple"]
            for u in range(4):
                pe.wait_ge(lo_ready, n0 + u + 1)
                for j in range(2):
                    pe.wait_ge(evacuated, XSLOTS + hp0 + 2 * u + j - 1)
                    for k in range(2):
                        for m in range(2):
                            c = k * 512 + (2 * j + m) * P
                            nc.tensor.matmul(gp[:, 2 * j + m, :], whi[:, u, c:c + P], pT[:, k, :],
                                             start=(k == 0), stop=False)
                            done = nc.tensor.matmul(gp[:, 2 * j + m, T:2 * T], wlo[:, u, c:c + P], pT[:, k, 0:T],
                                                    start=False, stop=(k == 1))
                    done.then_inc([ple_half, unit_used][j], 1)
            column_sums(1)
            with pe.Fori(0, 4) as rnd:
                for phase, M, ready in (("up0", B, (r_ready, 0, 4)), ("down0", A, (hidden_ready, 8 * rnd, 2))):
                    hp0, n0 = at[phase]
                    with pe.Fori(0, 4) as it:
                        for j in range(2):
                            step(hp0 + 16 * rnd + 2 * it + j, j, n0 + 64 * rnd + 8 * it + 4 * j, M, ready=ready)
            body("gate", 0, B, (r_ready, 16, 4), {2: [lambda: column_sums(2)]})
            with pe.Fori(1, 4) as it:
                body("gate", it, B, (r_ready, 16, 4))
            pe.wait_ge(meta_ready, 1)

            def conv2(it, after=None):
                hp0, n0 = at["conv2"]
                for j in range(2):
                    step(hp0 + 2 * it + j, j, n0 + 8 * it + 4 * j, A, ready=(r_ready, 32, 4), meta=True,
                         after=after if j == 0 else None)

            def taps(q):
                def f():
                    pe.wait_ge(c2_ready, 2 * q + 2)
                    pe.wait_ge(diag_ready, 2 * PE_TAPS * q + 2 * PE_TAPS)
                    if past(q):
                        pe.wait_ge(tap_done, 2 * DVE_TAPS * (q - 1) + 4)
                    for m in range(2):
                        for a in range(PE_TAPS):
                            t = DVE_TAPS + a
                            done = nc.tensor.matmul(xp[:, 2, m * T:m * T + T], diag[:, PE_TAPS * m + a, :],
                                                    cin2[:, ds(2 * q + m, 1), t:t + T].rearrange("p k t -> p (k t)"),
                                                    start=(a == 0), stop=(a == PE_TAPS - 1))
                    done.then_inc(pe_tapped, 1)
                return f

            def last_taps(m):
                pe.wait_ge(c2_ready, 16)
                pe.wait_ge(diag_last_ready, 2)
                for a in range(PE_LAST):
                    t = TAPS2 - PE_LAST + a
                    done = nc.tensor.matmul(xp[:, 3, m * T:m * T + T], diag_last[:, m, a, :], cin2[:, KT - 2 + m, t:t + T],
                                            start=(a == 0), stop=(a == PE_LAST - 1))
                done.then_inc(pe_tapped, 1)

            conv2(0, {3: [lambda: column_sums(3)]})
            conv2(1, {3: [taps(0)]})
            with pe.Fori(2, 8) as it:
                conv2(it, {3: [taps(it - 1)]})

            def sums_of_v(h):
                pe.wait_ge(v_ready, h + 1)
                for m in range(2):
                    done = nc.tensor.matmul(xp[:, 0, 0:T], ones, V[:, 2 * h + m, :], start=(h + m == 0), stop=(h + m == 7))
                return done

            pe.wait_ge(var_ready, 4)
            for h in range(6):
                sums_of_v(h)
            last_taps(0)
            sums_of_v(6).then_inc(stat_ready, 1)
            last_taps(1)

            def sums_of_squares(h):
                pe.wait_ge(ln_sq, h + 1)
                for m in range(2):
                    done = nc.tensor.matmul(xp[:, 1, 0:T], ones, [acc, root][h % 2][:, m * T:m * T + T],
                                            start=(h + m == 0), stop=(h + m == 8))
                return done

            for h in range(7):
                sums_of_squares(h).then_inc(ln_summed, 1)
            pe.wait_ge(last_centred, 1)
            for m in range(2):
                done = nc.tensor.matmul(xp[:, 0, T:2 * T], ones, V[:, KT - 2 + m, :], start=(m == 0), stop=(m == 1))
            done.then_inc(last_sum, 1)
            sums_of_squares(7).then_inc(stat_ready, 1)
            with pe.Fori(0, 4) as it:
                body("out2", it, B, (ln_ready, 0, 2))
            column_sums(4, 1)
            body("glu0", 0, A, (r_ready, 48, 4), {5: [lambda: column_sums(5)]})
            with pe.Fori(1, 8) as it:
                body("glu0", it, A, (r_ready, 48, 4))
            with pe.Fori(0, 4) as it:
                body("back0", it, B, (glu_ready, 0, 2))
            with pe.Fori(0, 8) as it:
                body("glu1", it, A, (r_ready, 48, 4))
            with pe.Fori(0, 4) as it:
                body("back1", it, B, (glu_ready, 8, 2))
            with pe.Fori(0, 6) as it:
                body("glu2", it, A, (r_ready, 48, 4))
            def turn_r(t):
                for kt in range(KT):
                    done = nc.tensor.transpose(xp[:, kt // 4, (kt % 4) * P:(kt % 4) * P + P], r[:, kt, t * P:t * P + P], ident[:])
                done.then_inc(r_turned, 1)

            pe.wait_ge(var_ready, 7)
            turn_r(0)
            hp0, n0 = at["back2"]
            with pe.Fori(0, 2) as it:
                for j in range(4):
                    step(hp0 + 4 * it + j, j % 2, n0 + 12 * it + 3 * j, B, 0, 3, 3 * j, (glu_ready, 16, 2))
            pe.wait_ge(rt_copied, 1)
            turn_r(1)

            def turn_f(t, c, kt_end):
                for kt in range(4 * c, kt_end):
                    k = kt % 4
                    done = nc.tensor.transpose((gp if t else xp)[:, c, k * P:k * P + P], F[:, kt, t * P:t * P + P], ident[:])
                return done

            pe.wait_ge(evacuated, XSLOTS + hp0 + 8)
            pe.wait_ge(gained, 15)
            for c in range(3):
                done = turn_f(1, c, 4 * c + 4)
            pe.wait_ge(acc_ready, 9 * 7)
            for part_of in range(2):
                if part_of:
                    pe.wait_ge(last_sq, 2)
                src = root if part_of else acc
                for t in range(2):
                    for m in range(2):
                        done = nc.tensor.matmul(gp[:, 3, 2 * t + part_of:2 * t + part_of + 1], src[:, m * T + t * P:m * T + t * P + P],
                                                ones_r[:, 0:1].bitcast(F32), start=(m == 0), stop=(m == 1))
            done.then_inc(stat_ready, 1)
            pe.wait_ge(rt_copied, 2)
            for c in range(3):
                turn_f(0, c, 4 * c + 4)
            pe.wait_ge(gained, 16)
            turn_f(0, 3, KT)
            pe.wait_ge(token_var, 1)
            turn_f(1, 3, KT).then_inc(f_turned, 1)

        @block.scalar
        def _(act):
            def take_hi(n, q, slot):
                act.wait_ge(loaded[slot], 16 * q + 16)
                if not isinstance(n, int) or n >= RING:
                    act.wait_ge(unit_used, n - RING + 1)
                nc.scalar.activation(whi[:, slot, :], stage[:, slot, :], ACT.Copy).then_inc(hi_ready, 1)

            def convert(n0, q0, units=4, slot0=0):
                for u in range(units):
                    if not isinstance(n0, int) or n0 + u + RING < UNITS:
                        take_hi(n0 + u + RING, q0 + 1 + (slot0 + u) // RING, (slot0 + u) % RING)

            def take_cross(hp, j, units_done, waited=None, bias=None):
                act.wait_ge(*(waited or (unit_used, units_done)))
                act.wait_ge(evacuated, XSLOTS + hp)
                if bias is None:
                    nc.scalar.activation(cross[:], gp[:, 2 * j:2 * j + 2, T:2 * T], ACT.Copy).then_inc(cross_out, 1)
                else:
                    for m in range(2):
                        last = nc.scalar.activation(cross[:, m, :], gp[:, 2 * j + m, T:2 * T], ACT.Identity, bias=bias(m))
                    last.then_inc(cross_out, 1)

            def body(phase, it, tail, units=None):
                hp0, n0 = at[phase]
                for j in range(2):
                    n = n0 + 8 * it + 4 * j
                    for u in range(4):
                        take_hi(n + RING + u, n0 // RING + 2 * it + j + 1, u)
                        if units and 4 * j + u in units:
                            for f in units[4 * j + u]:
                                f()
                    take_cross(hp0 + 2 * it + j, j, n + 4)
                    tail(it, j)

            def none(it, j):
                pass

            def root_of(k):
                act.wait_ge(inverse_ready, k + 1)
                nc.scalar.activation(root[:, 0:T], root[:, 0:T], ACT.Sqrt).then_inc(root_ready, 1)

            def apply_gain(src, gain, k, h, done):
                if isinstance(h, int) and h == 7:
                    act.wait_ge(last_sq, done)
                else:
                    act.wait_ge(acc_ready, 9 * k + h + 2)
                for m in range(2):
                    t = src[:, ds(2 * h + m, 1), :]
                    last = nc.scalar.activation(t, t, ACT.Copy, scale=col(gain, 2 * h + m))
                last.then_inc(gained, 1)

            def last_squares(src):
                nc.scalar.activation(root[:].rearrange("p (m t) -> p m t", m=2), src[:, KT - 2:KT, :],
                                     ACT.Square).then_inc(last_sq, 1)

            act.dma_start(first_gain, io["g_mix"].rearrange("o (k p) -> (o k) p", p=P)).then_inc(gain_loaded, 16)
            order = [("g_mix", 0, 0), ("g_mlp", 0, 16), ("g_ple", 0, 32), ("conv_b_in_2", 0, 48), ("conv_b_dw_2", 0, 80),
                     ("conv_ln_g_2", 0, 96), ("conv_ln_b_2", 0, 112), ("conv_b_out_2", 1, 0), ("norm_mix_pre_2", 1, 16),
                     ("norm_mix_post_2", 1, 32), ("norm_ffn_pre_2", 1, 48), ("norm_ffn_post_2", 1, 64), ("g_q", 1, 80),
                     ("g_k", 1, 81)]

            def load_vector(name, half, row):
                n = io[name].shape[1] // P
                act.dma_start([V1, V2][half][row:row + n, :], io[name].rearrange("o (k p) -> (o k) p", p=P)).then_inc(v_loaded, 16)

            def load_conv(t):
                act.dma_start(V2[82 + 8 * t:90 + 8 * t, :], io["w_conv"][0, t:t + 1, :].rearrange("o (k p) -> (o k) p", p=P)).then_inc(v_loaded, 16)

            vectors = [lambda a=a: load_vector(*a) for a in order] + [lambda t=t: load_conv(t) for t in range(3)]
            vectors.append(lambda: act.dma_start(taps_raw, io["conv_w_dw_2"].rearrange("o t d -> (o t) d")).then_inc(v_loaded, 16))

            act.wait_ge(vec_turned, 1)
            nc.scalar.activation(gv[:, 0, 0:KT], xp[:, 1, 0:KT], ACT.Copy).then_inc(vec_ready, 1)
            act.wait_ge(vec_ready, 1)
            for c in range(4):
                act.wait_ge(x_turned, c + 1)
                j = c % 2
                nc.scalar.activation(r[:, 4 * c:4 * c + 4, :].rearrange("p (a b) t -> p a (b t)", a=2),
                                     gp[:, 2 * j:2 * j + 2, :], ACT.Copy).then_inc(evacuated, 1)
                act.wait_ge(evacuated, c + 1)
                for kt in range(4 * c, 4 * c + 4):
                    nc.scalar.activation(A[:, kt, 0:T], r[:, kt, :], ACT.Copy, scale=col("g_mix", kt)).then_inc(x_hi, 1)
                take_hi(c, 0, c)

            def past(h):
                return not isinstance(h, int) or h >= 1

            def norms(h):
                def roots():
                    act.wait_ge(qk_var, h + 1)
                    if past(h):
                        act.wait_ge(qk_hat, 2 * h)
                    nc.scalar.activation(root[:], var[:], ACT.Ln).then_inc(qk_ln, 1)
                    act.wait_ge(qk_ln, h + 1)
                    nc.scalar.activation(root[:], root[:], ACT.Exp, scale=-0.5).then_inc(qk_root, 1)
                return roots

            def exponentials(h):
                def exps():
                    act.wait_ge(neg_max, h + 1)
                    for qt, (a, b) in enumerate(((0, P), (P, 3 * P))):
                        nc.scalar.activation(S[:, a:b], S[:, a:b], ACT.Exp, bias=small[:, 1, qt:qt + 1], scale=SCALE,
                                             accum_out=small[:, 2, qt:qt + 1]).then_inc(expd, 1)

                return exps

            def turn(h):
                def copies():
                    act.wait_ge(turned, h + 1)
                    if past(h):
                        act.wait_ge(pv_done, h)
                    nc.scalar.activation(PT[:], xp[:, 2, 0:3 * P], ACT.Copy).then_inc(pt_copied, 1)
                    nc.scalar.activation(vt[:], xp[:, 3, 0:2 * P], ACT.Copy).then_inc(pt_copied, 1)
                return copies

            def output(h):
                def hi():
                    act.wait_ge(pv_done, h + 1)
                    nc.scalar.activation(B[:, ds(h, 1), 0:T], xp[:, 3:4, T:2 * T], ACT.Copy).then_inc(attn_hi, 1)
                return hi

            def beside(i):
                if not isinstance(i, int):
                    return {5: [turn(i - 1)], 6: [norms(i + 1)], 7: [output(i - 1), exponentials(i)]}
                return {5: [turn(i - 1)] if i else [], 6: [norms(i + 1)] if i + 1 < HEADS else [],
                        7: ([output(i - 1)] if i else []) + ([exponentials(i)] if i < HEADS else [])}

            def root_first(k, tail):
                def f(it, j):
                    if j == 0:
                        root_of(k)
                    tail(it, j)
                return f

            body("qkv", 0, root_first(0, none), {u: vectors[3 * u:3 * u + 3] for u in range(6)})
            act.wait_ge(vec_turned, 3)
            nc.scalar.activation(gv[:, 0, KT:P], xp[:, 2, KT:P], ACT.Copy)
            nc.scalar.activation(gv[:, 1, 0:106], xp[:, 2, P:P + 106], ACT.Copy)
            nc.scalar.activation(taps2[:].rearrange("p k t -> p (k t)"), xp[:, 3, 0:KT * TAPS2], ACT.Copy).then_inc(vec_ready, 1)
            with act.Fori(1, 5) as it:
                body("qkv", it, none)
            body("qkv", 5, none, {6: [norms(0)]})
            body("ga", 0, none, beside(0))
            with act.Fori(1, 4) as it:
                body("ga", it, none, beside(it))
            with act.Fori(0, 3) as it:
                body("ccx", it, none, beside(it + 4))
            body("ccx", 3, none, beside(7))

            def cb_tail(it, j):
                hp = 2 * it + j
                act.wait_ge(cb_mul, hp + 1)
                nc.scalar.activation(B[:, ds(CT + 2 * hp, 2), 0:T], s[:, j, :, 0:T], ACT.Copy).then_inc(cb_hi, 1)

            body("cb", 0, cb_tail, beside(8))
            body("cb", 1, cb_tail)

            def gc_tail(it, j):
                o = GC[:, ds(4 * it + 2 * j, 2), :]
                act.wait_ge(gc_ready, 2 * it + j + 1)
                nc.scalar.activation(o, o, ACT.Sigmoid).then_inc(gc_sig, 1)

            with act.Fori(0, 4) as it:
                body("gc", it, gc_tail)

            def attn_out_tail(hp, j):
                act.wait_ge(ga_ready, 8)
                nc.scalar.activation(GA[:, ds(2 * hp, 2), :], GA[:, ds(2 * hp, 2), :], ACT.Sigmoid).then_inc(ga_sig, 1)

            def conv_out_tail(hp, j):
                for back in (1, 0) if j == 3 else (1,) if j else ():
                    act.wait_ge(merged, hp - back + 1)
                    nc.scalar.activation(part(A, 0, 2 * (hp - back), 2), s[:, (j - back) % 2, :, 0:T],
                                         ACT.Copy).then_inc(merged_hi, 1)

            for phase, tail in (("attn_out", attn_out_tail), ("conv_out", conv_out_tail)):
                hp0, n0 = at[phase]
                with act.Fori(0, 2) as it:
                    for j in range(4):
                        n = n0 + 8 * it + 2 * j
                        convert(n, n0 // RING + 2 * it, 2, 2 * j)
                        take_cross(hp0 + 4 * it + j, j % 2, n + 2)
                        tail(4 * it + j, j)

            act.wait_ge(late_turned, 1)
            nc.scalar.activation(pT[:, :, 0:T], xp[:, 1, :].rearrange("p (k t) -> p k t", k=2), ACT.Copy).then_inc(late_hi, 1)
            nc.scalar.activation(metaT[:].rearrange("p k t -> p (k t)"), xp[:, 2, 0:KT * META], ACT.Copy).then_inc(late_hi, 1)

            def hi_of_r(c0, M, gain, hp):
                act.wait_ge(r_updated, c0 + hp + 1)
                for m in range(2):
                    nc.scalar.activation(part(M, 0, 2 * hp + m, 1), r[:, ds(2 * hp + m, 1), :], ACT.Copy,
                                         scale=col(gain, 2 * hp + m)).then_inc(r_hi, 1)

            def w_o_tail(it, j):
                if not (isinstance(it, int) and j == 1):
                    hi_of_r(0, B, "g_mlp", 2 * it + j)

            with act.Fori(0, 3) as it:
                body("w_o", it, w_o_tail)
            body("w_o", 3, w_o_tail)
            hp0, n0 = at["ple"]
            for u in range(4):
                take_cross(hp0 + 2 * u, 0, None, (ple_half, u + 1))
                take_cross(hp0 + 2 * u + 1, 1, n0 + u + 1)
                take_hi(n0 + u + RING, n0 // RING + 1, u)
                if u == 0:
                    hi_of_r(0, B, "g_mlp", 7)
            root_of(1)
            act.wait_ge(meta_var, 1)
            nc.scalar.activation(root[:, T:TM], var[:, T:TM], ACT.Ln).then_inc(meta_act, 1)
            act.wait_ge(meta_act, 1)
            nc.scalar.activation(root[:, T:TM], root[:, T:TM], ACT.Exp, scale=-0.5).then_inc(meta_act, 1)

            def ffn1(rnd, last):
                hp0, n0 = at["up0"]
                with act.Fori(0, 4) as it:
                    for j in range(2):
                        n = n0 + 64 * rnd + 8 * it + 4 * j
                        convert(n, n0 // RING + 16 * rnd + 2 * it + j)
                        take_cross(hp0 + 16 * rnd + 2 * it + j, j, n + 4)
                        act.wait_ge(up_step, 16 * rnd + 4 * it + 2 * j + 2)
                        nc.scalar.activation(part(A, 0, 4 * it + 2 * j, 2), s[:, j, :, 0:T], ACT.Copy).then_inc(up_hi, 1)
                hp0, n0 = at["down0"]
                with act.Fori(0, 4) as it:
                    for j in range(2):
                        n = n0 + 64 * rnd + 8 * it + 4 * j
                        convert(n, n0 // RING + 16 * rnd + 2 * it + j)
                        take_cross(hp0 + 16 * rnd + 2 * it + j, j, n + 4)
                        if last:
                            hi_of_r(32, B, "g_ple", 2 * it + j)

            with act.Fori(0, 3) as rnd:
                ffn1(rnd, False)
            ffn1(3, True)

            def gate_tail(it, j):
                hp = 2 * it + j
                act.wait_ge(gate_normed, hp + 1)
                nc.scalar.activation(s[:, j, :, 0:T], s[:, j, :, 0:T], ACT.Sigmoid).then_inc(gate_sig, 1)
                hi_of_r(40, A, "mix_pre", hp)

            body("gate", 0, gate_tail, {2: [lambda: root_of(2)]})
            act.wait_ge(meta_step, 6)
            nc.scalar.activation(A[:, :, T:TM], metaT, ACT.Copy).then_inc(meta_hi, 1)
            with act.Fori(1, 4) as it:
                body("gate", it, gate_tail)
            def gates(q):
                act.wait_ge(c2_normed, q + 1)
                for m in range(2):
                    nc.scalar.activation(s[:, 1, m, :], s[:, 1, m, :], ACT.Sigmoid,
                                         bias=col("b_in", KT + 2 * q + m)).then_inc(c2_sig, 1)
                    nc.scalar.activation(s[:, 0, m, :], s[:, 0, m, :], ACT.Identity,
                                         bias=col("b_in", 2 * q + m)).then_inc(c2_sig, 1)
                if isinstance(q, int) and q == 7:
                    return
                if past(q):
                    act.wait_ge(pe_tapped, q)
                for m in range(2):
                    for a in range(PE_TAPS):
                        nc.scalar.activation(diag[:, PE_TAPS * m + a, :], ident[:], ACT.Copy,
                                             scale=taps2[:, ds(2 * q + m, 1), DVE_TAPS + a]).then_inc(diag_ready, 1)

            def conv2(it, first=False, q=None):
                hp0, n0 = at["conv2"]
                for j in range(2):
                    n, hp = n0 + 8 * it + 4 * j, hp0 + 2 * it + j
                    for u in range(4):
                        take_hi(n + RING + u, n0 // RING + 2 * it + j + 1, u)
                        if not first and j == 0 and u == 0:
                            gates(it - 1 if q is None else q)
                    act.wait_ge(unit_used, n + 4)
                    act.wait_ge(evacuated, XSLOTS + hp)
                    if not first:
                        act.wait_ge(c2_ready, 2 * it)
                    nc.scalar.activation(s[:, j, :, :], gp[:, 2 * j:2 * j + 2, 0:TM], ACT.Copy).then_inc(evacuated, 1)
                if first:
                    root_of(3)

            conv2(0, True)
            conv2(1)
            with act.Fori(2, 8) as it:
                conv2(it)
            gates(7)
            act.wait_ge(stat_ready, 5)
            centre = var[:, T:2 * T]
            nc.scalar.activation(centre, xp[:, 0, 0:T], ACT.Copy, scale=1.0 / FIRST14).then_inc(centre_ready, 1)
            for h in range(8):
                if h < 7:
                    act.wait_ge(centred, h + 1)
                else:
                    act.wait_ge(last_centred, 1)
                if h >= 2:
                    act.wait_ge(ln_summed, h - 1)
                nc.scalar.activation([acc, root][h % 2][:].rearrange("p (m t) -> p m t", m=2), V[:, 2 * h:2 * h + 2, :],
                                     ACT.Square).then_inc(ln_sq, 1)
            root_of(4)
            for c in range(8):
                act.wait_ge(ln_normed, c + 1)
                for kt in (2 * c, 2 * c + 1):
                    nc.scalar.activation(V[:, kt, :], V[:, kt, :], ACT.Silu, scale=col("ln_g", kt),
                                         bias=col("ln_b", kt)).then_inc(ln_silu, 1)
                act.wait_ge(ln_silu, 2 * c + 2)
                nc.scalar.activation(part(B, 0, 2 * c, 2), V[:, 2 * c:2 * c + 2, :], ACT.Copy).then_inc(ln_hi, 1)

            hp0, n0 = at["out2"]

            def out2(it, first=False):
                for j in range(2):
                    n = n0 + 8 * it + 4 * j
                    convert(n, n0 // RING + 2 * it + j)
                    take_cross(hp0 + 2 * it + j, j, n + 4, bias=lambda m: col("b_out", 4 * it + 2 * j + m))
                    if not first or j:
                        apply_gain(U, "mix_post", 4, 2 * it + j - 1, 1)

            out2(0, True)
            with act.Fori(1, 4) as it:
                out2(it)
            act.wait_ge(evacuated, XSLOTS + hp0 + 8)
            last_squares(U)
            apply_gain(U, "mix_post", 4, 7, 1)
            root_of(5)
            for h in range(9):
                if h < 8:
                    hi_of_r(48, A, "ffn_pre", h)
                if h >= 1:
                    nc.scalar.activation(U[:, 2 * h - 2:2 * h, :], r[:, 2 * h - 2:2 * h, :], ACT.Square).then_inc(post_sq, 1)

            def glu(rnd, it, hp_done=0, units=None):
                def tail(it, j):
                    if j == 1:
                        c = hp_done + it
                        act.wait_ge(glu_normed, c + 1)
                        nc.scalar.activation(root[:].rearrange("p (m t) -> p m t", m=2), s[:, 0, :, 0:T],
                                             ACT.Sigmoid).then_inc(glu_sig, 1)
                        act.wait_ge(glu_mul, 2 * c + 2)
                        nc.scalar.activation(B[:, ds(2 * it, 2), 0:T], s[:, 0, :, 0:T], ACT.Copy).then_inc(glu_hi, 1)
                body(f"glu{rnd}", it, tail, units)

            glu(0, 0, units={5: [lambda: root_of(6)]})
            with act.Fori(1, 8) as it:
                glu(0, it)
            with act.Fori(0, 4) as it:
                body("back0", it, none)
            with act.Fori(0, 8) as it:
                glu(1, it, 8)
            with act.Fori(0, 4) as it:
                body("back1", it, none)
            with act.Fori(0, 6) as it:
                glu(2, it, 16)
            hp0, n0 = at["back2"]

            def copy_r(t):
                act.wait_ge(r_turned, t + 1)
                nc.scalar.activation(rt[:, t, :], xp[:].rearrange("p b f -> p (b f)"), ACT.Copy).then_inc(rt_copied, 1)

            for h in range(8):
                convert(n0 + 3 * h, n0 // RING, 3, 3 * h)
                take_cross(hp0 + h, h % 2, n0 + 3 * h + 3)
                if h == 0:
                    copy_r(0)
                else:
                    apply_gain(F, "ffn_post", 6, h - 1, 2)
            copy_r(1)
            nc.scalar.activation(table_ahead, ones_r[:, 0:1].bitcast(F32), ACT.Sqrt)
            act.wait_ge(r_updated, 72)
            last_squares(F)
            apply_gain(F, "ffn_post", 6, 7, 2)
            act.wait_ge(token_inverse, 1)
            nc.scalar.activation(tok[:, 1, :], tok[:, 1, :], ACT.Sqrt).then_inc(token_root, 1)
            act.wait_ge(f_turned, 1)
            act.wait_ge(token_rstd, 1)
            for i, (c, t) in enumerate(OUT_POOL):
                nc.scalar.activation(ot[:, t, 512 * c:512 * c + 512], (gp if t else xp)[:, c, :], ACT.Copy,
                                     scale=tok[:, 3, t:t + 1]).then_inc(scaled, 1)

        @block.vector
        def _(dve):
            def take_lo(n, slot):
                dve.wait_ge(hi_ready, n + 1)
                nc.vector.tensor_tensor(wlo[:, slot, :], stage[:, slot, :], whi[:, slot, :].bitcast(F32),
                                        ALU.subtract).then_inc(lo_ready, 1)

            def convert(n0, units=4, slot0=0):
                for u in range(units):
                    if not isinstance(n0, int) or n0 + u + RING < UNITS:
                        take_lo(n0 + u + RING, (slot0 + u) % RING)

            def add_up(hp, j, dst):
                dve.wait_ge(cross_out, hp + 1 - no_cross[0])
                nc.vector.tensor_tensor(dst, gp[:, 2 * j:2 * j + 2, 0:T], cross[:], ALU.add).then_inc(evacuated, 1)
                dve.wait_ge(evacuated, XSLOTS + hp + 1)

            no_cross = [0]

            def by_rstd(n=2):
                return rstd[:, 0:T].unsqueeze(1).broadcast_to([P, n, T])

            def body(phase, it, tail, units=None):
                hp0, n0 = at[phase]
                for j in range(2):
                    for u in range(4):
                        take_lo(n0 + 8 * it + 4 * j + RING + u, u)
                        if units and 4 * j + u in units:
                            for f in units[4 * j + u]:
                                f()
                    tail(hp0 + 2 * it + j, it, j)

            def variance(k, n, eps, bank=0, plus=None):
                dve.wait_ge(stat_ready, n + 1)
                if plus is None:
                    nc.vector.tensor_scalar(var[:, 0:T], xp[:, bank, 0:T], 4.0 / D, 4.0 * eps, ALU.mult, ALU.add).then_inc(var_ready, 1)
                else:
                    nc.vector.scalar_tensor_tensor(var[:, 0:T], xp[:, bank, 0:T], 4.0 / D, plus, ALU.mult, ALU.add).then_inc(var_ready, 1)
                dve.wait_ge(var_ready, k + 1)
                nc.vector.reciprocal(root[:, 0:T], var[:, 0:T]).then_inc(inverse_ready, 1)
                dve.wait_ge(root_ready, k + 1)
                t, y, v = rstd[:, 0:T], root[:, 0:T], var[:, 0:T]
                nc.vector.tensor_tensor(t, y, y, ALU.mult).then_inc(newton, 1)
                dve.wait_ge(newton, 2 * k + 1)
                nc.vector.scalar_tensor_tensor(t, t, -1.0, v, ALU.mult, ALU.mult).then_inc(newton, 1)
                dve.wait_ge(newton, 2 * k + 2)
                nc.vector.scalar_tensor_tensor(t, t, 3.0, y, ALU.add, ALU.mult).then_inc(rstd_ready, 1)
                dve.wait_ge(rstd_ready, k + 1)

            def lo_of_r(c0, M, gain, hp):
                for m in range(2):
                    dve.wait_ge(r_hi, 2 * c0 + 2 * hp + m + 1)
                    nc.vector.scalar_tensor_tensor(part(M, 1, 2 * hp + m, 1), r[:, ds(2 * hp + m, 1), :],
                                                   col(gain, 2 * hp + m), part(M, 0, 2 * hp + m, 1).bitcast(F32),
                                                   ALU.mult, ALU.subtract).then_inc(r_ready, 1)

            dve.wait_ge(vec_ready, 1)
            for c in range(4):
                for kt in range(4 * c, 4 * c + 4):
                    dve.wait_ge(x_hi, kt + 1)
                    nc.vector.scalar_tensor_tensor(A[:, kt, TM:TM + T], r[:, kt, :], col("g_mix", kt),
                                                   A[:, kt, 0:T].bitcast(F32), ALU.mult, ALU.subtract).then_inc(h1_ready, 1)
                take_lo(c, c)

            def normed_into(dst, ready, first=None):
                def tail(hp, it, j):
                    d = dst(it, j)
                    add_up(hp, j, d)
                    if first and j == 0 and isinstance(it, int) and it == 0:
                        first()
                    nc.vector.tensor_tensor(d, d, by_rstd(), ALU.mult).then_inc(ready, 1)
                return tail

            def past(h):
                return not isinstance(h, int) or h >= 1

            def norms(h):
                def variances():
                    dve.wait_ge(qk_sum, h + 1)
                    if past(h):
                        dve.wait_ge(qk_rstd, h)
                    nc.vector.tensor_scalar(var[:], xp[:, 0, :], 4.0 / HD, 4.0 * RMS_EPS, ALU.mult, ALU.add).then_inc(qk_var, 1)
                return variances

            def hat(h):
                def hats():
                    dve.wait_ge(qk_rstd, h + 1)
                    if past(h):
                        dve.wait_ge(scored, h)
                    for i, g in enumerate(("g_q", "g_k")):
                        nc.vector.scalar_tensor_tensor(qk[:, i:i + 1, :], qkv[:, i, ds(h, 1), :], col(g, 0),
                                                       root[:, i * T:(i + 1) * T].unsqueeze(1), ALU.mult, ALU.mult).then_inc(qk_hat, 1)

                return hats

            def scores(h):
                def maxima():
                    dve.wait_ge(scored, h + 1)
                    if past(h):
                        dve.wait_ge(turned, h)
                    nc.vector.tensor_tensor(S[:], xp[:, 1, 0:3 * P], mask[:], ALU.add).then_inc(masked, 1)
                    dve.wait_ge(masked, h + 1)
                    nc.vector.tensor_reduce(small[:, 0, 0:1], S[:, 0:P], AX_X, ALU.max).then_inc(maxed, 1)
                    nc.vector.tensor_reduce(small[:, 0, 1:2], S[:, P:3 * P], AX_X, ALU.max).then_inc(maxed, 1)
                    dve.wait_ge(maxed, 2 * h + 2)
                    nc.vector.tensor_scalar(small[:, 1, :], small[:, 0, :], -SCALE, None, ALU.mult).then_inc(neg_max, 1)

                return maxima

            def probability(h):
                def probabilities():
                    dve.wait_ge(expd, 2 * h + 2)
                    nc.vector.reciprocal(small[:, 3, :], small[:, 2, :]).then_inc(inv_sum, 1)
                    dve.wait_ge(inv_sum, h + 1)
                    for qt, (a, b) in enumerate(((0, P), (P, 3 * P))):
                        nc.vector.tensor_scalar(S[:, a:b], S[:, a:b], small[:, 3, qt:qt + 1], None, ALU.mult).then_inc(probs, 1)
                return probabilities

            def output(h):
                def lo():
                    dve.wait_ge(attn_hi, h + 1)
                    nc.vector.tensor_tensor(B[:, ds(h, 1), T:2 * T], xp[:, 3:4, T:2 * T], B[:, ds(h, 1), 0:T].bitcast(F32),
                                            ALU.subtract).then_inc(attn_ready, 1)
                return lo

            def beside(i):
                if not isinstance(i, int):
                    return {1: [probability(i - 1), hat(i)], 5: [norms(i + 1)], 6: [scores(i)], 7: [output(i - 1)]}
                return {1: ([probability(i - 1)] if i else []) + ([hat(i)] if i < HEADS else []),
                        5: [norms(i + 1)] if i + 1 < HEADS else [], 6: [scores(i)] if i < HEADS else [],
                        7: [output(i - 1)] if i else []}

            qkv_tail = normed_into(lambda it, j: qkv_flat[:, ds(4 * it + 2 * j, 2), :], qkv_ready,
                                   lambda: variance(0, 0, RMS_EPS))
            body("qkv", 0, qkv_tail)
            with dve.Fori(1, 5) as it:
                body("qkv", it, qkv_tail)
            body("qkv", 5, qkv_tail, {5: [norms(0)]})
            ga_tail = normed_into(lambda it, j: GA[:, ds(4 * it + 2 * j, 2), :], ga_ready)
            body("ga", 0, ga_tail, beside(0))
            with dve.Fori(1, 4) as it:
                body("ga", it, ga_tail, beside(it))

            def ccx_tail(hp, it, j):
                add_up(hp, j, s[:, j, :, 0:T])
                if j == 0:
                    return
                four = s[:].rearrange("p j m t -> p (j m) t")[:, :, 0:T]
                nc.vector.tensor_tensor(four, four, by_rstd(4), ALU.mult).then_inc(cc_normed, 1)
                dve.wait_ge(cc_normed, it + 1)
                nc.vector.tensor_tensor(cin[:, :, 2:T + 2], s[:, 0, :, 0:T], s[:, 1, :, 0:T], ALU.mult).then_inc(cin_ready, 1)
                dve.wait_ge(cin_ready, it + 1)
                for tap in range(3):
                    for m in range(2):
                        o, i = cr[:, ds(2 * it + m, 1), :], cin[:, m:m + 1, tap:tap + T]
                        w = col("w_conv", 8 * tap + 2 * it + m)
                        if tap == 0:
                            nc.vector.tensor_scalar(o, i, w, None, ALU.mult).then_inc(cr_step, 1)
                        else:
                            dve.wait_ge(cr_step, 6 * it + 2 * (tap - 1) + m + 1)
                            nc.vector.scalar_tensor_tensor(o, i, w, o, ALU.mult, ALU.add).then_inc(cr_step, 1)

            dve.wait_ge(consts, 5)
            with dve.Fori(0, 3) as it:
                body("ccx", it, ccx_tail, beside(it + 4))
            body("ccx", 3, ccx_tail, beside(7))

            def cb_tail(hp, it, j):
                t = s[:, j, :, 0:T]
                add_up(hp, j, t)
                nc.vector.tensor_tensor(t, t, by_rstd(), ALU.mult).then_inc(cb_normed, 1)
                dve.wait_ge(cb_normed, 2 * it + j + 1)
                dve.wait_ge(cr_step, 24)
                nc.vector.tensor_tensor(t, t, cr[:, ds(4 * it + 2 * j, 2), :], ALU.mult).then_inc(cb_mul, 1)
                dve.wait_ge(cb_hi, 2 * it + j + 1)
                o = ds(CT + 4 * it + 2 * j, 2)
                nc.vector.tensor_tensor(B[:, o, T:2 * T], t, B[:, o, 0:T].bitcast(F32), ALU.subtract).then_inc(conv1_ready, 2)

            body("cb", 0, cb_tail, beside(8))
            body("cb", 1, cb_tail)
            gc_tail = normed_into(lambda it, j: GC[:, ds(4 * it + 2 * j, 2), :], gc_ready)
            with dve.Fori(0, 4) as it:
                body("gc", it, gc_tail)

            def attn_out_tail(hp, h, j):
                t, g = s[:, j, :, 0:T], GA[:, ds(2 * h, 2), :]
                add_up(hp, j, t)
                dve.wait_ge(ga_sig, h + 1)
                nc.vector.tensor_tensor(g, g, t, ALU.mult).then_inc(ga_y, 1)

            def conv_out_tail(hp, h, j):
                t = s[:, j, :, 0:T]
                add_up(hp, j, t)
                dve.wait_ge(gc_sig, h + 1)
                nc.vector.tensor_tensor(t, t, GC[:, ds(2 * h, 2), :], ALU.mult).then_inc(gc_y, 1)
                dve.wait_ge(gc_y, h + 1)
                dve.wait_ge(ga_y, 8)
                nc.vector.tensor_tensor(t, t, GA[:, ds(2 * h, 2), :], ALU.add).then_inc(merged, 1)

            def merged_lo(h, j):
                dve.wait_ge(merged_hi, h + 1)
                nc.vector.tensor_tensor(part(A, 1, 2 * h, 2), s[:, j, :, 0:T], part(A, 0, 2 * h, 2).bitcast(F32),
                                        ALU.subtract).then_inc(merged_ready, 1)

            for phase, tail in (("attn_out", attn_out_tail), ("conv_out", conv_out_tail)):
                hp0, n0 = at[phase]
                with dve.Fori(0, 2) as it:
                    for j in range(4):
                        convert(n0 + 8 * it + 2 * j, 2, 2 * j)
                        if phase == "conv_out" and j >= 2:
                            dve.wait_ge(merged_ready, 4 * it + j - 1)
                        tail(hp0 + 4 * it + j, 4 * it + j, j % 2)
                        if phase == "conv_out" and j:
                            merged_lo(4 * it + j - 1, (j - 1) % 2)
                    if phase == "conv_out":
                        merged_lo(4 * it + 3, 1)
                        dve.wait_ge(merged_ready, 4 * it + 4)

            dve.wait_ge(late_hi, 1)
            nc.vector.tensor_tensor(pT[:, :, T:2 * T], xp[:, 1, :].rearrange("p (k t) -> p k t", k=2),
                                    pT[:, :, 0:T].bitcast(F32), ALU.subtract).then_inc(p_ready, 1)

            def update_r(hp, h, j, c0, M, gain):
                t, rr = s[:, j, :, 0:T], r[:, ds(2 * h, 2), :]
                add_up(hp, j, t)
                nc.vector.tensor_tensor(rr, rr, t, ALU.add).then_inc(r_updated, 1)
                if M is not None:
                    lo_of_r(c0, M, gain, h)

            dve.wait_ge(meta_step, 1)
            nc.vector.tensor_reduce(meta_acc, meta_sq.rearrange("p k t -> p t k"), AX_X, ALU.add).then_inc(meta_acc_ready, 1)
            with dve.Fori(0, 3) as it:
                body("w_o", it, lambda hp, it, j: update_r(hp, 2 * it + j, j, 0, B, "g_mlp"))
            body("w_o", 3, lambda hp, it, j: update_r(hp, 6 + j, j, 0, None if j else B, "g_mlp"))
            hp0, n0 = at["ple"]
            for u in range(4):
                for j in range(2):
                    add_up(hp0 + 2 * u + j, j, PP[:, 4 * u + 2 * j:4 * u + 2 * j + 2, :])
                take_lo(n0 + u + RING, u)
                if u == 0:
                    lo_of_r(0, B, "g_mlp", 7)
            variance(1, 1, RMS_EPS)
            dve.wait_ge(meta_sum, 1)
            nc.vector.tensor_scalar(var[:, T:TM], xp[:, 1, 0:META], 4.0 / D, 4.0 * RMS_EPS, ALU.mult, ALU.add).then_inc(meta_var, 1)

            def ffn1(rnd, last):
                hp0, n0 = at["up0"]
                with dve.Fori(0, 4) as it:
                    for j in range(2):
                        convert(n0 + 64 * rnd + 8 * it + 4 * j)
                        t = s[:, j, :, 0:T]
                        add_up(hp0 + 16 * rnd + 2 * it + j, j, t)
                        c = 8 * rnd + 2 * it + j
                        nc.vector.tensor_tensor(t, t, by_rstd(), ALU.mult).then_inc(up_step, 1)
                        dve.wait_ge(up_step, 2 * c + 1)
                        nc.vector.scalar_tensor_tensor(t, t, 0.0, t, ALU.max, ALU.mult).then_inc(up_step, 1)
                        dve.wait_ge(up_hi, c + 1)
                        nc.vector.tensor_tensor(part(A, 1, 4 * it + 2 * j, 2), t, part(A, 0, 4 * it + 2 * j, 2).bitcast(F32),
                                                ALU.subtract).then_inc(hidden_ready, 1)
                hp0, n0 = at["down0"]
                with dve.Fori(0, 4) as it:
                    for j in range(2):
                        convert(n0 + 64 * rnd + 8 * it + 4 * j)
                        update_r(hp0 + 16 * rnd + 2 * it + j, 2 * it + j, j, 8, B if last else None, "g_ple")

            with dve.Fori(0, 3) as rnd:
                ffn1(rnd, False)
            ffn1(3, True)

            def gate_tail(hp, it, j):
                h, t, rr = 2 * it + j, s[:, j, :, 0:T], r[:, ds(4 * it + 2 * j, 2), :]
                add_up(hp, j, t)
                nc.vector.tensor_tensor(t, t, by_rstd(), ALU.mult).then_inc(gate_normed, 1)
                dve.wait_ge(gate_sig, h + 1)
                nc.vector.tensor_tensor(t, t, PP[:, ds(4 * it + 2 * j, 2), :], ALU.mult).then_inc(gate_mul, 1)
                dve.wait_ge(gate_mul, h + 1)
                nc.vector.tensor_tensor(rr, rr, t, ALU.add).then_inc(r_updated, 1)
                lo_of_r(16, A, "mix_pre", h)

            body("gate", 0, gate_tail, {2: [lambda: variance(2, 2, RMS_EPS)]})
            with dve.Fori(1, 4) as it:
                body("gate", it, gate_tail)
            variance(3, 3, RMS_EPS)
            dve.wait_ge(meta_ready, 1)
            for m in range(2):
                nc.vector.tensor_tensor(diag_last[:, m, :, :], ident[:].unsqueeze(1).broadcast_to([P, PE_LAST, P]),
                                        taps2[:, KT - 2 + m, TAPS2 - PE_LAST:TAPS2].unsqueeze(2).broadcast_to([P, PE_LAST, P]),
                                        ALU.mult).then_inc(diag_last_ready, 1)
            dve.wait_ge(c2_pad, 1)
            odd = sq[:].rearrange("p (m t) -> p m t", m=2)

            def conv2(it, taps=DVE_TAPS):
                last = taps < DVE_TAPS
                dve.wait_ge(c2_ready, 2 * it + 2)
                for tap in range(taps):
                    for m in range(2):
                        o = odd[:, m:m + 1, :] if tap % 2 else V[:, ds(2 * it + m, 1), :]
                        i, w = cin2[:, ds(2 * it + m, 1), tap:tap + T], taps2[:, ds(2 * it + m, 1), tap]
                        done = 2 * DVE_TAPS * it + 2 * tap + m
                        if tap == 0:
                            nc.vector.tensor_scalar(o, i, w, col("b_dw", 2 * it + m), ALU.mult, ALU.add).then_inc(tap_done, 1)
                        elif tap == 1 and last:
                            nc.vector.tensor_scalar(o, i, w, None, ALU.mult).then_inc(tap_done, 1)
                        elif tap == 1:
                            dve.wait_ge(pe_tapped, it + 1)
                            nc.vector.scalar_tensor_tensor(o, i, w, xp[:, 2:3, m * T:m * T + T], ALU.mult,
                                                           ALU.add).then_inc(tap_done, 1)
                        else:
                            dve.wait_ge(tap_done, done - 3)
                            nc.vector.scalar_tensor_tensor(o, i, w, o, ALU.mult, ALU.add).then_inc(tap_done, 1)
                dve.wait_ge(tap_done, 2 * DVE_TAPS * it + 2 * taps)
                v = V[:, ds(2 * it, 2), :]
                nc.vector.tensor_tensor(v, v, odd, ALU.add).then_inc(v_ready, 1)
                dve.wait_ge(v_ready, it + 1)

            conv2(0)
            with dve.Fori(0, 3) as it:
                conv2(2 * it + 1)
                conv2(2 * it + 2)
            conv2(7, TAPS2 - PE_LAST)
            no_cross[0] = 16
            v = V[:, KT - 2:KT, :]
            dve.wait_ge(pe_tapped, 9)
            nc.vector.tensor_tensor(v, v, xp[:, 3, :].rearrange("p (m t) -> p m t", m=2), ALU.add).then_inc(v_ready, 1)
            dve.wait_ge(v_ready, 9)
            dve.wait_ge(centre_ready, 1)
            nc.vector.tensor_tensor(v, v, var[:, T:2 * T].unsqueeze(1).broadcast_to([P, 2, T]), ALU.subtract).then_inc(last_centred, 1)
            dve.wait_ge(last_sum, 1)
            mean, square = sq[:, 0:T], sq[:, T:2 * T]
            nc.vector.tensor_scalar(mean, xp[:, 0, T:2 * T], 1.0 / D, None, ALU.mult).then_inc(mean_ready, 1)
            dve.wait_ge(mean_ready, 1)
            nc.vector.scalar_tensor_tensor(square, mean, -4.0, mean, ALU.mult, ALU.mult).then_inc(mean_ready, 1)
            dve.wait_ge(mean_ready, 2)
            nc.vector.tensor_scalar(square, square, 4.0 * LN_EPS, None, ALU.add).then_inc(corrected, 1)
            dve.wait_ge(corrected, 1)
            variance(4, 5, LN_EPS, bank=1, plus=square)
            for c in range(8 + 3):
                if c < 8:
                    v = V[:, 2 * c:2 * c + 2, :]
                    dve.wait_ge(mean_taken, c + 1)
                    nc.vector.tensor_tensor(v, v, by_rstd(), ALU.mult).then_inc(ln_normed, 1)
                if c >= 3:
                    h = c - 3
                    dve.wait_ge(ln_hi, h + 1)
                    nc.vector.tensor_tensor(part(B, 1, 2 * h, 2), V[:, 2 * h:2 * h + 2, :], part(B, 0, 2 * h, 2).bitcast(F32),
                                            ALU.subtract).then_inc(ln_ready, 1)
            dve.wait_ge(lo_ready, at["out2"][1] + RING)

            hp0, n0 = at["out2"]
            with dve.Fori(0, 4) as it:
                for j in range(2):
                    convert(n0 + 8 * it + 4 * j)
                    add_up(hp0 + 2 * it + j, j, U[:, ds(4 * it + 2 * j, 2), :])
            variance(5, 6, RMS_EPS)

            for h in range(8 + 3):
                if h < 8:
                    u = U[:, 2 * h:2 * h + 2, :]
                    dve.wait_ge(gained, h + 1)
                    nc.vector.tensor_tensor(u, u, by_rstd(), ALU.mult).then_inc(post_normed, 1)
                if h >= 3:
                    lo_of_r(24, A, "ffn_pre", h - 3)

            def glu(rnd, it, hp_done=0, units=None):
                def tail(hp, it, j):
                    c = hp_done + it
                    if j == 0 and not (isinstance(it, int) and c == 0):
                        dve.wait_ge(glu_ready, c)
                    add_up(hp, j, s[:, j, :, 0:T])
                    if j == 0:
                        return
                    four = s[:].rearrange("p j m t -> p (j m) t")[:, :, 0:T]
                    nc.vector.tensor_tensor(four, four, by_rstd(4), ALU.mult).then_inc(glu_normed, 1)
                    dve.wait_ge(glu_normed, c + 1)
                    a, b = s[:, 0, :, 0:T], s[:, 1, :, 0:T]
                    nc.vector.tensor_tensor(b, b, a, ALU.mult).then_inc(glu_mul, 1)
                    dve.wait_ge(glu_mul, 2 * c + 1)
                    dve.wait_ge(glu_sig, c + 1)
                    nc.vector.tensor_tensor(a, b, root[:].rearrange("p (m t) -> p m t", m=2), ALU.mult).then_inc(glu_mul, 1)
                    dve.wait_ge(glu_hi, c + 1)
                    nc.vector.tensor_tensor(B[:, ds(2 * it, 2), T:2 * T], a, B[:, ds(2 * it, 2), 0:T].bitcast(F32),
                                            ALU.subtract).then_inc(glu_ready, 1)
                body(f"glu{rnd}", it, tail, units)

            def back_tail(first):
                def tail(hp, it, j):
                    f = F[:, ds(4 * it + 2 * j, 2), :]
                    if first:
                        add_up(hp, j, f)
                    else:
                        t = s[:, j, :, 0:T]
                        add_up(hp, j, t)
                        nc.vector.tensor_tensor(f, f, t, ALU.add).then_inc(r_updated, 1)
                return tail

            glu(0, 0, units={5: [lambda: variance(6, 7, RMS_EPS)]})
            with dve.Fori(1, 8) as it:
                glu(0, it)
            with dve.Fori(0, 4) as it:
                body("back0", it, back_tail(True))
            with dve.Fori(0, 8) as it:
                glu(1, it, 8)
            with dve.Fori(0, 4) as it:
                body("back1", it, back_tail(False))
            with dve.Fori(0, 6) as it:
                glu(2, it, 16)
            hp0, n0 = at["back2"]
            for h in range(8):
                convert(n0 + 3 * h, 3, 3 * h)
                back_tail(False)(hp0 + h, h // 2, h % 2)
            dve.wait_ge(stat_ready, 9)
            v, y, w = tok[:, 0, :], tok[:, 1, :], tok[:, 2, :]
            nc.vector.tensor_reduce(w, gp[:, 3, 0:4].rearrange("p (t a) -> p t a", a=2), AX_X, ALU.add).then_inc(token_var, 1)
            dve.wait_ge(token_var, 1)
            nc.vector.tensor_scalar(v, w, 4.0 / D, 4.0 * RMS_EPS, ALU.mult, ALU.add).then_inc(token_var, 1)
            dve.wait_ge(token_var, 2)
            nc.vector.reciprocal(y, v).then_inc(token_inverse, 1)
            dve.wait_ge(token_root, 1)
            nc.vector.tensor_tensor(w, y, y, ALU.mult).then_inc(token_newton, 1)
            dve.wait_ge(token_newton, 1)
            nc.vector.scalar_tensor_tensor(w, w, -1.0, v, ALU.mult, ALU.mult).then_inc(token_newton, 1)
            dve.wait_ge(token_newton, 2)
            nc.vector.scalar_tensor_tensor(tok[:, 3, :], w, 3.0, y, ALU.add, ALU.mult).then_inc(token_rstd, 1)
            dve.wait_ge(token_rstd, 1)
            dve.wait_ge(f_turned, 1)
            dve.wait_ge(rt_copied, 2)
            for c in range(4):
                for t in range(2):
                    if (c, t) not in OUT_POOL:
                        o = slice(512 * c, 512 * c + 512)
                        nc.vector.scalar_tensor_tensor(ot[:, t, o], (gp if t else xp)[:, c, :], tok[:, 3, t:t + 1], rt[:, t, o],
                                                       ALU.mult, ALU.add).then_inc(added, 1)

        @block.gpsimd
        def _(pool):
            nc.gpsimd.memset(ident[:], 0.0).then_inc(consts0, 1)
            nc.gpsimd.memset(mask[:], 0.0).then_inc(consts0, 1)
            nc.gpsimd.memset(three[:], 3.0)
            nc.gpsimd.memset(sq[:, 0:P], 1.0).then_inc(consts, 1)
            pool.wait_ge(consts, 1)
            nc.gpsimd.tensor_copy(ones_r[:], sq[:, 0:P]).then_inc(consts, 1)
            pool.wait_ge(consts0, 1)
            nc.gpsimd.affine_select(out=ident[:], in_=ident[:], compare_op=ALU.not_equal, fill=1.0, base=0,
                                    pattern=[[-1, P]], channel_multiplier=1).then_inc(consts, 1)
            pool.wait_ge(consts0, 2)
            for c in (0, 2):
                last = nc.gpsimd.affine_select(out=mask[:, c * P:c * P + P], in_=mask[:, c * P:c * P + P],
                                               compare_op=ALU.is_ge, fill=NEG, base=0, pattern=[[-1, P]],
                                               channel_multiplier=1)
            last.then_inc(consts, 1)

            def clear(n):
                if n:
                    pool.wait_ge(stat_ready, n)
                nc.gpsimd.memset(acc[:], 0.0).then_inc(acc_ready, 1)

            def two(x):
                return x[:, :].rearrange("p (m t) -> p m t", m=2)

            def add_squares(k, h, src, nsq, steps=1):
                nc.gpsimd.tensor_tensor(two(sq), src, src, ALU.mult).then_inc(squared, 1)
                pool.wait_ge(squared, nsq + h + 1)
                pool.wait_ge(acc_ready, 9 * k + h + 1)
                nc.gpsimd.tensor_tensor(acc[:], acc[:], sq[:], ALU.add).then_inc(acc_ready, steps)
                pool.wait_ge(acc_ready, 9 * k + h + 1 + steps)

            clear(0)
            for h in range(8):
                pool.wait_ge(evacuated, h // 2 + 1)
                add_squares(0, h, r[:, 2 * h:2 * h + 2, :], 0)
            nc.gpsimd.memset(cin[:, :, 0:2], 0.0).then_inc(consts, 1)

            def squares(h):
                pool.wait_ge(qkv_ready, 8)
                if not isinstance(h, int) or h >= 1:
                    pool.wait_ge(qk_sum, h)
                x = qkv[:, 0:2, ds(h, 1), :].rearrange("p a h t -> p (a h) t")
                nc.gpsimd.tensor_tensor(two(sq), x, x, ALU.mult).then_inc(qk_sq, 1)
                nc.gpsimd.tensor_tensor(two(sq_parts[:, 0, :]), x, x, ALU.mult).then_inc(qk_sq, 1)
                pool.wait_ge(qk_sq, 3 * h + 2)
                nc.gpsimd.tensor_tensor(sq_parts[:, 1, :], sq[:], sq_parts[:, 0, :].bitcast(F32), ALU.subtract).then_inc(qk_sq, 1)
                pool.wait_ge(qk_sq, 3 * h + 3)

            def refine(h):
                pool.wait_ge(qk_root, h + 1)
                nc.gpsimd.tensor_tensor(sq[:], root[:], root[:], ALU.mult).then_inc(qk_newton, 1)
                pool.wait_ge(qk_newton, 3 * h + 1)
                nc.gpsimd.tensor_tensor(sq[:], sq[:], var[:], ALU.mult).then_inc(qk_newton, 1)
                pool.wait_ge(qk_newton, 3 * h + 2)
                nc.gpsimd.tensor_tensor(sq[:], three[:].broadcast_to([P, 2 * T]), sq[:], ALU.subtract).then_inc(qk_newton, 1)
                pool.wait_ge(qk_newton, 3 * h + 3)
                nc.gpsimd.tensor_tensor(root[:], root[:], sq[:], ALU.mult).then_inc(qk_rstd, 1)
                pool.wait_ge(qk_rstd, h + 1)

            def values(h):
                if not isinstance(h, int) or h >= 1:
                    pool.wait_ge(turned, h)
                pool.wait_ge(qkv_ready, 12)
                nc.gpsimd.tensor_copy(vh[:].unsqueeze(1), qkv[:, 2, ds(h, 1), :]).then_inc(vh_ready, 1)

            squares(0)
            refine(0)
            squares(1)
            values(0)
            refine(1)
            with pool.Fori(2, HEADS) as h:
                squares(h)
                values(h - 1)
                refine(h)
            values(HEADS - 1)

            def squares_of_r(k, c0, nsq):
                clear(k)
                with pool.Fori(0, 8) as h:
                    pool.wait_ge(r_updated, c0 + h + 1)
                    add_squares(k, h, r[:, ds(2 * h, 2), :], nsq)

            pool.wait_ge(late_hi, 2)
            nc.gpsimd.tensor_tensor(meta_sq, metaT, metaT, ALU.mult).then_inc(meta_step, 1)
            squares_of_r(1, 0, 8)
            nc.gpsimd.memset(rstd[:, T:TM], 1.0)
            mt, my, mv = sq[:, 0:META], root[:, T:TM], var[:, T:TM]
            pool.wait_ge(meta_act, 2)
            nc.gpsimd.tensor_tensor(mt, my, my, ALU.mult).then_inc(meta_step, 1)
            pool.wait_ge(meta_step, 2)
            nc.gpsimd.tensor_tensor(mt, mt, mv, ALU.mult).then_inc(meta_step, 1)
            pool.wait_ge(meta_step, 3)
            nc.gpsimd.tensor_tensor(mt, three[:].broadcast_to([P, META]), mt, ALU.subtract).then_inc(meta_step, 1)
            pool.wait_ge(meta_step, 4)
            nc.gpsimd.tensor_tensor(my, my, mt, ALU.mult)
            half, c = vec["mix_pre"]
            nc.gpsimd.tensor_tensor(metaT, metaT, gv[:, half, c:c + KT].unsqueeze(2).broadcast_to([P, KT, META]),
                                    ALU.mult).then_inc(meta_step, 1)
            pool.wait_ge(meta_step, 5)
            nc.gpsimd.tensor_tensor(metaT, metaT, my.unsqueeze(1).broadcast_to([P, KT, META]), ALU.mult).then_inc(meta_step, 1)
            squares_of_r(2, 32, 16)
            pool.wait_ge(meta_hi, 1)
            nc.gpsimd.tensor_tensor(A[:, :, TM + T:2 * TM], metaT, A[:, :, T:TM].bitcast(F32), ALU.subtract).then_inc(meta_ready, 1)
            squares_of_r(3, 40, 24)
            pool.wait_ge(gate_mul, 8)
            nc.gpsimd.memset(cin2[:, :, 0:PAD2], 0.0).then_inc(c2_pad, 1)

            def take_lo(n, slot):
                pool.wait_ge(hi_ready, n + 1)
                nc.gpsimd.tensor_tensor(wlo[:, slot, :], stage[:, slot, :], whi[:, slot, :].bitcast(F32),
                                        ALU.subtract).then_inc(lo_ready, 1)

            def gating(q):
                pool.wait_ge(evacuated, XSLOTS + at["conv2"][0] + 2 * q + 2)
                four = s[:].rearrange("p j m t -> p (j m) t")
                nc.gpsimd.tensor_tensor(four, four, rstd[:].unsqueeze(1).broadcast_to([P, 4, TM]), ALU.mult).then_inc(c2_normed, 1)

            def gated(q):
                pool.wait_ge(c2_sig, 4 * q + 4)
                o = cin2[:, ds(2 * q, 2), :]
                for dst, a, b in ((o[:, :, PAD2 + META:LEN2], 0, T), (o[:, :, PAD2:PAD2 + META], T, TM)):
                    nc.gpsimd.tensor_tensor(dst, s[:, 0, :, a:b], s[:, 1, :, a:b], ALU.mult).then_inc(c2_ready, 1)

            n0 = at["conv2"][1]
            pool.wait_ge(lo_ready, n0 + RING)
            for u in range(8):
                take_lo(n0 + RING + u, u % RING)
            pool.wait_ge(rstd_ready, 4)
            with pool.Fori(1, 8) as it:
                gating(it - 1)
                take_lo(n0 + RING + 8 * it, 0)
                gated(it - 1)
                for u in range(1, 8):
                    take_lo(n0 + RING + 8 * it + u, u % RING)
            gating(7)
            gated(7)
            pool.wait_ge(centre_ready, 1)
            for h in range(7):
                v = V[:, 2 * h:2 * h + 2, :]
                nc.gpsimd.tensor_tensor(v, v, var[:, T:2 * T].unsqueeze(1).broadcast_to([P, 2, T]), ALU.subtract).then_inc(centred, 1)
            pool.wait_ge(mean_ready, 1)
            for h in range(8):
                v = V[:, 2 * h:2 * h + 2, :]
                pool.wait_ge(ln_sq, h + 1)
                nc.gpsimd.tensor_tensor(v, v, sq[:, 0:T].unsqueeze(1).broadcast_to([P, 2, T]), ALU.subtract).then_inc(mean_taken, 1)
            clear(6)
            for h in range(7):
                pool.wait_ge(evacuated, XSLOTS + at["out2"][0] + h + 1)
                add_squares(4, h, U[:, 2 * h:2 * h + 2, :], 32, 2 if h == 6 else 1)
            for h in range(8):
                pool.wait_ge(post_normed, h + 1)
                o = r[:, 2 * h:2 * h + 2, :]
                nc.gpsimd.tensor_tensor(o, o, U[:, 2 * h:2 * h + 2, :], ALU.add).then_inc(r_updated, 1)
            clear(7)
            for h in range(8):
                pool.wait_ge(post_sq, h + 1)
                pool.wait_ge(acc_ready, 9 * 5 + h + 1)
                nc.gpsimd.tensor_tensor(two(acc), two(acc), U[:, 2 * h:2 * h + 2, :], ALU.add).then_inc(acc_ready, 1)
            clear(8)
            for h in range(7):
                pool.wait_ge(r_updated, 64 + h + 1)
                add_squares(6, h, F[:, 2 * h:2 * h + 2, :], 39, 2 if h == 6 else 1)
            for i, (c, t) in enumerate(OUT_POOL):
                o = ot[:, t, 512 * c:512 * c + 512]
                pool.wait_ge(scaled, i + 1)
                nc.gpsimd.tensor_tensor(o, o, rt[:, t, 512 * c:512 * c + 512], ALU.add).then_inc(out_ready, 1)


_INS = ["x", "p", "g_mix", "w_in", "g_q", "g_k", "w_conv", "w_attn_out", "w_conv_out", "w_o", "g_mlp", "w_up", "w_down",
        "g_ple", "w_ple_gate", "w_ple_proj", "meta_tokens_2", "conv_w_in_2", "conv_b_in_2", "conv_w_dw_2", "conv_b_dw_2",
        "conv_ln_g_2", "conv_ln_b_2", "conv_w_out_2", "conv_b_out_2", "norm_mix_pre_2", "norm_mix_post_2",
        "norm_ffn_pre_2", "norm_ffn_post_2", "ffn_w_gate_2", "ffn_w_up_2", "ffn_w_down_2"]


def kernel(**inputs):
    import numpy as _np
    import concourse.bacc as _bacc
    from concourse import mybir as _mybir
    from concourse.bass_utils import run_bass_kernel_spmd as _run

    nc = _bacc.Bacc("TRN2", target_bir_lowering=False, num_devices=1)
    arrays, io = {}, {}
    for name in _INS:
        a = _np.ascontiguousarray(inputs[name])
        arrays[f"in_{name}"] = a
        io[name] = nc.dram_tensor(f"in_{name}", a.shape, _mybir.dt.from_np(a.dtype), kind="ExternalInput").ap()
    out = nc.dram_tensor("out_0", (1, T, D), F32, kind="ExternalOutput").ap()
    two_block_kernel(nc, io, out)
    r = _run(nc, [arrays], core_ids=[0])
    return r.results[0]["out_0"]
```
